# Optimizing a Trainium2 kernel written in Bass

```python
import jax, jax.numpy as jnp
from jax import lax
import numpy as np

D_MODEL = 1024
BATCH = 1
SEQ = 256
DEPTH = 2

GRID_W = 64
CTX_LEN = 256
D_MIX = D_MODEL
HEAD_DIM = 64
CONV_CH = D_MIX // 4
CONV_K = 3
ATT_HEADS = D_MIX // 2 // HEAD_DIM
ATT_KV_HEADS = 2
ATT_GROUP = ATT_HEADS // ATT_KV_HEADS
WINDOW = 128
BLOCK = 128
GLA_HEADS = D_MIX // 4 // HEAD_DIM
GLA_DK = HEAD_DIM
GLA_DV = HEAD_DIM
GLA_RANK = 16
GLA_NORMALIZER = 16.0
GLA_CHUNK = 32
D_FF = ((8 * D_MODEL + 3 * 256 - 1) // (3 * 256)) * 256
N_MOD = 6
ROPE_BASE = 10000.0
EPS = 1e-6
COL_SIZES = (CONV_CH, CONV_CH, CONV_CH,
             ATT_HEADS * HEAD_DIM, ATT_KV_HEADS * HEAD_DIM, ATT_KV_HEADS * HEAD_DIM,
             GLA_HEADS * GLA_DK, GLA_HEADS * GLA_DK, GLA_HEADS * GLA_DV, GLA_HEADS * GLA_DV,
             2 * GLA_RANK)
N_IN = sum(COL_SIZES)
COL_SPLITS = tuple(int(v) for v in np.cumsum(COL_SIZES)[:-1])


def rmsnorm(x, g):
    x32 = x.astype(jnp.float32)
    y = x32 * lax.rsqrt(jnp.mean(x32 * x32, axis=-1, keepdims=True) + EPS)
    return (y * g.astype(jnp.float32)).astype(x.dtype)

def heads(a, n):
    return a.reshape(a.shape[:-1] + (n, a.shape[-1] // n))

def axial_rope_tables(rows):
    t = jnp.arange(rows * GRID_W)
    row = (t // GRID_W).astype(jnp.float32)
    col = (t % GRID_W).astype(jnp.float32)
    n_freq = HEAD_DIM // 4
    inv_freq = ROPE_BASE ** (-jnp.arange(n_freq, dtype=jnp.float32) / n_freq)
    ang = jnp.stack([row[:, None] * inv_freq, col[:, None] * inv_freq], axis=1)
    return jnp.cos(ang), jnp.sin(ang)

def apply_rope(x, cos, sin):
    B, S, H, D = x.shape
    xs = x.astype(jnp.float32).reshape(B, S, H, 2, D // 2)
    half = D // 4
    x1, x2 = xs[..., :half], xs[..., half:]
    c = cos[None, :, None]
    s = sin[None, :, None]
    out = jnp.concatenate([x1 * c - x2 * s, x2 * c + x1 * s], axis=-1)
    return out.reshape(B, S, H, D).astype(x.dtype)

def short_conv(x_in, b_gate, c_gate, w):
    T = x_in.shape[1]
    u = c_gate * x_in
    up = jnp.pad(u, ((0, 0), (CONV_K // 2, CONV_K // 2), (0, 0)))
    y = sum(w[j] * up[:, j:j + T] for j in range(CONV_K))
    return b_gate * y

def softmax_with_sink(scores, sink):
    s = jnp.broadcast_to(sink.astype(jnp.float32).reshape(ATT_KV_HEADS, ATT_GROUP, 1, 1),
                         scores.shape[:-1] + (1,))
    p = jax.nn.softmax(jnp.concatenate([s, scores], axis=-1), axis=-1)
    return p[..., 1:]

def context_attention(q, k, v, sink):
    B, L = q.shape[:2]
    qg = q.reshape(B, L, ATT_KV_HEADS, ATT_GROUP, HEAD_DIM)
    s = jnp.einsum('bqhgd,bkhd->bhgqk', qg, k).astype(jnp.float32) * HEAD_DIM ** -0.5
    p = softmax_with_sink(s, sink).astype(v.dtype)
    o = jnp.einsum('bhgqk,bkhd->bqhgd', p, v)
    return o.reshape(B, L, ATT_HEADS * HEAD_DIM)

def window_attention(q, k, v, k_ctx, v_ctx, sink):
    B, S = q.shape[:2]
    L = k_ctx.shape[1]
    nb = S // BLOCK
    qb = q.reshape(B, nb, BLOCK, ATT_KV_HEADS, ATT_GROUP, HEAD_DIM).transpose(1, 0, 2, 3, 4, 5)
    pad = ((0, 0), (BLOCK, BLOCK), (0, 0), (0, 0))
    kp = jnp.pad(k, pad)
    vp = jnp.pad(v, pad)
    r = jnp.arange(BLOCK)
    j = jnp.arange(3 * BLOCK)
    scale = HEAD_DIM ** -0.5

    def one_block(args):
        qi, i = args
        start = i * BLOCK
        ks = lax.dynamic_slice_in_dim(kp, start, 3 * BLOCK, axis=1)
        vs = lax.dynamic_slice_in_dim(vp, start, 3 * BLOCK, axis=1)
        s_ctx = jnp.einsum('bqhgd,bkhd->bhgqk', qi, k_ctx).astype(jnp.float32)
        s_loc = jnp.einsum('bqhgd,bkhd->bhgqk', qi, ks).astype(jnp.float32)
        tq = start + r
        tk = start - BLOCK + j
        valid = (jnp.abs(tq[:, None] - tk[None, :]) <= WINDOW) & (tk[None, :] >= 0) & (tk[None, :] < S)
        s_loc = jnp.where(valid, s_loc, -jnp.inf)
        p = softmax_with_sink(jnp.concatenate([s_ctx, s_loc], axis=-1) * scale, sink).astype(v.dtype)
        o = (jnp.einsum('bhgqk,bkhd->bqhgd', p[..., :L], v_ctx)
             + jnp.einsum('bhgqk,bkhd->bqhgd', p[..., L:], vs))
        return o.reshape(B, BLOCK, ATT_HEADS * HEAD_DIM)

    out = lax.map(one_block, (qb, jnp.arange(nb)))
    return out.transpose(1, 0, 2, 3).reshape(B, S, ATT_HEADS * HEAD_DIM)

def gla_chunk_scan(q, k, v, log_g, state0, with_output):
    B, T, H, _ = q.shape
    n = T // GLA_CHUNK

    def to_chunks(a):
        return a.reshape(B, n, GLA_CHUNK, H, a.shape[-1]).transpose(1, 0, 3, 2, 4)

    lower_tri = jnp.tril(jnp.ones((GLA_CHUNK, GLA_CHUNK), dtype=bool))[:, :, None]

    def step(state, inp):
        qc, kc, vc, gc = inp
        b = jnp.cumsum(gc.astype(jnp.float32), axis=2)
        b_last = b[:, :, -1:, :]
        new_state = (jnp.exp(b_last[:, :, 0, :])[..., None] * state
                     + jnp.einsum('bhsk,bhsv->bhkv', kc * jnp.exp(b_last - b), vc))
        if not with_output:
            return new_state, None
        diff = jnp.where(lower_tri, b[:, :, :, None, :] - b[:, :, None, :, :], -jnp.inf)
        a = jnp.einsum('bhtk,bhsk,bhtsk->bhts', qc, kc, jnp.exp(diff))
        o = (jnp.einsum('bhts,bhsv->bhtv', a, vc)
             + jnp.einsum('bhtk,bhkv->bhtv', qc * jnp.exp(b), state))
        return new_state, o

    state, o = lax.scan(step, state0, (to_chunks(q), to_chunks(k), to_chunks(v), to_chunks(log_g)))
    if not with_output:
        return None, state
    return o.transpose(1, 0, 3, 2, 4).reshape(B, T, H, v.shape[-1]), state

def gla_output(o, g, norm_g):
    o32 = o.astype(jnp.float32)
    o32 = o32 * lax.rsqrt(jnp.mean(o32 * o32, axis=-1, keepdims=True) + EPS) * norm_g.astype(jnp.float32)
    B, T = o.shape[:2]
    return (o32.reshape(B, T, GLA_HEADS * GLA_DV) * jax.nn.silu(g.astype(jnp.float32))).astype(g.dtype)

def gla_bidir(q, k, v, lr, g, q_c, k_c, v_c, lr_c, g_c, w_gate, b_gate, norm_g, ctx_out):
    B = q.shape[0]
    q = heads(q, GLA_HEADS) * GLA_DK ** -0.5
    k = heads(k, GLA_HEADS)
    v = heads(v, GLA_HEADS)
    q_c = heads(q_c, GLA_HEADS) * GLA_DK ** -0.5
    k_c = heads(k_c, GLA_HEADS)
    v_c = heads(v_c, GLA_HEADS)
    outs_x, outs_c = [], []
    for d in range(2):
        sl = slice(d * GLA_RANK, (d + 1) * GLA_RANK)
        gate_x = heads(jax.nn.log_sigmoid(lr[..., sl] @ w_gate[d] + b_gate[d]) / GLA_NORMALIZER, GLA_HEADS)
        gate_c = heads(jax.nn.log_sigmoid(lr_c[..., sl] @ w_gate[d] + b_gate[d]) / GLA_NORMALIZER, GLA_HEADS)
        flip = (lambda a: jnp.flip(a, axis=1)) if d == 1 else (lambda a: a)
        state0 = jnp.zeros((B, GLA_HEADS, GLA_DK, GLA_DV), jnp.float32)
        o_c, s_c = gla_chunk_scan(flip(q_c), flip(k_c), flip(v_c), flip(gate_c), state0, ctx_out)
        o_x, _ = gla_chunk_scan(flip(q), flip(k), flip(v), flip(gate_x), s_c, True)
        outs_x.append(flip(o_x))
        if ctx_out:
            outs_c.append(flip(o_c))
    y_x = gla_output(outs_x[0] + outs_x[1], g, norm_g)
    y_c = gla_output(outs_c[0] + outs_c[1], g_c, norm_g) if ctx_out else None
    return y_x, y_c

def swiglu(h, w_up, w_down):
    a, b = jnp.split(h @ w_up, 2, axis=-1)
    return (jax.nn.silu(a) * b) @ w_down

def layer(x, ctx, mod_x, mod_c, cos, sin, g1, g2, w_in, conv_w, sink, gate_w, gate_b, norm_g,
          w_out, w_up, w_down, ctx_out):
    sh1, sc1, gt1, sh2, sc2, gt2 = jnp.split(mod_x[:, None, :], N_MOD, axis=-1)
    csh1, csc1, cgt1, csh2, csc2, cgt2 = jnp.split(mod_c, N_MOD, axis=-1)
    hx = rmsnorm(x, g1) * (1 + sc1) + sh1
    hc = rmsnorm(ctx, g1) * (1 + csc1) + csh1
    (xc_in, xc_b, xc_c, xq, xk, xv, xgq, xgk, xgv, xgg, xlr) = jnp.split(hx @ w_in, COL_SPLITS, axis=-1)
    (cc_in, cc_b, cc_c, cq, ck, cv, cgq, cgk, cgv, cgg, clr) = jnp.split(hc @ w_in, COL_SPLITS, axis=-1)
    k_ctx = heads(ck, ATT_KV_HEADS)
    v_ctx = heads(cv, ATT_KV_HEADS)
    conv_x = short_conv(xc_in, xc_b, xc_c, conv_w)
    attn_x = window_attention(apply_rope(heads(xq, ATT_HEADS), cos, sin),
                              apply_rope(heads(xk, ATT_KV_HEADS), cos, sin),
                              heads(xv, ATT_KV_HEADS), k_ctx, v_ctx, sink)
    gla_x, gla_c = gla_bidir(xgq, xgk, xgv, xlr, xgg, cgq, cgk, cgv, clr, cgg,
                             gate_w, gate_b, norm_g, ctx_out)
    x = x + gt1 * (jnp.concatenate([conv_x, attn_x, gla_x], axis=-1) @ w_out)
    x = x + gt2 * swiglu(rmsnorm(x, g2) * (1 + sc2) + sh2, w_up, w_down)
    if ctx_out:
        conv_c = short_conv(cc_in, cc_b, cc_c, conv_w)
        attn_c = context_attention(heads(cq, ATT_HEADS), k_ctx, v_ctx, sink)
        ctx = ctx + cgt1 * (jnp.concatenate([conv_c, attn_c, gla_c], axis=-1) @ w_out)
        ctx = ctx + cgt2 * swiglu(rmsnorm(ctx, g2) * (1 + csc2) + csh2, w_up, w_down)
    return x, ctx

def first_inputs(seed: int = 0) -> dict:
    key = jax.random.key(seed)
    ks = jax.random.split(key, 18)

    def nrm(k, shape, s):
        return jax.random.normal(k, shape, jnp.float32) * s

    return {
        "x": nrm(ks[0], (BATCH, SEQ, D_MODEL), 1.0),
        "c": nrm(ks[1], (BATCH, D_MODEL), 1.0),
        "ctx": nrm(ks[2], (BATCH, CTX_LEN, D_MODEL), 1.0),
        "c_ctx": nrm(ks[3], (D_MODEL,), 1.0),
        "w_mod": nrm(ks[4], (DEPTH, D_MODEL, N_MOD * D_MODEL), 0.02),
        "b_mod": nrm(ks[5], (DEPTH, N_MOD * D_MODEL), 0.01),
        "norm1_g": 1.0 + nrm(ks[6], (DEPTH, D_MODEL), 0.02),
        "norm2_g": 1.0 + nrm(ks[7], (DEPTH, D_MODEL), 0.02),
        "w_in": nrm(ks[8], (DEPTH, D_MODEL, N_IN), D_MODEL ** -0.5),
        "conv_w": nrm(ks[9], (DEPTH, CONV_K, CONV_CH), CONV_K ** -0.5),
        "attn_sink": nrm(ks[10], (DEPTH, ATT_HEADS), 1.0),
        "gla_gate_w": nrm(ks[11], (DEPTH, 2, GLA_RANK, GLA_HEADS * GLA_DK), GLA_RANK ** -0.5),
        "gla_gate_b": nrm(ks[12], (DEPTH, 2, GLA_HEADS * GLA_DK), 0.1),
        "gla_norm_g": 1.0 + nrm(ks[13], (DEPTH, GLA_DV), 0.02),
        "w_out": nrm(ks[14], (DEPTH, D_MIX, D_MODEL), D_MIX ** -0.5),
        "w_up": nrm(ks[15], (DEPTH, D_MODEL, 2 * D_FF), D_MODEL ** -0.5),
        "w_down": nrm(ks[16], (DEPTH, D_FF, D_MODEL), D_FF ** -0.5),
        "final_norm_g": 1.0 + nrm(ks[17], (D_MODEL,), 0.02),
    }

def first_block(x, c, ctx, c_ctx, w_mod, b_mod, norm1_g, norm2_g, w_in, conv_w, attn_sink,
              gla_gate_w, gla_gate_b, gla_norm_g, w_out, w_up, w_down, final_norm_g):
    ROWS = x.shape[1] // GRID_W
    cos, sin = axial_rope_tables(ROWS)
    for l in range(DEPTH):
        mod_x = jax.nn.silu(c) @ w_mod[l] + b_mod[l]
        mod_c = jax.nn.silu(c_ctx) @ w_mod[l] + b_mod[l]
        x, ctx = layer(x, ctx, mod_x, mod_c, cos, sin, norm1_g[l], norm2_g[l], w_in[l], conv_w[l],
                       attn_sink[l], gla_gate_w[l], gla_gate_b[l], gla_norm_g[l], w_out[l],
                       w_up[l], w_down[l], l < DEPTH - 1)
    return rmsnorm(x, final_norm_g)


N_MEM = 256
MLSTM_HEADS = 4
MLSTM_HEAD_DIM = D_MODEL // 16
MLSTM_WIDTH = MLSTM_HEADS * MLSTM_HEAD_DIM
MLSTM_CHUNK = 64
MLSTM_CONV = 4
CONF_CHANNELS = D_MODEL // 4
CONF_KERNEL = 31
FOX_HEADS = 8
FOX_HEAD_DIM = D_MODEL // 16
FOX_WIDTH = FOX_HEADS * FOX_HEAD_DIM
FOX_BLOCK = 128
MIX_WIDTH = MLSTM_WIDTH + CONF_CHANNELS + FOX_WIDTH
XATTN_HEADS = 4
XATTN_HEAD_DIM = D_MODEL // 8
XATTN_WIDTH = XATTN_HEADS * XATTN_HEAD_DIM
D_FF_2 = ((8 * D_MODEL // 3) + 255) // 256 * 256
N_EXPERTS = 8
TOP_K = 2
EXPERT_FF = D_FF_2
N_DENSE_LAYERS = (DEPTH + 1) // 2
N_MOE_LAYERS = DEPTH // 2

IN_SPLITS = (2 * MLSTM_WIDTH, MLSTM_WIDTH, MLSTM_WIDTH, MLSTM_HEADS, MLSTM_HEADS,
             2 * CONF_CHANNELS, FOX_WIDTH, FOX_WIDTH, FOX_WIDTH, FOX_HEADS)
IN_WIDTH = sum(IN_SPLITS)
IN_SPLIT_IDX = tuple(int(i) for i in np.cumsum(IN_SPLITS)[:-1])


def rmsnorm_2(x, w):
    xf = x.astype(jnp.float32)
    y = xf * lax.rsqrt(jnp.mean(xf * xf, axis=-1, keepdims=True) + EPS)
    return (y * w.astype(jnp.float32)).astype(x.dtype)

def layernorm_f32(x, w, b):
    mu = jnp.mean(x, axis=-1, keepdims=True)
    xc = x - mu
    var = jnp.mean(xc * xc, axis=-1, keepdims=True)
    return xc * lax.rsqrt(var + EPS) * w.astype(jnp.float32) + b.astype(jnp.float32)

def causal_dwconv(x, w, b):
    K, C = w.shape
    y = lax.conv_general_dilated(
        x, w.astype(jnp.float32)[:, None, :], window_strides=(1,), padding=[(K - 1, 0)],
        dimension_numbers=("NWC", "WIO", "NWC"), feature_group_count=C)
    return y + b.astype(jnp.float32)

def mlstm_chunkwise(q, k, v, i_pre, f_pre):
    B, S, H, Dh = q.shape
    L = MLSTM_CHUNK
    nc = S // L
    log_f = jax.nn.log_sigmoid(f_pre)
    log_i = i_pre

    def chunks(t):
        return t.reshape(B, nc, L, H, Dh).transpose(1, 0, 3, 2, 4)

    def gchunks(t):
        return t.reshape(B, nc, L, H).transpose(1, 0, 3, 2)

    causal = jnp.tril(jnp.ones((L, L), dtype=bool))

    def step(carry, xs):
        C, n, m = carry
        qc, kc, vc, lic, lfc = xs
        b = jnp.cumsum(lfc, axis=-1)
        d_log = b[..., :, None] - b[..., None, :] + lic[..., None, :]
        d_log = jnp.where(causal, d_log, -jnp.inf)
        inter = b + m[..., None]
        m_t = jnp.maximum(jnp.max(d_log, axis=-1), inter)
        s = jnp.einsum("bhtd,bhsd->bhts", qc, kc) * jnp.exp(d_log - m_t[..., None])
        w_inter = jnp.exp(inter - m_t)
        num = (jnp.einsum("bhts,bhsd->bhtd", s, vc)
               + w_inter[..., None] * jnp.einsum("bhtk,bhkv->bhtv", qc, C))
        den = jnp.sum(s, axis=-1) + w_inter * jnp.einsum("bhtk,bhk->bht", qc, n)
        h = num / jnp.maximum(jnp.abs(den), jnp.exp(-m_t))[..., None]
        b_tot = b[..., -1]
        g = b_tot[..., None] - b + lic
        m_new = jnp.maximum(b_tot + m, jnp.max(g, axis=-1))
        wg = jnp.exp(g - m_new[..., None])
        decay = jnp.exp(b_tot + m - m_new)
        C_new = decay[..., None, None] * C + jnp.einsum("bhsk,bhsv->bhkv", kc * wg[..., None], vc)
        n_new = decay[..., None] * n + jnp.einsum("bhs,bhsk->bhk", wg, kc)
        return (C_new, n_new, m_new), h

    init = (jnp.zeros((B, H, Dh, Dh), jnp.float32), jnp.zeros((B, H, Dh), jnp.float32),
            jnp.zeros((B, H), jnp.float32))
    _, hs = lax.scan(step, init, (chunks(q), chunks(k), chunks(v), gchunks(log_i), gchunks(log_f)))
    return hs.transpose(1, 0, 3, 2, 4).reshape(B, S, H, Dh)

def forgetting_attention(q, k, v, log_f):
    B, S, H, Dh = q.shape
    nb = S // FOX_BLOCK
    c = jnp.cumsum(log_f, axis=1).transpose(0, 2, 1)
    kh = k.transpose(0, 2, 1, 3)
    vh = v.transpose(0, 2, 1, 3)
    qb = (q * (Dh ** -0.5)).reshape(B, nb, FOX_BLOCK, H, Dh).transpose(1, 0, 3, 2, 4)
    cb = c.reshape(B, H, nb, FOX_BLOCK).transpose(2, 0, 1, 3)
    qpos = jnp.arange(S).reshape(nb, FOX_BLOCK)
    kpos = jnp.arange(S)

    def one_block(args):
        qi, ci, pi = args
        logits = jnp.einsum("bhqd,bhkd->bhqk", qi, kh) + ci[..., None] - c[:, :, None, :]
        logits = jnp.where(pi[:, None] >= kpos[None, :], logits, -jnp.inf)
        p = jax.nn.softmax(logits, axis=-1)
        return jnp.einsum("bhqk,bhkd->bhqd", p, vh)

    o = lax.map(one_block, (qb, cb, qpos))
    return o.transpose(1, 0, 3, 2, 4).reshape(B, S, H * Dh)

def hybrid_mixer(h, w_in, mlstm_conv_w, mlstm_conv_b, mlstm_b_i, mlstm_b_f, mlstm_norm_w,
                 conf_conv_w, conf_conv_b, conf_ln_w, conf_ln_b, fox_b_f, w_out):
    B, S, _ = h.shape
    z = jnp.einsum("bsd,de->bse", h, w_in).astype(jnp.float32)
    m_qk, m_v, m_o, m_i, m_f, c_glu, f_q, f_k, f_v, f_f = jnp.split(z, IN_SPLIT_IDX, axis=-1)

    qk = jax.nn.silu(causal_dwconv(m_qk, mlstm_conv_w, mlstm_conv_b))
    mq, mk = jnp.split(qk, 2, axis=-1)
    hd = (B, S, MLSTM_HEADS, MLSTM_HEAD_DIM)
    hm = mlstm_chunkwise(mq.reshape(hd), mk.reshape(hd) * (MLSTM_HEAD_DIM ** -0.5), m_v.reshape(hd),
                         m_i + mlstm_b_i.astype(jnp.float32), m_f + mlstm_b_f.astype(jnp.float32))
    hm = hm * lax.rsqrt(jnp.mean(hm * hm, axis=-1, keepdims=True) + EPS)
    hm = hm.reshape(B, S, MLSTM_WIDTH) * mlstm_norm_w.astype(jnp.float32) * jax.nn.sigmoid(m_o)

    a, g = jnp.split(c_glu, 2, axis=-1)
    hc = causal_dwconv(a * jax.nn.sigmoid(g), conf_conv_w, conf_conv_b)
    hc = jax.nn.silu(layernorm_f32(hc, conf_ln_w, conf_ln_b))

    fd = (B, S, FOX_HEADS, FOX_HEAD_DIM)
    log_f = jax.nn.log_sigmoid(f_f + fox_b_f.astype(jnp.float32))
    hf = forgetting_attention(f_q.reshape(fd), f_k.reshape(fd), f_v.reshape(fd), log_f)

    cat = jnp.concatenate([hm, hc, hf], axis=-1).astype(h.dtype)
    return jnp.einsum("bse,ed->bsd", cat, w_out)

def memory_cross_attention(h, mem_n, w_q, w_kv, w_o):
    B, S, _ = h.shape
    q = jnp.einsum("bsd,de->bse", h, w_q).reshape(B, S, XATTN_HEADS, XATTN_HEAD_DIM)
    kv = jnp.einsum("bmd,de->bme", mem_n, w_kv)
    k, v = jnp.split(kv, 2, axis=-1)
    k = k.reshape(B, N_MEM, XATTN_HEADS, XATTN_HEAD_DIM)
    v = v.reshape(B, N_MEM, XATTN_HEADS, XATTN_HEAD_DIM)
    logits = jnp.einsum("bshd,bmhd->bhsm", q.astype(jnp.float32), k.astype(jnp.float32))
    p = jax.nn.softmax(logits * (XATTN_HEAD_DIM ** -0.5), axis=-1)
    o = jnp.einsum("bhsm,bmhd->bshd", p, v.astype(jnp.float32)).reshape(B, S, XATTN_WIDTH)
    return jnp.einsum("bse,ed->bsd", o.astype(h.dtype), w_o)

def swiglu_2(h, w_gate, w_up, w_down):
    a = jnp.einsum("bsd,df->bsf", h, w_gate)
    u = jnp.einsum("bsd,df->bsf", h, w_up)
    return jnp.einsum("bsf,fd->bsd", jax.nn.silu(a) * u, w_down)

def moe_swiglu(h, router_w, w_gate, w_up, w_down):
    logits = jnp.einsum("bsd,de->bse", h, router_w).astype(jnp.float32)
    top_v, top_i = lax.top_k(logits, TOP_K)
    top_w = jax.nn.softmax(top_v, axis=-1)
    gates = jnp.sum(jax.nn.one_hot(top_i, N_EXPERTS, dtype=jnp.float32) * top_w[..., None], axis=-2)
    y = jnp.zeros(h.shape, jnp.float32)
    for e in range(N_EXPERTS):
        y = y + gates[..., e:e + 1] * swiglu_2(h, w_gate[e], w_up[e], w_down[e]).astype(jnp.float32)
    return y.astype(h.dtype)

def second_inputs(seed: int = 0) -> dict:
    key = jax.random.key(seed)
    ks = jax.random.split(key, 32)

    def nrm(k, shape, scale):
        return jax.random.normal(k, shape, jnp.float32) * scale

    D, L = D_MODEL, DEPTH
    return {
        "x": nrm(ks[0], (BATCH, SEQ, D), 1.0),
        "mem": nrm(ks[1], (BATCH, N_MEM, D), 1.0),
        "norm_mix_w": 1.0 + nrm(ks[2], (L, D), 0.02),
        "w_in": nrm(ks[3], (L, D, IN_WIDTH), D ** -0.5),
        "mlstm_conv_w": nrm(ks[4], (L, MLSTM_CONV, 2 * MLSTM_WIDTH), MLSTM_CONV ** -0.5),
        "mlstm_conv_b": nrm(ks[5], (L, 2 * MLSTM_WIDTH), 0.02),
        "mlstm_b_i": nrm(ks[6], (L, MLSTM_HEADS), 0.1),
        "mlstm_b_f": 3.0 + nrm(ks[7], (L, MLSTM_HEADS), 0.5),
        "mlstm_norm_w": 1.0 + nrm(ks[8], (L, MLSTM_WIDTH), 0.02),
        "conf_conv_w": nrm(ks[9], (L, CONF_KERNEL, CONF_CHANNELS), CONF_KERNEL ** -0.5),
        "conf_conv_b": nrm(ks[10], (L, CONF_CHANNELS), 0.02),
        "conf_ln_w": 1.0 + nrm(ks[11], (L, CONF_CHANNELS), 0.02),
        "conf_ln_b": nrm(ks[12], (L, CONF_CHANNELS), 0.02),
        "fox_b_f": 2.0 + nrm(ks[13], (L, FOX_HEADS), 0.5),
        "w_out": nrm(ks[14], (L, MIX_WIDTH, D), MIX_WIDTH ** -0.5),
        "norm_xattn_w": 1.0 + nrm(ks[15], (L, D), 0.02),
        "norm_mem_w": 1.0 + nrm(ks[16], (L, D), 0.02),
        "xattn_w_q": nrm(ks[17], (L, D, XATTN_WIDTH), D ** -0.5),
        "xattn_w_kv": nrm(ks[18], (L, D, 2 * XATTN_WIDTH), D ** -0.5),
        "xattn_w_o": nrm(ks[19], (L, XATTN_WIDTH, D), XATTN_WIDTH ** -0.5),
        "norm_ffn_w": 1.0 + nrm(ks[20], (L, D), 0.02),
        "ffn_w_gate": nrm(ks[21], (N_DENSE_LAYERS, D, D_FF_2), D ** -0.5),
        "ffn_w_up": nrm(ks[22], (N_DENSE_LAYERS, D, D_FF_2), D ** -0.5),
        "ffn_w_down": nrm(ks[23], (N_DENSE_LAYERS, D_FF_2, D), D_FF_2 ** -0.5),
        "router_w": nrm(ks[24], (N_MOE_LAYERS, D, N_EXPERTS), D ** -0.5),
        "moe_w_gate": nrm(ks[25], (N_MOE_LAYERS, N_EXPERTS, D, EXPERT_FF), D ** -0.5),
        "moe_w_up": nrm(ks[26], (N_MOE_LAYERS, N_EXPERTS, D, EXPERT_FF), D ** -0.5),
        "moe_w_down": nrm(ks[27], (N_MOE_LAYERS, N_EXPERTS, EXPERT_FF, D), EXPERT_FF ** -0.5),
        "norm_final_w": 1.0 + nrm(ks[28], (D,), 0.02),
    }

def second_block(x, mem, norm_mix_w, w_in, mlstm_conv_w, mlstm_conv_b, mlstm_b_i, mlstm_b_f,
              mlstm_norm_w, conf_conv_w, conf_conv_b, conf_ln_w, conf_ln_b, fox_b_f, w_out,
              norm_xattn_w, norm_mem_w, xattn_w_q, xattn_w_kv, xattn_w_o, norm_ffn_w,
              ffn_w_gate, ffn_w_up, ffn_w_down, router_w, moe_w_gate, moe_w_up, moe_w_down,
              norm_final_w):
    for l in range(DEPTH):
        h = rmsnorm_2(x, norm_mix_w[l])
        x = x + hybrid_mixer(h, w_in[l], mlstm_conv_w[l], mlstm_conv_b[l], mlstm_b_i[l], mlstm_b_f[l],
                             mlstm_norm_w[l], conf_conv_w[l], conf_conv_b[l], conf_ln_w[l],
                             conf_ln_b[l], fox_b_f[l], w_out[l])
        h = rmsnorm_2(x, norm_xattn_w[l])
        mem_n = rmsnorm_2(mem, norm_mem_w[l])
        x = x + memory_cross_attention(h, mem_n, xattn_w_q[l], xattn_w_kv[l], xattn_w_o[l])
        h = rmsnorm_2(x, norm_ffn_w[l])
        if l % 2 == 0:
            j = l // 2
            x = x + swiglu_2(h, ffn_w_gate[j], ffn_w_up[j], ffn_w_down[j])
        else:
            j = l // 2
            x = x + moe_swiglu(h, router_w[j], moe_w_gate[j], moe_w_up[j], moe_w_down[j])
    return rmsnorm_2(x, norm_final_w)


def setup_inputs(seed=0):
    out = dict(first_inputs(seed))
    for name, value in second_inputs(seed + 1).items():
        if name != "x":
            out[name + "_2"] = value
    return out


def reference(
    x, c, ctx, c_ctx, w_mod, b_mod, norm1_g, norm2_g, w_in, conv_w, attn_sink, gla_gate_w,
    gla_gate_b, gla_norm_g, w_out, w_up, w_down, final_norm_g, mem_2, norm_mix_w_2, w_in_2,
    mlstm_conv_w_2, mlstm_conv_b_2, mlstm_b_i_2, mlstm_b_f_2, mlstm_norm_w_2, conf_conv_w_2,
    conf_conv_b_2, conf_ln_w_2, conf_ln_b_2, fox_b_f_2, w_out_2, norm_xattn_w_2, norm_mem_w_2,
    xattn_w_q_2, xattn_w_kv_2, xattn_w_o_2, norm_ffn_w_2, ffn_w_gate_2, ffn_w_up_2,
    ffn_w_down_2, router_w_2, moe_w_gate_2, moe_w_up_2, moe_w_down_2, norm_final_w_2,
):
    x = first_block(
        x, c, ctx, c_ctx, w_mod, b_mod, norm1_g, norm2_g, w_in, conv_w, attn_sink, gla_gate_w,
        gla_gate_b, gla_norm_g, w_out, w_up, w_down, final_norm_g,
    )
    return second_block(
        x, mem_2, norm_mix_w_2, w_in_2, mlstm_conv_w_2, mlstm_conv_b_2, mlstm_b_i_2,
        mlstm_b_f_2, mlstm_norm_w_2, conf_conv_w_2, conf_conv_b_2, conf_ln_w_2, conf_ln_b_2,
        fox_b_f_2, w_out_2, norm_xattn_w_2, norm_mem_w_2, xattn_w_q_2, xattn_w_kv_2,
        xattn_w_o_2, norm_ffn_w_2, ffn_w_gate_2, ffn_w_up_2, ffn_w_down_2, router_w_2,
        moe_w_gate_2, moe_w_up_2, moe_w_down_2, norm_final_w_2,
    )


_drawn_inputs = setup_inputs


def setup_inputs(seed=0):
    import zlib

    import numpy as np

    out = dict(_drawn_inputs(seed))
    spreads = {}
    factors = {'attn_sink': 3.886,
     'gla_norm_g': 3.989,
     'mlstm_b_i_2': 51.435,
     'conf_ln_b_2': 3.094,
     'norm_xattn_w_2': 3.54,
     'norm_final_w_2': 8.481,
     'mlstm_norm_w_2': 3.621}
    for name, (base, spread) in spreads.items():
        noise = np.random.default_rng([zlib.crc32(name.encode()), seed]).standard_normal(out[name].shape)
        drawn = base * np.exp(spread * noise) if base else spread * noise
        out[name] = __import__('jax').numpy.asarray(drawn.astype(out[name].dtype))
    for name, factor in factors.items():
        out[name] = (out[name] * factor).astype(out[name].dtype)
    return out
```

```python
from contextlib import ExitStack

import numpy as np

import concourse.bass as bass
from concourse import mybir

F32 = mybir.dt.float32
U8 = mybir.dt.uint8
ALU = mybir.AluOpType
ACT = mybir.ActivationFunctionType
AX = mybir.AxisListType

P = 128
D = 1024
KT = D // P
T = 256
TT = T // P
EPS = 1e-6
DEPTH = 2
FF = 2816
FT = FF // P
HD = 64
N_EXP = 8
PIECE = 2048
SLOTS = 11
FFN_PIECES = FT + 2 * FT // 4
MOD_PIECES = 6 * D // 256
NEG = -1.0e30

B1_COLS = dict(b_mod=48, norm1=8, norm2=8, conv_w=6, sink=8, gla_g=1)
B2_COLS = dict(norm_mix=8, m_conv_w=16, m_conv_b=4, gate_b=16, m_norm=2, c_conv_w=62, c_conv_b=2,
               ln_w=2, ln_b=2, norm_x=8, norm_mem=8, norm_ffn=8)


def vector_columns():
    at, n = {}, 0
    for layer in range(DEPTH):
        for name, width in B1_COLS.items():
            at[name, layer] = (n, n + width)
            n += width
    for layer in range(DEPTH):
        for name, width in B2_COLS.items():
            at[name, layer] = (n, n + width)
            n += width
    for name, width in dict(final1=8, final2=8, c=16).items():
        at[name, 0] = (n, n + width)
        n += width
    return at, n


VEC, N_VEC = vector_columns()

CONST = {}
N_CONST = 0
for _name, _w in (("ident", P), ("mean", P), ("head_mean", P), ("tri", P), ("tri_r", P), ("ones", P),
                  ("strict", P), ("rot", P), ("masks", 7 * P), ("cos", T), ("sin", T)):
    CONST[_name] = (N_CONST, N_CONST + _w)
    N_CONST += _w
LEVELS = 7


def build(nc, A, y_out):
    with ExitStack() as ctx:
        def sb(name, shape, dt=F32):
            return ctx.enter_context(nc.sbuf_tensor(name, shape, dt))

        xT = sb("xT", [P, KT, 2 * T])
        hT = sb("hT", [P, KT, 2 * T])
        Z = sb("Z", [P, FT * 2 * T])
        mixT = sb("mixT", [P, KT, 2 * T])
        tok = sb("tok", [P, 4 * 384])
        ring = sb("ring", [P, SLOTS, PIECE])
        cst = sb("cst", [P, N_CONST])
        vec = sb("vec", [P, N_VEC])
        lvl_mask = sb("lvl_mask", [P, 2 * LEVELS, P], U8)
        gate_w = sb("gate_w", [17, DEPTH, 2, 256])
        lr_w = sb("lr_w", [P, DEPTH, KT, 32])
        sg_w = sb("sg_w", [P, DEPTH, KT, 16])
        rt_w = sb("rt_w", [P, KT, N_EXP])
        modT = sb("modT", [P, 48, 2])
        a1 = sb("a1", [P, 2, KT, 2])
        sc = sb("sc", [P, 96])
        psum = ctx.enter_context(nc.psum_tensor("psum", [P, 8, 512], F32))
        bank = [psum[:, i, :] for i in range(8)]
        Zt = Z[:, :].rearrange("p (f n) -> p f n", n=2 * T)
        hflat = hT[:, :, :].rearrange("p a b -> p (a b)")
        mixflat = mixT[:, :, :].rearrange("p a b -> p (a b)")

        def const(name, lo=0, hi=None):
            a, b = CONST[name]
            return cst[:, a + lo:(b if hi is None else a + hi)]

        def v(name, layer=0, lo=0, hi=None):
            a, b = VEC[name, layer]
            return vec[:, a + lo:(b if hi is None else a + hi)]

        sems, seen = {}, {}

        def sem(name):
            if name not in sems:
                sems[name] = ctx.enter_context(nc.semaphore(name))
            return sems[name]

        def await_next(e, name, n=1):
            k = seen[e.engine, name] = seen.get((e.engine, name), 0) + n
            e.wait_ge(sem(name), k)

        def base(e, name):
            return seen.get((e.engine, name), 0)

        def advance(e, name, n):
            seen[e.engine, name] = base(e, name) + n

        def link(e, ins):
            name = f"own_{str(e.engine).split('.')[-1]}"
            ins.then_inc(sem(name), 1)
            await_next(e, name)

        def phase_end(e):
            me = {nc.tensor.engine: "pe", nc.scalar.engine: "act", nc.vector.engine: "dve"}[e.engine]
            e.drain().then_inc(sem(f"phase_{me}"), 1)
            for other in ("pe", "act", "dve"):
                if other != me:
                    await_next(e, f"phase_{other}")

        n_pieces = A["stream"].shape[0]
        stream = {"n": 0, "release": False}

        def piece_slot(pe, first_of_loop=None, it=0):
            n = stream["n"]
            stream["n"] += 1
            pe.wait_ge(sem(f"piece_in_{n % SLOTS}"), 16 * (n // SLOTS + 1) + it * (16 * FFN_PIECES // SLOTS))
            return ring[:, n % SLOTS, :]

        def mm(pe, *args, last_of=None, **kw):
            ins = pe.matmul(*args, **kw)
            if last_of:
                ins.then_inc(sem(last_of), 1)
            elif stream["release"]:
                ins.then_inc(sem("piece_used"), 1)
                stream["release"] = False
            return ins

        def whose(g, who):
            return who or ("act" if g % 2 == 0 else "dve")

        def pe_products(pe, groups, who=None):
            counts = {"act": base(pe, "product_out_act"), "dve": base(pe, "product_out_dve")}
            ends = []
            for g, (pairs, lo, hi, n, _, held) in enumerate(groups):
                if g >= 4:
                    w, k = ends[g - 4]
                    pe.wait_ge(sem(f"product_out_{w}"), k)
                if held == "new":
                    slot = piece_slot(pe)
                    cur = slot
                ps = bank[g % 4][lo:hi, 0:n]
                for k, (l, r) in enumerate(pairs):
                    l = l(cur) if callable(l) else l
                    r = r(cur) if callable(r) else r
                    last = k == len(pairs) - 1
                    mm(pe, ps, l, r, start=k == 0, stop=last,
                       last_of=f"product_in_{whose(g, who)}" if last else None)
                nxt = groups[g + 1][5] if g + 1 < len(groups) else "new"
                if nxt in ("new", None) and held is not None:
                    stream["release"] = True
                w = whose(g, who)
                counts[w] += 1
                ends.append((w, counts[w]))
            for w, k in counts.items():
                seen[pe.engine, f"product_out_{w}"] = k

        def take_products(e, me, groups, who=None):
            for g, (_, lo, hi, n, evs, _) in enumerate(groups):
                if whose(g, who) != me:
                    continue
                await_next(e, f"product_in_{me}")
                for k, ev in enumerate(evs):
                    if ev[0] == "copy":
                        _, out, scale, a, b = ev
                        src = bank[g % 4][lo:hi, a:b]
                        if me == "act":
                            ins = e.activation(out, src, ACT.Copy, scale=scale)
                        elif scale == 1.0:
                            ins = e.tensor_copy(out, src)
                        else:
                            ins = e.tensor_scalar(out, src, scale, None, ALU.mult)
                    else:
                        _, x, gain, a, b = ev
                        ins = e.scalar_tensor_tensor(x, bank[g % 4][lo:hi, a:b], gain, x, ALU.mult, ALU.add)
                ins.then_inc(sem(f"product_out_{me}"), 1)

        def copy(out, n, scale=1.0):
            return [("copy", out, scale, 0, n)]

        def feature_major(outs, a, b, scale=1.0, cols=256):
            res = []
            for c, out in enumerate(outs):
                pairs = [((lambda s, k=k, c=c: s[:, k * cols + c * P:k * cols + (c + 1) * P]), hT[:, k, a:b])
                         for k in range(KT)]
                res.append((pairs, 0, P, b - a, copy(out, b - a, scale), "new" if c == 0 else "same"))
            return res

        def token_major(outs, first=0, lo=0, hi=256, held="new"):
            res = []
            for i, out in enumerate(outs):
                t0 = (first + i) * P
                pairs = [(hT[:, k, t0:t0 + P], (lambda s, k=k: s[:, k * 256 + lo:k * 256 + hi]))
                         for k in range(KT)]
                res.append((pairs, 0, P, hi - lo, copy(out, hi - lo), held if i == 0 else "same"))
            return res

        def pe_norm(pe, n0, n1):
            for k in range(KT):
                await_next(pe, "squared")
                mm(pe, bank[0][:, n0:n1], const("mean"), hT[:, k, n0:n1], start=k == 0, stop=k == KT - 1,
                   last_of="mean_square" if k == KT - 1 else None)
            phase_end(pe)

        def act_norm(act, n0, n1, segments):
            for k in range(KT):
                act.activation(hT[:, k, n0:n1], xT[:, k, n0:n1], ACT.Square).then_inc(sem("squared"), 1)
            await_next(act, "mean_square")
            rs = mixT[:, 0, n0:n1]
            link(act, act.activation(rs, bank[0][:, n0:n1], ACT.Ln, bias=EPS))
            act.activation(rs, rs, ACT.Exp, scale=-0.5).then_inc(sem("inverse_rms"), 1)
            if segments[0][3] is not None:
                for k in range(KT):
                    await_next(act, "normed")
                    for a, b, gain, shift in segments:
                        act.activation(hT[:, k, a:b], hT[:, k, a:b], ACT.Identity, bias=shift(k))
            phase_end(act)

        def dve_norm(dve, n0, n1, segments):
            await_next(dve, "inverse_rms")
            for k in range(KT):
                for a, b, gain, shift in segments:
                    ins = dve.scalar_tensor_tensor(hT[:, k, a:b], xT[:, k, a:b], gain(k), mixT[:, 0, a:b],
                                                   ALU.mult, ALU.mult)
                if segments[0][3] is not None:
                    ins.then_inc(sem("normed"), 1)
            phase_end(dve)

        def hid(f, n):
            return Z[:, f * n:(f + 1) * n]

        def pe_ffn(pe, n, run, it=0):
            for f in range(FT):
                slot = piece_slot(pe, it=it)
                if f >= 2:
                    pe.wait_ge(sem("hidden"), run * FT + f - 1)
                for half, b in ((0, 2 * (f % 2)), (1, 2 * (f % 2) + 1)):
                    for k in range(KT):
                        last = half == 1 and k == KT - 1
                        mm(pe, bank[b][:, 0:n], slot[:, k * 256 + half * P:k * 256 + (half + 1) * P],
                           hT[:, k, 0:n], start=k == 0, stop=k == KT - 1, last_of="up" if last else None)
                stream["release"] = True
            for q in range(2 * FT):
                half, f = divmod(q, FT)
                if q % 4 == 0:
                    slot = piece_slot(pe, it=it)
                if half == 0:
                    pe.wait_ge(sem("hidden"), run * FT + f + 1)
                for d in range(4):
                    if f == 0 and half == 1:
                        pe.wait_ge(sem("down_added"), run * 8 + d + 1)
                    mm(pe, bank[4 + d][:, 0:n], slot[:, (q % 4) * 512 + d * P:(q % 4) * 512 + (d + 1) * P],
                       hid(f, n), start=f == 0, stop=f == FT - 1,
                       last_of="down" if f == FT - 1 else None)
                if q % 4 == 3:
                    stream["release"] = True

        def act_ffn(act, n, run):
            for f in range(FT):
                act.wait_ge(sem("up"), run * FT + f + 1)
                if f >= 2:
                    act.wait_ge(sem("hidden"), run * FT + f - 1)
                act.activation(mixT[:, f % 2, 0:n], bank[2 * (f % 2)][:, 0:n], ACT.Silu)\
                   .then_inc(sem("silu"), 1)

        def dve_ffn(dve, n, run, gains=None, expert=None):
            for f in range(FT):
                dve.wait_ge(sem("silu"), run * FT + f + 1)
                dve.tensor_tensor(hid(f, n), mixT[:, f % 2, 0:n], bank[2 * (f % 2) + 1][:, 0:n], ALU.mult)\
                   .then_inc(sem("hidden"), 1)
            for q in range(8):
                dve.wait_ge(sem("down"), run * 8 + q + 1)
                ps = bank[4 + q % 4]
                if expert is not None:
                    dve.tensor_tensor(mixT[:, 2 + q % 2, 0:n], ps[:, 0:n], expert, ALU.mult)\
                       .then_inc(sem("gated"), 1)
                    dve.wait_ge(sem("gated"), (run - 3) * 8 + q + 1)
                    dve.tensor_tensor(xT[:, q, 0:n], xT[:, q, 0:n], mixT[:, 2 + q % 2, 0:n], ALU.add)\
                       .then_inc(sem("down_added"), 1)
                else:
                    for s in range(n // T):
                        gain = gains(q, s)
                        ins = dve.scalar_tensor_tensor(xT[:, q, s * T:(s + 1) * T], ps[:, s * T:(s + 1) * T],
                                                       gain, xT[:, q, s * T:(s + 1) * T], ALU.mult, ALU.add)
                    ins.then_inc(sem("down_added"), 1)

        S = [hT[:, i, 0:512] for i in range(2)]
        PT = [hT[:, 2 + i, 0:512] for i in range(2)]

        def pe_attention(pe, units):
            n = len(units)
            s_rd, p_rdy, pt_cp, o_cp = (base(pe, x) for x in ("scores_read", "probs", "probs_turned", "heads_out"))
            for i in range(n + 2):
                if i < n:
                    u = units[i]
                    if i >= 2:
                        pe.wait_ge(sem("scores_read"), s_rd + i - 1)
                    for j, (l, r, m) in enumerate(u["scores"]):
                        last = j == len(u["scores"]) - 1
                        mm(pe, bank[(6 if u["apart"] else 0) + i % 2][:, 0:m], l, r, start=j == 0, stop=last,
                           last_of="scores" if last and not u["apart"] else None)
                    if u["apart"]:
                        l, r = u["apart"]
                        mm(pe, bank[i % 2][:, 0:u["nk"]], l, r, start=True, stop=True, last_of="scores")
                if 1 <= i <= n:
                    u, j = units[i - 1], i - 1
                    pe.wait_ge(sem("probs"), p_rdy + j + 1)
                    if j >= 2:
                        pe.wait_ge(sem("probs_turned"), pt_cp + j - 1)
                    for b in range(u["nk"] // P):
                        ins = pe.transpose(bank[2 + j % 2][:, b * P:(b + 1) * P],
                                           S[j % 2][:, b * P:(b + 1) * P], const("ident"))
                    ins.then_inc(sem("turned"), 1)
                if i >= 2:
                    u, j = units[i - 2], i - 2
                    pe.wait_ge(sem("probs_turned"), pt_cp + j + 1)
                    if j >= 2:
                        pe.wait_ge(sem("heads_out"), o_cp + j - 1)
                    lo, hi = u["rows"]
                    for b, vt in enumerate(u["v"]):
                        last = b == len(u["v"]) - 1
                        mm(pe, bank[4 + j % 2][lo:hi, 0:P], vt, PT[j % 2][:, b * P:(b + 1) * P],
                           start=b == 0, stop=last, last_of="mixed" if last else None)
            for x in ("scores_read", "probs", "probs_turned", "heads_out"):
                advance(pe, x, n)

        def act_attention(act, units):
            n = len(units)
            nm, td, mx = (base(act, x) for x in ("neg_max", "turned", "mixed"))
            for i in range(n + 2):
                if i < n:
                    u = units[i]
                    col = (i % 2) * 8
                    act.wait_ge(sem("neg_max"), nm + i + 1)
                    if u["apart"]:
                        act.activation(sc[:, col + 3:col + 4], sc[:, col + 1:col + 2], ACT.Exp)
                        act.activation(S[i % 2][:, 0:u["nk"]], S[i % 2][:, 0:u["nk"]], ACT.Exp,
                                       bias=sc[:, col + 1:col + 2]).then_inc(sem("exps"), 1)
                    else:
                        if u["sink"] is not None:
                            act.activation(sc[:, col + 3:col + 4], u["sink"], ACT.Exp, bias=sc[:, col + 1:col + 2])
                        act.activation(S[i % 2][:, 0:u["nk"]], S[i % 2][:, 0:u["nk"]], ACT.Exp,
                                       bias=sc[:, col + 1:col + 2], accum_out=sc[:, col + 2:col + 3])\
                           .then_inc(sem("exps"), 1)
                if 1 <= i <= n:
                    u, j = units[i - 1], i - 1
                    act.wait_ge(sem("turned"), td + j + 1)
                    if j >= 2:
                        act.wait_ge(sem("mixed"), mx + j - 1)
                    act.activation(PT[j % 2][:, 0:u["nk"]], bank[2 + j % 2][:, 0:u["nk"]], ACT.Copy)\
                       .then_inc(sem("probs_turned"), 1)
                if i >= 2:
                    u, j = units[i - 2], i - 2
                    act.wait_ge(sem("mixed"), mx + j + 1)
                    lo, hi = u["rows"]
                    act.activation(u["out"], bank[4 + j % 2][lo:hi, 0:P], ACT.Copy)\
                       .then_inc(sem("heads_out"), 1)
            for x in ("neg_max", "turned", "mixed"):
                advance(act, x, n)

        def dve_attention(dve, units):
            n = len(units)
            so, ex, td = (base(dve, x) for x in ("scores", "exps", "turned"))
            for i in range(n + 1):
                if i < n:
                    u = units[i]
                    col = (i % 2) * 8
                    dve.wait_ge(sem("scores"), so + i + 1)
                    if i >= 2:
                        dve.wait_ge(sem("turned"), td + i - 1)
                    src = bank[6 + i % 2] if u["apart"] else bank[i % 2]
                    ins = dve.tensor_tensor_reduce(S[i % 2][:, 0:u["nk"]], src[:, 0:u["nk"]], u["mask"], 1.0,
                                                   u["init"], ALU.add, ALU.max, sc[:, col:col + 1])
                    if u["apart"]:
                        link(dve, ins)
                    else:
                        ins.then_inc(sem("scores_read"), 1)
                        await_next(dve, "scores_read")
                    dve.tensor_scalar(sc[:, col + 1:col + 2], sc[:, col:col + 1], -1.0, None, ALU.mult)\
                       .then_inc(sem("neg_max"), 1)
                if i >= 1:
                    u, j = units[i - 1], i - 1
                    col = (j % 2) * 8
                    den = sc[:, col + 2:col + 3]
                    Sj = S[j % 2][:, 0:u["nk"]]
                    dve.wait_ge(sem("exps"), ex + j + 1)
                    if u["apart"]:
                        ins = dve.tensor_tensor_reduce(Sj, bank[j % 2][:, 0:u["nk"]], Sj, HD ** -0.5, 0.0, ALU.mult,
                                                       ALU.add, den)
                        ins.then_inc(sem("scores_read"), 1)
                        await_next(dve, "scores_read")
                        link(dve, dve.tensor_scalar(sc[:, col + 4:col + 5], den, -1.0, None, ALU.mult))
                        link(dve, dve.tensor_tensor(den, den, sc[:, col + 4:col + 5], ALU.max))
                        link(dve, dve.tensor_tensor(den, den, sc[:, col + 3:col + 4], ALU.max))
                    elif u["sink"] is not None:
                        link(dve, dve.tensor_tensor(den, den, sc[:, col + 3:col + 4], ALU.add))
                    link(dve, dve.reciprocal(sc[:, col + 5:col + 6], den))
                    dve.tensor_scalar(Sj, Sj, sc[:, col + 5:col + 6], None, ALU.mult).then_inc(sem("probs"), 1)
            for x in ("scores", "exps", "turned"):
                advance(dve, x, n)

        def dve_log_sigmoid_a(dve, z, t):
            link(dve, dve.tensor_scalar(t, z, -1.0, None, ALU.mult))
            dve.tensor_tensor(t, t, z, ALU.min).then_inc(sem("neg_abs"), 1)

        def act_log_sigmoid(act, t):
            await_next(act, "neg_abs")
            link(act, act.activation(t, t, ACT.Exp))
            act.activation(t, t, ACT.Ln, bias=1.0).then_inc(sem("log1p"), 1)

        def dve_log_sigmoid_b(dve, z, t, scale):
            link(dve, dve.tensor_scalar(z, z, 0.0, scale, ALU.min, ALU.mult))
            await_next(dve, "log1p")
            link(dve, dve.scalar_tensor_tensor(z, t, -scale, z, ALU.mult, ALU.add))

        G_X, G_CTX = (0, T), (T, 2 * T)

        def b1_groups(layer):
            n = 2 * T if layer == 0 else T
            zt = lambda i, b=n: Zt[:, i, 0:b]
            g = []
            for j, tiles in enumerate(((0, 1), (2, 3), (4, 5))):
                g += feature_major([zt(i) for i in tiles], 0, n)
            for tiles in ((6, 7), (8, 9)):
                g += feature_major([zt(i) for i in tiles], 0, n, HD ** -0.5)
            g += feature_major([zt(10, 2 * T)], 0, 2 * T)
            g += token_major([tok[:, t * 384:t * 384 + P] for t in range(4)], 0, P, 256, "same")
            g += feature_major([zt(11), zt(12)], 0, n, HD ** -0.5)
            g += feature_major([zt(13, 2 * T), zt(14, 2 * T)], 0, 2 * T)
            g += token_major([tok[:, t * 384 + P:(t + 1) * 384] for t in range(4)])
            g += feature_major([zt(15), zt(16)], 0, n)
            for d in range(2):
                g.append(([(lr_w[:, layer, k, 16 * d:16 * (d + 1)], hT[:, k, :]) for k in range(KT)],
                          0, 16, 2 * T, copy(lrT(d), 2 * T), None))
            return g

        lr_ones = Zt[0:32, 17:19, :]

        def lrT(d):
            return Zt[0:16, 17 + d, :]

        def pe_mod(pe, layer):
            if layer == 0:
                await_next(pe, "silu_c")
            for p in range(MOD_PIECES):
                slot = piece_slot(pe)
                for c in range(2):
                    j = 2 * p + c
                    for k in range(KT):
                        last = j == 47 and k == KT - 1
                        mm(pe, bank[0][:, 2 * j:2 * j + 2], slot[:, k * 256 + c * P:k * 256 + (c + 1) * P],
                           v("c")[:, 2 * k:2 * k + 2], start=k == 0, stop=k == KT - 1,
                           last_of="modulation" if last else None)
                stream["release"] = True
            phase_end(pe)

        def act_mod(act, layer):
            if layer == 0:
                act.wait_ge(sem("vectors_in"), 16 * N_LOADS)
                act.activation(v("c"), v("c"), ACT.Silu).then_inc(sem("silu_c"), 1)
            phase_end(act)

        def dve_mod(dve, layer):
            dve.memset(lr_ones, 1.0)
            if layer == 0:
                dve.wait_ge(sem("vectors_in"), 16 * N_LOADS)
                dve.tensor_copy(lvl_mask[:, :, :].rearrange("p l n -> p (l n)"), Z[:, 0:2 * LEVELS * P])
            await_next(dve, "modulation")
            link(dve, dve.tensor_tensor(modT[:, :, :], bank[0][:, 0:96].rearrange("p (j s) -> p j s", s=2),
                                        v("b_mod", layer).unsqueeze(2).to_broadcast([P, 48, 2]), ALU.add))
            for i, name in ((0, "norm1"), (1, "norm2")):
                lo = 8 + 24 * i
                dve.scalar_tensor_tensor(a1[:, i, :, :], modT[:, lo:lo + 8, :], 1.0,
                                         v(name, layer).unsqueeze(2).to_broadcast([P, KT, 2]),
                                         ALU.add, ALU.mult)
            phase_end(dve)

        def b1_segments(which, n):
            segs = [(s * T, (s + 1) * T,
                     (lambda k, s=s: a1[:, which, k, s:s + 1]),
                     (lambda k, s=s: modT[:, 24 * which + k, s:s + 1])) for s in range(n // T)]
            return segs

        U = Zt[:, 19:22, :].rearrange("p a b -> p (a b)")[:, 0:2 * 2 * 258].rearrange("p (c s n) -> p c s n", c=2, s=2)

        def pe_rope(pe, layer):
            for j in range(5):
                if j >= 4:
                    await_next(pe, "rotated_read")
                mm(pe, bank[j % 4][:, 0:T], const("rot"), Zt[:, 6 + j, 0:T], start=True, stop=True,
                   last_of="rotated")
            advance(pe, "rotated_read", 4)
            phase_end(pe)

        def act_rope(act, layer):
            phase_end(act)

        def dve_rope_conv(dve, layer):
            for j in range(5):
                await_next(dve, "rotated")
                z, t = Zt[:, 6 + j, 0:T], hT[:, j, 0:T]
                dve.tensor_tensor(t, bank[j % 4][:, 0:T], const("sin"), ALU.mult).then_inc(sem("rotated_read"), 1)
                link(dve, dve.tensor_tensor(z, z, const("cos"), ALU.mult))
                await_next(dve, "rotated_read")
                dve.tensor_tensor(z, z, t, ALU.add)
            ns = 2 if layer == 0 else 1
            link(dve, dve.memset(U[:, :, :, :], 0.0))
            for c in range(2):
                seg = lambda i: Zt[:, i + c, 0:ns * T].rearrange("p (s n) -> p s n", s=ns)
                w = lambda j: v("conv_w", layer, 2 * j + c, 2 * j + c + 1)
                y = hT[:, 5 + c, 0:ns * T].rearrange("p (s n) -> p s n", s=ns)
                link(dve, dve.tensor_tensor(U[:, c, 0:ns, 1:T + 1], seg(0), seg(4), ALU.mult))
                link(dve, dve.tensor_scalar(y, U[:, c, 0:ns, 0:T], w(0), None, ALU.mult))
                for j in (1, 2):
                    link(dve, dve.scalar_tensor_tensor(y, U[:, c, 0:ns, j:T + j], w(j), y, ALU.mult, ALU.add))
                link(dve, dve.tensor_tensor(mixT[:, c, 0:ns * T].rearrange("p (s n) -> p s n", s=ns), y, seg(2),
                                            ALU.mult))
            phase_end(dve)

        def b1_units(layer):
            units = []
            for s in range(2 if layer == 0 else 1):
                for h in range(8):
                    g, t = divmod(h, 4)
                    r0 = g * HD
                    for q in range(TT):
                        tq = s * T + q * P
                        keys = (0, 2 * T) if s == 0 else (T, 2 * T)
                        nk = keys[1] - keys[0]
                        if s == 0:
                            mask = const("masks", 0, 512) if q == 1 else const("masks", 384, 896)
                        else:
                            mask = const("masks", 128, 384)
                        units.append(dict(apart=None,
                            scores=[(Zt[r0:r0 + HD, 6 + t, tq:tq + P], Zt[r0:r0 + HD, 10, keys[0]:keys[1]], nk)],
                            nk=nk, mask=mask, init=v("sink", layer, h, h + 1), sink=v("sink", layer, h, h + 1),
                            v=[tok[:, b * 384 + g * HD:b * 384 + (g + 1) * HD] for b in range(keys[0] // P, keys[1] // P)],
                            rows=((h % 2) * HD, (h % 2 + 1) * HD),
                            out=mixT[(h % 2) * HD:(h % 2 + 1) * HD, 2 + h // 2, tq:tq + P]))
            return units

        gB = [hflat[:, d * 1024:(d + 1) * 1024].rearrange("p (c n) -> p c n", c=2) for d in range(2)]
        gG = hflat[:, 2048:4096].rearrange("p (t c) -> p t c", t=4)
        gM = [Z[:, i * 1024:(i + 1) * 1024].rearrange("p (c n) -> p c n", c=2) for i in range(2)]
        gE = [Z[:, (2 + i) * 1024:(3 + i) * 1024].rearrange("p (c n) -> p c n", c=2) for i in range(2)]
        gA = Z[:, 19 * 512 - 1024:19 * 512 + 1024].rearrange("p (t h n) -> p t h n", t=4, h=4)
        gK = Z[:, 4096:4352].rearrange("p (c n) -> p c n", c=2)
        gKt = Z[:, 4352:4608]
        gS = Z[:, 4608:5120].rearrange("p (d c n) -> p d c n", d=2, c=2)
        gX = Z[:, 5120:5376].rearrange("p (c n) -> p c n", c=2)
        gQ = Z[:, 0:2048].rearrange("p (d t c n) -> p d t c n", d=2, t=4, c=2)
        gD = sc[:, 16:32].rearrange("p (d t c) -> p d t c", d=2, t=4)

        GQ, GK = Zt[:, 11:13, :], Zt[:, 13:15, :]
        ORDER = ((2, 3, 0, 1), (3, 2, 1, 0))

        def pe_gla_gates(pe, layer):
            for t in range(4):
                for d in range(2):
                    ps = bank[t][:, d * 256:(d + 1) * 256]
                    mm(pe, ps, lr_ones[0:17, d, t * P:(t + 1) * P], gate_w[:, layer, d, :], start=True, stop=True,
                       last_of="gates" if d == 1 else None)
            await_next(pe, "log_gates")
            for d in range(2):
                for c in range(2):
                    for t in range(4):
                        mm(pe, bank[4 + 2 * d + c][:, t * P:(t + 1) * P], gG[:, t, d * 256 + c * P:d * 256 + (c + 1) * P],
                           const("tri" if d == 0 else "tri_r"), start=True, stop=True,
                           last_of="decays" if t == 3 else None)
            phase_end(pe)

        def act_gla_gates(act, layer):
            act_log_sigmoid(act, Z[:, 0:2048])
            for d in range(2):
                for c in range(2):
                    await_next(act, "decays")
                    link(act, act.activation(gB[d][:, c, :], bank[4 + 2 * d + c][:, :], ACT.Copy))
                    edge = slice(P - 1, 512, P) if d == 0 else slice(0, 512, P)
                    act.activation(gD[:, d, :, c], gB[d][:, c, edge], ACT.Exp)
            phase_end(act)

        def dve_gla_gates(dve, layer):
            for t in range(4):
                await_next(dve, "gates")
                ins = dve.tensor_copy(gG[:, t, :], bank[t][:, :])
            link(dve, ins)
            g = hflat[:, 2048:4096]
            dve_log_sigmoid_a(dve, g, Z[:, 0:2048])
            link(dve, dve.tensor_scalar(g, g, 0.0, 1.0 / 16, ALU.min, ALU.mult))
            await_next(dve, "log1p")
            dve.scalar_tensor_tensor(g, Z[:, 0:2048], -1.0 / 16, g, ALU.mult, ALU.add).then_inc(sem("log_gates"), 1)
            phase_end(dve)

        def gla_level(l, buf, d, n):
            h = 1 << l
            x = buf[:, :, 0:n].rearrange("p c (b u h) -> p c b u h", u=2, h=h)
            return x[:, :, :, 0, :], x[:, :, :, 1, :]

        def gram(t, h):
            return bank[2 * t + h % 2][:, (h // 2) * P:(h // 2 + 1) * P]

        def grams(t):
            return psum[:, 2 * t:2 * t + 2, 0:2 * P].rearrange("p u (v n) -> p u v n", v=2)

        def by_bank(t):
            return gA[:, t].rearrange("p (v u) n -> p u v n", v=2)

        def gla_steps():
            return [(l, d) for l in range(LEVELS) for d in range(2)]

        def pe_gla_levels(pe, layer):
            tiles = range(4 if layer == 0 else 2)
            for t in tiles:
                for h in range(4):
                    r = slice((h % 2) * HD, (h % 2 + 1) * HD)
                    mm(pe, gram(t, h), GK[r, h // 2, t * P:(t + 1) * P],
                       GQ[r, h // 2, t * P:(t + 1) * P], start=True, stop=True,
                       last_of="grams" if h == 3 else None)
            rd = base(pe, "gram_read")
            nt = len(tiles)
            for i, (l, d) in enumerate(gla_steps()):
                await_next(pe, "level")
                for t in tiles:
                    pe.wait_ge(sem("gram_read"), rd + i * nt + t + 1)
                    for h in range(4):
                        r = slice((h % 2) * HD, (h % 2 + 1) * HD)
                        m = gM[i % 2][r, h // 2, t * P:(t + 1) * P]
                        mm(pe, gram(t, h), m, m, start=True, stop=True,
                           last_of="grams" if h == 3 else None)
            advance(pe, "gram_read", nt * (1 + 2 * LEVELS))
            phase_end(pe)

        def act_gla_levels(act, layer):
            n = 2 * T if layer == 0 else T
            for i, (l, d) in enumerate(gla_steps()):
                await_next(act, "level_decay")
                e = gE[i % 2][:, :, 0:n]
                act.activation(e, e, ACT.Exp).then_inc(sem("level_exp"), 1)
            phase_end(act)

        def dve_gla_levels(dve, layer):
            n = 2 * T if layer == 0 else T
            nt = n // P
            steps = gla_steps()

            def decay(i):
                l, d = steps[i]
                h = 1 << l
                lo, hi = gla_level(l, gB[d], d, n)
                e_lo, e_hi = gla_level(l, gE[i % 2], d, n)
                m = (lo[:, :, :, h - 1:h] if d == 0 else hi[:, :, :, 0:1])
                for c in range(2):
                    mb = m[:, c].to_broadcast([P, n // (2 * h), h])
                    a, b = (hi, lo) if d == 0 else (lo, hi)
                    ea, eb = (e_hi, e_lo) if d == 0 else (e_lo, e_hi)
                    dve.tensor_tensor(ea[:, c], a[:, c], mb, ALU.subtract)
                    ins = dve.tensor_tensor(eb[:, c], mb, b[:, c], ALU.subtract)
                ins.then_inc(sem("level_decay"), 1)

            def scaled(i):
                l, d = steps[i]
                q_lo, q_hi = gla_level(l, GQ, d, n)
                k_lo, k_hi = gla_level(l, GK, d, n)
                e_lo, e_hi = gla_level(l, gE[i % 2], d, n)
                m_lo, m_hi = gla_level(l, gM[i % 2], d, n)
                await_next(dve, "level_exp")
                if i >= 2:
                    dve.wait_ge(sem("grams"), gr + nt * i)
                for c in range(2):
                    dve.tensor_tensor(m_lo[:, c], (k_lo if d == 0 else q_lo)[:, c], e_lo[:, c], ALU.mult)
                    ins = dve.tensor_tensor(m_hi[:, c], (q_hi if d == 0 else k_hi)[:, c], e_hi[:, c], ALU.mult)
                ins.then_inc(sem("level"), 1)

            gr = base(dve, "grams")
            own = base(dve, "gram_read")
            decay(0)
            for t in range(nt):
                dve.wait_ge(sem("grams"), gr + t + 1)
                eye = const("ident").unsqueeze(1).to_broadcast([P, 2, P])
                for u in range(2):
                    ins = dve.scalar_tensor_tensor(by_bank(t)[:, u], grams(t)[:, u], 2.0, eye, ALU.mult, ALU.mult)
                ins.then_inc(sem("gram_read"), 1)
            for i, (l, d) in enumerate(steps):
                scaled(i)
                if i + 1 < len(steps):
                    decay(i + 1)
                mask = lvl_mask[:, 2 * l + d, :].unsqueeze(1).unsqueeze(1).to_broadcast([P, 2, 2, P])
                for t in range(nt):
                    dve.wait_ge(sem("grams"), gr + nt * (i + 1) + t + 1)
                    dve.wait_ge(sem("gram_read"), own + nt * i + t + 1)
                    dve.copy_predicated(by_bank(t), mask, grams(t))\
                       .then_inc(sem("gram_read"), 1)
            advance(dve, "grams", nt * (1 + 2 * LEVELS))
            advance(dve, "gram_read", nt * (1 + 2 * LEVELS))
            phase_end(dve)

        def pe_gla_out(pe, layer):
            outs = (0, 1, 2, 3) if layer == 0 else (0, 1)
            await_next(pe, "queries_decayed")
            first = {t: True for t in outs}
            for d in range(2):
                for i, t in enumerate(ORDER[d]):
                    if i > 0 and t in outs:
                        await_next(pe, "state")
                        for c in range(2):
                            mm(pe, bank[t][:, c * P:(c + 1) * P], gS[:, d, c, :], gQ[:, d, t, c, :],
                               start=first[t] and c == 0, stop=False, skip_group_check=True,
                               last_of="state_used" if c == 1 else None)
                        first[t] = False
                    elif i > 0:
                        await_next(pe, "state")
                        pe.nop().then_inc(sem("state_used"), 1)
                    if i < 3:
                        await_next(pe, "keys_decayed")
                        for c in range(2):
                            ins = pe.transpose(bank[4][:, c * P:(c + 1) * P], gK[:, c, :], const("ident"))
                        ins.then_inc(sem("keys_turned"), 1)
                        await_next(pe, "keys_copied")
                        for c in range(2):
                            mm(pe, bank[5][:, c * P:(c + 1) * P], gKt[:, c * P:(c + 1) * P],
                               tok[:, t * 384 + P + c * P:t * 384 + P + (c + 1) * P], start=True, stop=True,
                               last_of="state_step" if c == 1 else None)
            for t in outs:
                for h in range(4):
                    mm(pe, bank[t][(h % 2) * HD:(h % 2 + 1) * HD, (h // 2) * P:(h // 2 + 1) * P],
                       tok[:, t * 384 + P + h * HD:t * 384 + P + (h + 1) * HD], gA[:, t, h, :],
                       start=False, stop=True, skip_group_check=True, last_of="gla_sum" if h == 3 else None)
            phase_end(pe)

        def act_gla_out(act, layer):
            outs = (0, 1, 2, 3) if layer == 0 else (0, 1)
            for d in range(2):
                for t in outs:
                    for c in range(2):
                        ins = act.activation(gQ[:, d, t, c, :], gB[d][:, c, t * P:(t + 1) * P], ACT.Exp)
            ins.then_inc(sem("query_exp"), 1)
            for d in range(2):
                for i, t in enumerate(ORDER[d][:3]):
                    if d or i:
                        await_next(act, "keys_decayed")
                    edge = t * P + (P - 1 if d == 0 else 0)
                    for c in range(2):
                        ins = act.activation(gX[:, c, :], gB[d][:, c, t * P:(t + 1) * P], ACT.Exp, scale=-1.0,
                                             bias=gB[d][:, c, edge:edge + 1])
                    ins.then_inc(sem("key_exp"), 1)
                    await_next(act, "keys_turned")
                    act.activation(gKt, bank[4][:, 0:256], ACT.Copy).then_inc(sem("keys_copied"), 1)
            advance(act, "keys_decayed", 1)
            phase_end(act)

        def dve_gla_out(dve, layer):
            outs = (0, 1, 2, 3) if layer == 0 else (0, 1)
            link(dve, dve.memset(gS[:, :, :, :].rearrange("p d c n -> p (d c n)"), 0.0))
            await_next(dve, "query_exp")
            for d in range(2):
                for t in outs:
                    ins = dve.tensor_tensor(gQ[:, d, t, :, :], gQ[:, d, t, :, :], GQ[:, :, t * P:(t + 1) * P], ALU.mult)
            ins.then_inc(sem("queries_decayed"), 1)
            for d in range(2):
                for i, t in enumerate(ORDER[d][:3]):
                    await_next(dve, "key_exp")
                    dve.tensor_tensor(gK[:, :, :], gX[:, :, :], GK[:, :, t * P:(t + 1) * P], ALU.mult)\
                       .then_inc(sem("keys_decayed"), 1)
                    await_next(dve, "state_step")
                    if i > 0:
                        await_next(dve, "state_used")
                    for c in range(2):
                        for r in range(2):
                            rr = slice(r * HD, (r + 1) * HD)
                            s = gS[rr, d, c, rr]
                            ins = dve.scalar_tensor_tensor(s, s, gD[rr, d, t, c:c + 1],
                                                           bank[5][rr, c * P + r * HD:c * P + (r + 1) * HD],
                                                           ALU.mult, ALU.add)
                    link(dve, ins)
                    dve.nop().then_inc(sem("state"), 1)
                await_next(dve, "state_used")
            phase_end(dve)

        def gla_o(layer):
            n = 2 * T if layer == 0 else T
            return n, Z[:, 0:2 * n].rearrange("p (c n) -> p c n", c=2)

        def pe_gla_norm(pe, layer):
            for c in range(2):
                await_next(pe, "gla_squared")
                n = 2 * T if layer == 0 else T
                mm(pe, bank[4 + c][:, 0:n], const("head_mean"), gSq[:, c, 0:n], start=True, stop=True,
                   last_of="gla_mean_square")
            phase_end(pe)

        gSq = hflat[:, 0:1024].rearrange("p (c n) -> p c n", c=2)
        gR = hflat[:, 1024:2048].rearrange("p (c n) -> p c n", c=2)
        gSi = hflat[:, 2048:3072].rearrange("p (c n) -> p c n", c=2)

        def act_gla_norm(act, layer):
            n, o = gla_o(layer)
            for t in range(n // P):
                link(act, act.activation(o[:, :, t * P:(t + 1) * P],
                                         bank[t][:, 0:256].rearrange("p (c n) -> p c n", c=2), ACT.Copy))
            for c in range(2):
                act.activation(gSq[:, c, 0:n], o[:, c, :], ACT.Square).then_inc(sem("gla_squared"), 1)
            for c in range(2):
                await_next(act, "gla_mean_square")
                link(act, act.activation(gR[:, c, 0:n], bank[4 + c][:, 0:n], ACT.Ln, bias=EPS))
                act.activation(gR[:, c, 0:n], gR[:, c, 0:n], ACT.Exp, scale=-0.5).then_inc(sem("gla_rms"), 1)
            for c in range(2):
                act.activation(gSi[:, c, 0:n], Zt[:, 15 + c, 0:n], ACT.Silu).then_inc(sem("gla_silu"), 1)
            phase_end(act)

        def dve_gla_norm(dve, layer):
            n, o = gla_o(layer)
            for c in range(2):
                await_next(dve, "gla_rms")
                link(dve, dve.scalar_tensor_tensor(gR[:, c, 0:n], gR[:, c, 0:n], v("gla_g", layer), o[:, c, :],
                                                   ALU.mult, ALU.mult))
            for c in range(2):
                await_next(dve, "gla_silu")
                dve.tensor_tensor(mixT[:, 6 + c, 0:n], gR[:, c, 0:n], gSi[:, c, 0:n], ALU.mult)
            phase_end(dve)

        def out_groups(kts, n, gains, per_piece):
            res = []
            for d in range(KT):
                c = d % per_piece
                w = per_piece * P
                pairs = [((lambda s, k=k, c=c, w=w: s[:, k * w + c * P:k * w + (c + 1) * P]), mixT[:, k, 0:n])
                         for k in range(kts)]
                evs = [("resid", xT[:, d, s * T:(s + 1) * T], gains(d, s), s * T, (s + 1) * T) for s in range(n // T)]
                res.append((pairs, 0, P, n, evs, "new" if c == 0 else "same"))
            return res

        UP = mixT[:, 0:5, :].rearrange("p a b -> p (a b)")[:, 0:4 * 259].rearrange("p (c n) -> p c n", c=4)
        CP = mixflat[:, 1040:1040 + 2 * 286].rearrange("p (c n) -> p c n", c=2)
        SG = sc[:, 44:76].rearrange("p (t c) -> p t c", t=2)
        FC = sc[:, 76:84].rearrange("p (t c) -> p t c", t=2)
        BH = Z[:, 18 * 512:18 * 512 + 1536].rearrange("p (h n) -> p h n", h=4)

        def mv(t, h):
            return tok[:, t * 768 + h * HD:t * 768 + (h + 1) * HD]

        def fv(t, h):
            return tok[:, t * 768 + 256 + h * HD:t * 768 + 256 + (h + 1) * HD]

        def z2(i):
            return Zt[:, i, 0:T]

        def b2_groups(layer):
            g = feature_major([UP[:, 0, 3:259], UP[:, 1, 3:259]], 0, T)
            g += feature_major([UP[:, 2, 3:259], UP[:, 3, 3:259]], 0, T)
            g += token_major([tok[:, t * 768:t * 768 + 256] for t in range(2)])
            g += feature_major([z2(4), z2(5)], 0, T)
            g += feature_major([z2(6), z2(7)], 0, T)
            g += feature_major([z2(8), z2(9)], 0, T)
            for j in range(2):
                g += feature_major([z2(10 + 2 * j), z2(11 + 2 * j)], 0, T, HD ** -0.5)
            for j in range(2):
                g += feature_major([z2(14 + 2 * j), z2(15 + 2 * j)], 0, T)
            for j in range(2):
                g += token_major([tok[:, t * 768 + 256 + 256 * j:t * 768 + 512 + 256 * j] for t in range(2)])
            for t in range(2):
                g.append(([(hT[:, k, t * P:(t + 1) * P], sg_w[:, layer, k, :]) for k in range(KT)],
                          0, P, 16, copy(SG[:, t, :], 16), None))
            return g

        def act_b2_conv(act, layer):
            act_log_sigmoid(act, sc[:, 0:24].rearrange("p (t c) -> p t c", t=2))
            for c in range(2):
                act.activation(z2(8 + c), z2(8 + c), ACT.Sigmoid).then_inc(sem("glu"), 1)
            for c in range(4):
                await_next(act, "m_conv")
                act.activation(z2(c), z2(c), ACT.Silu)
            phase_end(act)

        def pe_b2_conv(pe, layer):
            await_next(pe, "log_f")
            mm(pe, bank[0][:, 0:4], const("tri"), SG[:, 0, 4:8], start=True, stop=True, last_of=None)
            mm(pe, bank[1][:, 0:4], const("ones"), SG[:, 0, 4:8], start=True, stop=False, last_of=None)
            mm(pe, bank[1][:, 0:4], const("tri"), SG[:, 1, 4:8], start=False, stop=True, last_of="f_sums")
            phase_end(pe)

        def dve_b2_conv(dve, layer):
            bias = v("gate_b", layer).unsqueeze(1).to_broadcast([P, 2, 16])
            link(dve, dve.tensor_tensor(SG[:, :, :], SG[:, :, :], bias, ALU.add))
            z, t = SG[:, :, 4:16], sc[:, 0:24].rearrange("p (t c) -> p t c", t=2)
            dve_log_sigmoid_a(dve, z, t)
            link(dve, dve.tensor_scalar(z, z, 0.0, None, ALU.min))
            await_next(dve, "log1p")
            dve.tensor_tensor(z, z, t, ALU.subtract).then_inc(sem("log_f"), 1)
            for c in range(2):
                link(dve, dve.memset(CP[:, c, 0:30], 0.0))
                dve.memset(UP[:, 2 * c, 0:3], 0.0)
                link(dve, dve.memset(UP[:, 2 * c + 1, 0:3], 0.0))
            for c in range(4):
                w = lambda j: v("m_conv_w", layer, 4 * j + c, 4 * j + c + 1)
                link(dve, dve.tensor_scalar(z2(c), UP[:, c, 0:T], w(0), v("m_conv_b", layer, c, c + 1),
                                            ALU.mult, ALU.add))
                for j in (1, 2):
                    link(dve, dve.scalar_tensor_tensor(z2(c), UP[:, c, j:j + T], w(j), z2(c), ALU.mult, ALU.add))
                dve.scalar_tensor_tensor(z2(c), UP[:, c, 3:3 + T], w(3), z2(c), ALU.mult, ALU.add)\
                   .then_inc(sem("m_conv"), 1)
            for c in range(2):
                await_next(dve, "glu")
                link(dve, dve.tensor_tensor(CP[:, c, 30:30 + T], z2(6 + c), z2(8 + c), ALU.mult))
            for j in range(31):
                for c in range(2):
                    w = v("c_conv_w", layer, 2 * j + c, 2 * j + c + 1)
                    if j == 0:
                        ins = dve.tensor_scalar(z2(6 + c), CP[:, c, 0:T], w, v("c_conv_b", layer, c, c + 1),
                                                ALU.mult, ALU.add)
                    else:
                        ins = dve.scalar_tensor_tensor(z2(6 + c), CP[:, c, j:j + T], w, z2(6 + c), ALU.mult, ALU.add)
                link(dve, ins)
            await_next(dve, "f_sums")
            dve.tensor_copy(FC[:, 0, :], bank[0][:, 0:4])
            dve.tensor_copy(FC[:, 1, :], bank[1][:, 0:4])
            phase_end(dve)

        def pe_b2_ln(pe, layer):
            for c in range(2):
                mm(pe, bank[0][:, 0:T], const("mean"), z2(6 + c), start=c == 0, stop=c == 1,
                   last_of="ln_mean" if c == 1 else None)
            for c in range(2):
                await_next(pe, "ln_squared")
                mm(pe, bank[1][:, 0:T], const("mean"), z2(8 + c), start=c == 0, stop=c == 1,
                   last_of="ln_var" if c == 1 else None)
            phase_end(pe)

        def act_b2_ln(act, layer):
            for c in range(2):
                await_next(act, "ln_centred")
                act.activation(z2(8 + c), z2(6 + c), ACT.Square).then_inc(sem("ln_squared"), 1)
            await_next(act, "ln_var")
            link(act, act.activation(hT[:, 4, 0:T], bank[1][:, 0:T], ACT.Ln, bias=EPS, scale=4.0))
            act.activation(hT[:, 4, 0:T], hT[:, 4, 0:T], ACT.Exp, scale=-0.5).then_inc(sem("ln_rms"), 1)
            for c in range(2):
                await_next(act, "ln_scaled")
                act.activation(mixT[:, 2 + c, 0:T], z2(6 + c), ACT.Silu, bias=v("ln_b", layer, c, c + 1))
            phase_end(act)

        def dve_b2_ln(dve, layer):
            await_next(dve, "ln_mean")
            for c in range(2):
                dve.scalar_tensor_tensor(z2(6 + c), bank[0][:, 0:T], -4.0, z2(6 + c), ALU.mult, ALU.add)\
                   .then_inc(sem("ln_centred"), 1)
            await_next(dve, "ln_rms")
            for c in range(2):
                dve.scalar_tensor_tensor(z2(6 + c), z2(6 + c), v("ln_w", layer, c, c + 1), hT[:, 4, 0:T],
                                         ALU.mult, ALU.mult).then_inc(sem("ln_scaled"), 1)
            phase_end(dve)

        def dve_decay_columns(dve, f0, i0):
            for j in range(4):
                f = [SG[:, t, f0 + j:f0 + j + 1] for t in range(2)]
                dve.tensor_scalar(BH[:, j, 0:P], const("strict"), f[0], None, ALU.mult)
                both = cst[:, CONST["ones"][0]:CONST["strict"][1]]
                ins = dve.tensor_scalar(BH[:, j, P:384], both, f[1], None, ALU.mult)
                if i0 is not None:
                    link(dve, ins)
                    i = [SG[:, t, i0 + j:i0 + j + 1] for t in range(2)]
                    dve.scalar_tensor_tensor(BH[:, j, 0:P], const("ident"), i[0], BH[:, j, 0:P], ALU.mult, ALU.add)
                    dve.scalar_tensor_tensor(BH[:, j, 256:384], const("ident"), i[1], BH[:, j, 256:384],
                                             ALU.mult, ALU.add)
            phase_end(dve)

        def decay_pairs(j, q):
            if q == 0:
                return [(const("tri"), BH[:, j, 0:P], P)]
            return [(const("tri"), BH[:, j, P:384], 256), (const("ones"), BH[:, j, 0:P], P)]

        def causal(q):
            return const("masks", 512, 640) if q == 0 else const("masks", 384, 640)

        def fox_units(part):
            units = []
            for j in range(4):
                h = 4 * part + j
                r = slice((h % 2) * HD, (h % 2 + 1) * HD)
                for q in range(TT):
                    nk = (q + 1) * P
                    units.append(dict(apart=None,
                        scores=[(Zt[r, 10 + h // 2, q * P:(q + 1) * P], Zt[r, 14 + h // 2, 0:nk], nk)] + decay_pairs(j, q),
                        nk=nk, mask=causal(q), init=3 * NEG, sink=None,
                        v=[fv(t, h) for t in range(q + 1)], rows=(r.start, r.stop),
                        out=mixT[r, 4 + h // 2, q * P:(q + 1) * P]))
            return units

        def mlstm_units():
            units = []
            for h in range(4):
                r = slice((h % 2) * HD, (h % 2 + 1) * HD)
                for q in range(TT):
                    nk = (q + 1) * P
                    units.append(dict(
                        apart=(Zt[r, h // 2, q * P:(q + 1) * P], Zt[r, 2 + h // 2, 0:nk]),
                        scores=decay_pairs(h, q), nk=nk, mask=causal(q), init=FC[:, q, h:h + 1], sink=None,
                        v=[mv(t, h) for t in range(q + 1)], rows=(r.start, r.stop),
                        out=Zt[r, 6 + h // 2, q * P:(q + 1) * P]))
            return units

        def pe_m_norm(pe, layer):
            for c in range(2):
                await_next(pe, "m_squared")
                mm(pe, bank[c][:, 0:T], const("head_mean"), z2(8 + c), start=True, stop=True, last_of="m_mean_square")
            phase_end(pe)

        def act_m_norm(act, layer):
            for c in range(2):
                act.activation(z2(8 + c), z2(6 + c), ACT.Square).then_inc(sem("m_squared"), 1)
                act.activation(z2(4 + c), z2(4 + c), ACT.Sigmoid).then_inc(sem("m_gate"), 1)
            for c in range(2):
                await_next(act, "m_mean_square")
                link(act, act.activation(hT[:, 4 + c, 0:T], bank[c][:, 0:T], ACT.Ln, bias=EPS))
                act.activation(hT[:, 4 + c, 0:T], hT[:, 4 + c, 0:T], ACT.Exp, scale=-0.5).then_inc(sem("m_rms"), 1)
            phase_end(act)

        def dve_m_norm(dve, layer):
            for c in range(2):
                await_next(dve, "m_gate")
                await_next(dve, "m_rms")
                link(dve, dve.scalar_tensor_tensor(z2(6 + c), z2(6 + c), v("m_norm", layer, c, c + 1), hT[:, 4 + c, 0:T],
                                                   ALU.mult, ALU.mult))
                dve.tensor_tensor(mixT[:, c, 0:T], z2(6 + c), z2(4 + c), ALU.mult)
            phase_end(dve)

        def x_groups(layer):
            g = []
            for j in range(2):
                g += feature_major([z2(2 * j), z2(2 * j + 1)], 0, T, float(P) ** -0.5)
            for j in range(2):
                g += feature_major([z2(4 + 2 * j), z2(5 + 2 * j)], T, 2 * T)
            for j in range(2):
                g += token_major([tok[:, t * 768 + 256 * j:t * 768 + 256 * (j + 1)] for t in range(2)], 2)
            return g

        def x_units():
            return [dict(apart=None, scores=[(Zt[:, h, q * P:(q + 1) * P], z2(4 + h), T)], nk=T,
                         mask=const("masks", 128, 384), init=3 * NEG, sink=None,
                         v=[tok[:, t * 768 + h * P:t * 768 + (h + 1) * P] for t in range(2)], rows=(0, P),
                         out=mixT[:, h, q * P:(q + 1) * P]) for h in range(4) for q in range(TT)]

        LG = sc[:, 0:16].rearrange("p (t e) -> p t e", t=2)
        RK = sc[:, 16:32].rearrange("p (t e) -> p t e", t=2)
        EX = sc[:, 32:48].rearrange("p (t e) -> p t e", t=2)
        TOP = sc[:, 48:50].rearrange("p (t e) -> p t e", t=2)
        CMP = mixT[:, 0, 0:128].rearrange("p (t i j) -> p t i j", t=2, i=N_EXP)
        EQ = mixT[:, 1, 0:16].rearrange("p (t e) -> p t e", t=2)
        gates_all = mixT[:, 4:8, :].rearrange("p a b -> p (a b)")

        def router_groups():
            return [([(hT[:, k, t * P:(t + 1) * P], rt_w[:, k, :]) for k in range(KT)], 0, P, N_EXP,
                     copy(LG[:, t, :], N_EXP), None) for t in range(2)]

        def dve_router(dve):
            for t in range(2):
                ins = dve.tensor_tensor(CMP[:, t], LG[:, t].unsqueeze(1).to_broadcast([P, N_EXP, N_EXP]),
                                        LG[:, t].unsqueeze(2).to_broadcast([P, N_EXP, N_EXP]), ALU.is_gt)
            dve.tensor_reduce(TOP[:, :, 0], LG[:, :, :], AX.X, ALU.max)
            link(dve, dve.tensor_copy(EX[:, :, :], LG[:, :, :]))
            link(dve, dve.tensor_reduce(RK[:, :, :], CMP[:, :, :, :], AX.X, ALU.add))
            for j in range(N_EXP - 1):
                m = N_EXP - 1 - j
                link(dve, dve.tensor_tensor(EQ[:, :, 0:m], LG[:, :, j + 1:N_EXP],
                                            LG[:, :, j:j + 1].to_broadcast([P, 2, m]), ALU.is_equal))
                link(dve, dve.tensor_tensor(RK[:, :, j + 1:N_EXP], RK[:, :, j + 1:N_EXP], EQ[:, :, 0:m], ALU.add))
            link(dve, dve.tensor_scalar(RK[:, :, :], RK[:, :, :], 1.5, None, ALU.is_lt))
            dve.tensor_tensor(EX[:, :, :], EX[:, :, :], TOP[:, :, :].to_broadcast([P, 2, N_EXP]), ALU.subtract)\
               .then_inc(sem("logits_below_max"), 1)
            await_next(dve, "logits_exp")
            link(dve, dve.tensor_tensor(EX[:, :, :], EX[:, :, :], RK[:, :, :], ALU.mult))
            link(dve, dve.tensor_reduce(TOP[:, :, 0], EX[:, :, :], AX.X, ALU.add))
            link(dve, dve.reciprocal(TOP[:, :, :], TOP[:, :, :]))
            dve.tensor_tensor(LG[:, :, :], EX[:, :, :], TOP[:, :, :].to_broadcast([P, 2, N_EXP]), ALU.mult)\
               .then_inc(sem("gates_ready"), 1)
            for b in range(4):
                await_next(dve, "gates_spread")
                dve.tensor_copy(mixT[:, 4 + b, :], bank[b][:, :])
            phase_end(dve)

        def act_router(act):
            await_next(act, "logits_below_max")
            act.activation(EX[:, :, :], EX[:, :, :], ACT.Exp).then_inc(sem("logits_exp"), 1)
            phase_end(act)

        def pe_router(pe):
            await_next(pe, "gates_ready")
            for b in range(4):
                for e in (2 * b, 2 * b + 1):
                    for t in range(2):
                        last = e == 2 * b + 1 and t == 1
                        mm(pe, bank[b][:, (e % 2) * T + t * P:(e % 2) * T + (t + 1) * P],
                           LG[:, t, e:e + 1].to_broadcast([P, P]), const("ident"), start=True, stop=True,
                           last_of="gates_spread" if last else None)
            phase_end(pe)

        X_ONLY = T
        b2_seg = lambda name, layer: [(0, T, (lambda k: v(name, layer, k, k + 1)), None)]
        mem_seg = lambda layer: b2_seg("norm_x", layer) + [(T, 2 * T, (lambda k: v("norm_mem", layer, k, k + 1)), None)]
        one = lambda q, s: 1.0

        def gate_gain(which):
            return lambda d, s: modT[:, 16 + 24 * which + d, s:s + 1]

        block = ctx.enter_context(nc.Block())

        @block.sync
        def _(sp):
            for name, dst in (("xT", xT[:, :, 0:T]), ("ctxT", xT[:, :, T:2 * T]), ("vectors", vec[:, :]),
                              ("constants", cst[:, :]), ("level_masks", Z[:, 0:2 * LEVELS * P]),
                              ("gate_w", gate_w[:, :, :, :]), ("lr_w", lr_w[:, :, :, :]),
                              ("sg_w", sg_w[:, :, :, :]), ("rt_w", rt_w[:, :, :])):
                sp.dma_start(dst, A[name]).then_inc(sem("vectors_in"), 16)

            def load(n, s):
                src = A["stream"][n] if isinstance(n, int) else A["stream"][bass.ds(n, 1)].rearrange("o p c -> (o p) c")
                sp.dma_start(ring[:, s, :], src).then_inc(sem(f"piece_in_{s}"), 16)

            for s in range(SLOTS):
                load(s, s)
            rounds = n_pieces // SLOTS
            with sp.Fori(1, rounds, 1) as r:
                for s in range(SLOTS):
                    sp.wait_ge(sem("piece_used"), (r - 1) * SLOTS + s + 1)
                    load(r * SLOTS + s, s)
            for s in range(n_pieces % SLOTS):
                sp.wait_ge(sem("piece_used"), (rounds - 1) * SLOTS + s + 1)
                load(rounds * SLOTS + s, s)
            sp.wait_ge(sem("y_ready"), 1)
            sp.dma_start(y_out, hT[:, :, 0:T]).then_inc(sem("y_stored"), 16)
            sp.wait_ge(sem("y_stored"), 16)

        @block.tensor
        def _(pe):
            for layer in range(DEPTH):
                n = 2 * T if layer == 0 else T
                pe_mod(pe, layer)
                pe_norm(pe, 0, 2 * T)
                pe_products(pe, b1_groups(layer))
                phase_end(pe)
                pe_rope(pe, layer)
                pe_attention(pe, b1_units(layer))
                phase_end(pe)
                pe_gla_gates(pe, layer)
                pe_gla_levels(pe, layer)
                pe_gla_out(pe, layer)
                pe_gla_norm(pe, layer)
                pe_products(pe, out_groups(KT, n, gate_gain(0), 2), "dve")
                phase_end(pe)
                pe_norm(pe, 0, n)
                pe_ffn(pe, n, layer)
                phase_end(pe)
            pe_norm(pe, 0, T)
            phase_end(pe)
            for layer in range(DEPTH):
                pe_norm(pe, 0, T)
                pe_products(pe, b2_groups(layer))
                phase_end(pe)
                pe_b2_conv(pe, layer)
                pe_b2_ln(pe, layer)
                phase_end(pe)
                pe_attention(pe, mlstm_units())
                phase_end(pe)
                pe_m_norm(pe, layer)
                for part in range(2):
                    phase_end(pe)
                    pe_attention(pe, fox_units(part))
                    phase_end(pe)
                pe_products(pe, out_groups(KT, T, one, 2), "dve")
                phase_end(pe)
                pe_norm(pe, 0, 2 * T)
                pe_products(pe, x_groups(layer))
                phase_end(pe)
                pe_attention(pe, x_units())
                phase_end(pe)
                pe_products(pe, out_groups(4, T, one, 4), "dve")
                phase_end(pe)
                pe_norm(pe, 0, T)
                if layer == 0:
                    pe_ffn(pe, T, 2)
                    phase_end(pe)
                else:
                    pe_products(pe, router_groups())
                    phase_end(pe)
                    pe_router(pe)
                    if stream["release"]:
                        pe.drain().then_inc(sem("piece_used"), 1)
                        stream["release"] = False
                    with pe.Fori(0, N_EXP, 1) as e:
                        pe_ffn(pe, T, e + 3, it=e)
                        pe.drain().then_inc(sem("piece_used"), 1)
                        stream["release"] = False
                    phase_end(pe)
            pe_norm(pe, 0, T)

        @block.scalar
        def _(act):
            for layer in range(DEPTH):
                n = 2 * T if layer == 0 else T
                act_mod(act, layer)
                act_norm(act, 0, 2 * T, b1_segments(0, 2 * T))
                take_products(act, "act", b1_groups(layer))
                phase_end(act)
                act_rope(act, layer)
                act_attention(act, b1_units(layer))
                phase_end(act)
                act_gla_gates(act, layer)
                act_gla_levels(act, layer)
                act_gla_out(act, layer)
                act_gla_norm(act, layer)
                phase_end(act)
                act_norm(act, 0, n, b1_segments(1, n))
                act_ffn(act, n, layer)
                phase_end(act)
            act_norm(act, 0, T, [(0, T, None, None)])
            phase_end(act)
            for layer in range(DEPTH):
                act_norm(act, 0, T, b2_seg("norm_mix", layer))
                take_products(act, "act", b2_groups(layer))
                phase_end(act)
                act_b2_conv(act, layer)
                act_b2_ln(act, layer)
                phase_end(act)
                act_attention(act, mlstm_units())
                phase_end(act)
                act_m_norm(act, layer)
                for part in range(2):
                    phase_end(act)
                    act_attention(act, fox_units(part))
                    phase_end(act)
                phase_end(act)
                act_norm(act, 0, 2 * T, mem_seg(layer))
                take_products(act, "act", x_groups(layer))
                phase_end(act)
                act_attention(act, x_units())
                phase_end(act)
                phase_end(act)
                act_norm(act, 0, T, b2_seg("norm_ffn", layer))
                if layer == 0:
                    act_ffn(act, T, 2)
                    phase_end(act)
                else:
                    take_products(act, "act", router_groups())
                    phase_end(act)
                    act_router(act)
                    with act.Fori(0, N_EXP, 1) as e:
                        act_ffn(act, T, e + 3)
                    phase_end(act)
            act_norm(act, 0, T, [(0, T, None, None)])

        @block.vector
        def _(dve):
            for layer in range(DEPTH):
                n = 2 * T if layer == 0 else T
                dve_mod(dve, layer)
                dve_norm(dve, 0, 2 * T, b1_segments(0, 2 * T))
                take_products(dve, "dve", b1_groups(layer))
                phase_end(dve)
                dve_rope_conv(dve, layer)
                dve_attention(dve, b1_units(layer))
                phase_end(dve)
                dve_gla_gates(dve, layer)
                dve_gla_levels(dve, layer)
                dve_gla_out(dve, layer)
                dve_gla_norm(dve, layer)
                take_products(dve, "dve", out_groups(KT, n, gate_gain(0), 2), "dve")
                phase_end(dve)
                dve_norm(dve, 0, n, b1_segments(1, n))
                dve_ffn(dve, n, layer, gate_gain(1))
                phase_end(dve)
            dve_norm(dve, 0, T, [(0, T, (lambda k: v("final1", 0, k, k + 1)), None)])
            dve.wait_ge(sem("mem_in"), 16)
            for k in range(KT):
                dve.tensor_copy(xT[:, k, 0:T], hT[:, k, 0:T])
            phase_end(dve)
            for layer in range(DEPTH):
                dve_norm(dve, 0, T, b2_seg("norm_mix", layer))
                take_products(dve, "dve", b2_groups(layer))
                phase_end(dve)
                dve_b2_conv(dve, layer)
                dve_b2_ln(dve, layer)
                dve_decay_columns(dve, 4, 0)
                dve_attention(dve, mlstm_units())
                phase_end(dve)
                dve_m_norm(dve, layer)
                for part in range(2):
                    dve_decay_columns(dve, 8 + 4 * part, None)
                    dve_attention(dve, fox_units(part))
                    phase_end(dve)
                take_products(dve, "dve", out_groups(KT, T, one, 2), "dve")
                phase_end(dve)
                dve_norm(dve, 0, 2 * T, mem_seg(layer))
                take_products(dve, "dve", x_groups(layer))
                phase_end(dve)
                dve_attention(dve, x_units())
                phase_end(dve)
                take_products(dve, "dve", out_groups(4, T, one, 4), "dve")
                phase_end(dve)
                dve_norm(dve, 0, T, b2_seg("norm_ffn", layer))
                if layer == 0:
                    dve_ffn(dve, T, 2, one)
                    phase_end(dve)
                else:
                    take_products(dve, "dve", router_groups())
                    phase_end(dve)
                    dve_router(dve)
                    with dve.Fori(0, N_EXP, 1) as e:
                        dve_ffn(dve, T, e + 3, expert=gates_all[:, bass.ds(e * T, T)])
                    phase_end(dve)
            dve_norm(dve, 0, T, [(0, T, (lambda k: v("final2", 0, k, k + 1)), None)])
            dve.nop().then_inc(sem("y_ready"), 1)

        @block.gpsimd
        def _(pool):
            for other in ("pe", "act", "dve"):
                pool.wait_ge(sem(f"phase_{other}"), B1_PHASES)
            pool.dma_start(xT[:, :, T:2 * T], A["memT"]).then_inc(sem("mem_in"), 16)


N_LOADS = 9
B1_PHASES = 24


def constants():
    r = np.arange(P)
    c = {}
    c["ident"] = np.eye(P)
    c["mean"] = np.full((P, P), 1.0 / D)
    c["head_mean"] = (r[:, None] // HD == r[None, :] // HD) / HD
    c["tri"] = r[:, None] <= r[None, :]
    c["tri_r"] = r[:, None] >= r[None, :]
    c["ones"] = np.ones((P, P))
    c["strict"] = r[:, None] > r[None, :]
    rot = np.zeros((P, P))
    for m in range(P):
        if m % 32 < 16:
            rot[m + 16, m] = -1.0
        else:
            rot[m - 16, m] = 1.0
    c["rot"] = rot
    zero = np.zeros((P, P))
    after = np.where(r[None, :] >= r[:, None], 0.0, NEG)
    upto = np.where(r[None, :] <= r[:, None], 0.0, NEG)
    c["masks"] = np.concatenate([after, zero, zero, zero, upto, zero, zero], 1)
    inv = np.float32(10000.0) ** (-np.arange(16, dtype=np.float32) / np.float32(16))
    t = np.arange(T)
    pos = np.stack([t // 64, t % 64]).astype(np.float32)
    ch = r % HD
    ang = pos[ch // 32] * inv[ch % 16][:, None]
    c["cos"], c["sin"] = np.cos(ang), np.sin(ang)
    out = np.zeros((P, N_CONST), np.float32)
    for name, (a, b) in CONST.items():
        out[:, a:b] = c[name]
    lv = np.zeros((P, 2 * LEVELS, P), np.float32)
    s, q = r[:, None], r[None, :]
    for l in range(LEVELS):
        same = (s >> (l + 1)) == (q >> (l + 1))
        up_s, up_q = (s >> l) & 1, (q >> l) & 1
        lv[:, 2 * l] = same & (up_s == 0) & (up_q == 1)
        lv[:, 2 * l + 1] = same & (up_s == 1) & (up_q == 0)
    return out, lv.reshape(P, -1)


def by_columns(w, width=256):
    k, n = w.shape
    return w.reshape(k // P, P, n // width, width).transpose(2, 1, 0, 3).reshape(-1, P, PIECE)


def ffn_pieces(gate, up, down):
    g = gate.reshape(KT, P, FT, P).transpose(2, 1, 0, 3)
    u = up.reshape(KT, P, FT, P).transpose(2, 1, 0, 3)
    d = down.reshape(FT, P, 2, 512).transpose(2, 0, 1, 3).reshape(2 * FT // 4, 4, P, 512).transpose(0, 2, 1, 3)
    return [np.concatenate([g, u], 3).reshape(FT, P, PIECE), d.reshape(-1, P, PIECE)]


def columns(x, tile=P):
    x = np.asarray(x)
    return x.reshape(-1, P).T


def rows(x):
    x = np.asarray(x).reshape(1, -1)
    return np.broadcast_to(x, (P, x.shape[1]))


def kernel(**inputs):
    import concourse.bacc as bacc
    from concourse.bass_utils import run_bass_kernel_spmd

    i = {k: np.asarray(a) for k, a in inputs.items()}
    pieces = []
    heads = np.array([64 * h + k for t in range(4) for h in (t, t + 4) for k in range(64)])
    for l in range(DEPTH):
        w = i["w_in"][l]
        w = np.concatenate([w[:, 0:768], w[:, 768:1280][:, heads], w[:, 1280:2560]], 1)
        pieces += [by_columns(i["w_mod"][l]), by_columns(w), by_columns(i["w_out"][l])]
        pieces += ffn_pieces(i["w_up"][l][:, 0:FF], i["w_up"][l][:, FF:2 * FF], i["w_down"][l])
    for l in range(DEPTH):
        w = i["w_in_2"][l]
        w = np.concatenate([w[:, 0:1024], w[:, 1032:3080]], 1)
        pieces += [by_columns(w), by_columns(i["w_out_2"][l]), by_columns(i["xattn_w_q_2"][l]),
                   by_columns(i["xattn_w_kv_2"][l]), by_columns(i["xattn_w_o_2"][l], 512)]
        if l == 0:
            pieces += ffn_pieces(i["ffn_w_gate_2"][0], i["ffn_w_up_2"][0], i["ffn_w_down_2"][0])
        else:
            for e in range(N_EXP):
                pieces += ffn_pieces(i["moe_w_gate_2"][0, e], i["moe_w_up_2"][0, e], i["moe_w_down_2"][0, e])

    vec = np.zeros((P, N_VEC), np.float32)

    def put(name, layer, cols):
        a, b = VEC[name, layer]
        vec[:, a:b] = cols

    for l in range(DEPTH):
        put("b_mod", l, columns(i["b_mod"][l]))
        put("norm1", l, columns(i["norm1_g"][l]))
        put("norm2", l, columns(i["norm2_g"][l]))
        put("conv_w", l, columns(i["conv_w"][l]))
        put("sink", l, rows(i["attn_sink"][l]))
        put("gla_g", l, columns(np.concatenate([i["gla_norm_g"][l], i["gla_norm_g"][l]])))
        put("norm_mix", l, columns(i["norm_mix_w_2"][l]))
        put("m_conv_w", l, columns(i["mlstm_conv_w_2"][l]))
        put("m_conv_b", l, columns(i["mlstm_conv_b_2"][l]))
        put("gate_b", l, rows(np.concatenate([i["mlstm_b_i_2"][l], i["mlstm_b_f_2"][l], i["fox_b_f_2"][l]])))
        put("m_norm", l, columns(i["mlstm_norm_w_2"][l]))
        put("c_conv_w", l, columns(i["conf_conv_w_2"][l]))
        put("c_conv_b", l, columns(i["conf_conv_b_2"][l]))
        put("ln_w", l, columns(i["conf_ln_w_2"][l]))
        put("ln_b", l, columns(i["conf_ln_b_2"][l]))
        put("norm_x", l, columns(i["norm_xattn_w_2"][l]))
        put("norm_mem", l, columns(i["norm_mem_w_2"][l]))
        put("norm_ffn", l, columns(i["norm_ffn_w_2"][l]))
    put("final1", 0, columns(i["final_norm_g"]))
    put("final2", 0, columns(i["norm_final_w_2"]))
    put("c", 0, np.stack([columns(i["c"][0]), columns(i["c_ctx"])], 2).reshape(P, 16))

    gate_w = np.zeros((17, DEPTH, 2, 256), np.float32)
    gate_w[0:16] = i["gla_gate_w"].transpose(2, 0, 1, 3)
    gate_w[16] = i["gla_gate_b"]
    consts, level_masks = constants()

    def by_rows(w):
        return np.ascontiguousarray(w.reshape(w.shape[0], KT, P, -1).transpose(2, 0, 1, 3))

    def turned(x):
        return np.ascontiguousarray(x.T.reshape(KT, P, T).transpose(1, 0, 2))

    w2 = i["w_in_2"]
    arrays = dict(
        stream=np.concatenate(pieces, 0), xT=turned(i["x"][0]), ctxT=turned(i["ctx"][0]), memT=turned(i["mem_2"][0]),
        vectors=vec, constants=consts, level_masks=level_masks, gate_w=gate_w,
        lr_w=by_rows(i["w_in"][:, :, 2560:2592]),
        sg_w=by_rows(np.concatenate([w2[:, :, 1024:1032], w2[:, :, 3080:3088]], 2)),
        rt_w=by_rows(i["router_w_2"])[:, 0])
    nc = bacc.Bacc("TRN2", target_bir_lowering=False, num_devices=1)
    A = {}
    for name, a in arrays.items():
        A[name] = nc.dram_tensor(f"in_{name}", a.shape, mybir.dt.from_np(a.dtype), kind="ExternalInput").ap()
    y = nc.dram_tensor("out_y", (P, KT, T), F32, kind="ExternalOutput").ap()
    build(nc, A, y)
    r = run_bass_kernel_spmd(nc, [{f"in_{k}": a for k, a in arrays.items()}], core_ids=[0])
    got = r.results[0]["out_y"]
    return np.ascontiguousarray(got.transpose(1, 0, 2).reshape(D, T).T).reshape(1, T, D)
```

```python
from contextlib import ExitStack

import numpy as np

import concourse.bass as bass
from concourse import mybir

F32 = mybir.dt.float32
F32R = mybir.dt.float32r
U8 = mybir.dt.uint8
ALU = mybir.AluOpType
ACT = mybir.ActivationFunctionType
AX = mybir.AxisListType

P = 128
D = 1024
KT = D // P
T = 256
TT = T // P
EPS = 1e-6
DEPTH = 2
FF = 2816
FT = FF // P
HD = 64
N_EXP = 8
PIECE = 2048
SLOTS = 6
SPLITS = 3
AHEAD = 2
FFN_PIECES = FT + 2 * FT // 4
MOD_PIECES = 6 * D // 256
NEG = -1.0e30

B1_COLS = dict(b_mod=48, norm1=8, norm2=8, conv_w=6, sink=8, gla_g=1)
B2_COLS = dict(norm_mix=8, m_conv_w=16, m_conv_b=4, gate_b=16, m_norm=2, c_conv_w=62, c_conv_b=2,
               ln_w=2, ln_b=2, norm_x=8, norm_mem=8, norm_ffn=8)


def vector_columns():
    at, n = {}, 0
    for layer in range(DEPTH):
        for name, width in B1_COLS.items():
            at[name, layer] = (n, n + width)
            n += width
    for layer in range(DEPTH):
        for name, width in B2_COLS.items():
            at[name, layer] = (n, n + width)
            n += width
    for name, width in dict(final1=8, final2=8, c=16).items():
        at[name, 0] = (n, n + width)
        n += width
    return at, n


VEC, N_VEC = vector_columns()

CONST = {}
N_CONST = 0
for _name, _w in (("ident", P), ("mean", P), ("head_mean", P), ("tri", P), ("tri_r", P), ("ones", P),
                  ("strict", P), ("rot", P), ("pair", 2), ("iota", P), ("masks", 7 * P), ("cos", T), ("sin", T)):
    CONST[_name] = (N_CONST, N_CONST + _w)
    N_CONST += _w
LEVELS = 7


def build(nc, A, y_out):
    with ExitStack() as ctx:
        place = {"at": -(-nc.sbuf_base // 32) * 32}

        def sb(name, shape, dt=F32, over=None):
            n = int(np.prod(shape[1:])) * (1 if dt == U8 else 4)
            at = place[over] if over else place["at"]
            if not over:
                place[name] = at
                place["at"] += -(-n // 32) * 32
            return nc.alloc_sbuf_tensor_at(name, shape, dt, offset=at)

        xT = sb("xT", [P, KT, 2 * T])
        hT = sb("hT", [P, KT, 2 * T])
        h_lo = sb("h_lo", [P, KT, 2 * T], F32R, over="hT")
        mixT = sb("mixT", [P, KT, 2 * T])
        mix_lo = sb("mix_lo", [P, KT, 2 * T], F32R, over="mixT")
        a_hi = sb("a_hi", [P, KT, 2 * T], F32R)
        Z = sb("Z", [P, FT * 2 * T])
        Zr = sb("Zr", [P, FT * 2 * T], F32R, over="Z")
        tok = sb("tok", [P, 4 * 384])
        ring = sb("ring", [P, SLOTS, PIECE])
        ring_lo = sb("ring_lo", [P, SLOTS, PIECE], F32R, over="ring")
        ring_hi = sb("ring_hi", [P, SPLITS, PIECE], F32R)
        cst = sb("cst", [P, N_CONST])
        vec = sb("vec", [P, N_VEC])
        lvl_mask = sb("lvl_mask", [P, 2 * LEVELS, P], U8)
        gate_w = sb("gate_w", [17, DEPTH, 2, 256])
        modT = sb("modT", [P, 48, 2])
        a1 = sb("a1", [P, 2, KT, 2])
        sc = sb("sc", [P, 96])
        overflow = sb("overflow", [P, 1], mybir.dt.int32)
        assert place["at"] <= nc.sbuf_usable_end
        psum = ctx.enter_context(nc.psum_tensor("psum", [P, 8, 512], F32))
        bank = [psum[:, i, :] for i in range(8)]
        Zt = Z[:, :].rearrange("p (f n) -> p f n", n=2 * T)
        hflat = hT[:, :, :].rearrange("p a b -> p (a b)")
        mixflat = mixT[:, :, :].rearrange("p a b -> p (a b)")

        def const(name, lo=0, hi=None):
            a, b = CONST[name]
            return cst[:, a + lo:(b if hi is None else a + hi)]

        def v(name, layer=0, lo=0, hi=None):
            a, b = VEC[name, layer]
            return vec[:, a + lo:(b if hi is None else a + hi)]

        sems, seen = {}, {}

        def sem(name):
            if name not in sems:
                sems[name] = ctx.enter_context(nc.semaphore(name))
            return sems[name]

        def await_next(e, name, n=1):
            k = seen[e.engine, name] = seen.get((e.engine, name), 0) + n
            e.wait_ge(sem(name), k)

        def base(e, name):
            return seen.get((e.engine, name), 0)

        def advance(e, name, n):
            seen[e.engine, name] = base(e, name) + n

        def link(e, ins):
            name = f"own_{str(e.engine).split('.')[-1]}"
            ins.then_inc(sem(name), 1)
            await_next(e, name)

        def phase_end(e):
            me = {nc.tensor.engine: "pe", nc.scalar.engine: "act", nc.vector.engine: "dve"}[e.engine]
            e.drain().then_inc(sem(f"phase_{me}"), 1)
            for other in ("pe", "act", "dve"):
                if other != me:
                    await_next(e, f"phase_{other}")

        n_pieces = A["stream"].shape[0]
        stream = {"n": 0, "release": False}
        splits = {}
        LOOP = 2 * FFN_PIECES

        def piece_slot(pe, it=0):
            n = stream["n"]
            stream["n"] += 1
            pe.wait_ge(sem("piece_split"), n + 1 + it * LOOP)
            return ring_hi[:, n % SPLITS, :], ring_lo[:, n % SLOTS, :]

        def split_ahead(e, who, more=1, it=0):
            more += 0 if who in splits else AHEAD
            for n in range(splits.get(who, 0), splits.get(who, 0) + more):
                raw, hi, lo = ring[:, n % SLOTS, :], ring_hi[:, n % SPLITS, :], ring_lo[:, n % SLOTS, :]
                if who == "act":
                    e.wait_ge(sem(f"piece_in_{n % SLOTS}"), 16 * (n // SLOTS + 1) + it * (16 * LOOP // SLOTS))
                    if n >= SPLITS:
                        e.wait_ge(sem("piece_used"), n - SPLITS + 1 + it * LOOP)
                    e.activation(hi, raw, ACT.Copy).then_inc(sem("piece_rounded"), 1)
                else:
                    e.wait_ge(sem("piece_rounded"), n + 1 + it * LOOP)
                    e.tensor_tensor(lo, raw, hi.bitcast(F32), ALU.subtract).then_inc(sem("piece_split"), 1)
            splits[who] = splits.get(who, 0) + more

        def mm(pe, *args, last_of=None, **kw):
            ins = pe.matmul(*args, **kw)
            if last_of:
                ins.then_inc(sem(last_of), 1)
            elif stream["release"]:
                ins.then_inc(sem("piece_used"), 1)
                stream["release"] = False
            return ins

        def whose(g, who):
            return who or ("act" if g % 2 == 0 else "dve")

        def pe_products(pe, groups, ready, who=None):
            counts = {"act": base(pe, "product_out_act"), "dve": base(pe, "product_out_dve")}
            ends = []
            for g, (terms, rows_, n, _, held) in enumerate(groups):
                if g >= 4:
                    w, k = ends[g - 4]
                    pe.wait_ge(sem(f"product_out_{w}"), k)
                if held == "new":
                    hi, lo = piece_slot(pe)
                for k, (stationary, moving) in enumerate(terms):
                    if g == 0:
                        await_next(pe, ready)
                    for i, (w, a) in enumerate(((hi, 0), (hi, 1), (lo, 0))):
                        last = k == len(terms) - 1 and i == 2
                        mm(pe, bank[g % 4][:, 0:n], stationary(w, a), moving(w, a), start=k == 0 and i == 0, stop=last,
                           last_of=f"product_in_{whose(g, who)}" if last else None)
                if g + 1 == len(groups) or groups[g + 1][4] == "new":
                    stream["release"] = True
                w = whose(g, who)
                counts[w] += 1
                ends.append((w, counts[w]))
            for w, k in counts.items():
                seen[pe.engine, f"product_out_{w}"] = k

        def take_products(e, me, groups, who=None):
            for g, (_, rows_, n, evs, held) in enumerate(groups):
                if held == "new":
                    split_ahead(e, me)
                if whose(g, who) != me:
                    continue
                await_next(e, f"product_in_{me}")
                for ev in evs:
                    if ev[0] == "copy":
                        _, out, scale, a, b = ev
                        src = bank[g % 4][0:rows_, a:b]
                        if me == "act":
                            ins = e.activation(out, src, ACT.Copy, scale=scale)
                        elif scale == 1.0:
                            ins = e.tensor_copy(out, src)
                        else:
                            ins = e.tensor_scalar(out, src, scale, None, ALU.mult)
                    else:
                        _, x, gain, a, b = ev
                        ins = e.scalar_tensor_tensor(x, bank[g % 4][0:rows_, a:b], gain, x, ALU.mult, ALU.add)
                ins.then_inc(sem(f"product_out_{me}"), 1)

        def h(part, k, a, b):
            return (h_lo if part else a_hi)[:, k, a:b]

        def mix(part, k, a, b):
            return (mix_lo if part else a_hi)[:, k, a:b]

        def copy(out, n, scale=1.0):
            return [("copy", out, scale, 0, n)]

        def feature_major(outs, a, b, scale=1.0, rows_=P):
            res = []
            for c, out in enumerate(outs):
                terms = [((lambda w, _, k=k, c=c: w[:, k * 256 + c * P:k * 256 + (c + 1) * P]),
                          (lambda _, p, k=k: h(p, k, a, b))) for k in range(KT)]
                res.append((terms, rows_, b - a, copy(out, b - a, scale), "new" if c == 0 else "same"))
            return res

        def token_major(outs, first=0, lo=0, n=256, held="new"):
            res = []
            for i, out in enumerate(outs):
                t0 = (first + i) * P
                wide = 256 if lo == 0 else n
                terms = [((lambda _, p, k=k, t0=t0: h(p, k, t0, t0 + P)),
                          (lambda w, _, k=k: w[:, k * 256 + lo:k * 256 + lo + wide])) for k in range(KT)]
                res.append((terms, P, wide, copy(out, n), held if i == 0 else "same"))
            return res

        def pe_norm(pe, n0, n1):
            for k in range(KT):
                await_next(pe, "squared")
                mm(pe, bank[0][:, n0:n1], const("mean"), hT[:, k, n0:n1], start=k == 0, stop=k == KT - 1,
                   last_of="mean_square" if k == KT - 1 else None)

        def act_norm(act, n0, n1, segments, split=True):
            for k in range(KT):
                act.activation(hT[:, k, n0:n1], xT[:, k, n0:n1], ACT.Square).then_inc(sem("squared"), 1)
            await_next(act, "mean_square")
            rs = mixT[:, 0, n0:n1]
            link(act, act.activation(rs, bank[0][:, n0:n1], ACT.Ln, bias=EPS))
            act.activation(rs, rs, ACT.Exp, scale=-0.5).then_inc(sem("inverse_rms"), 1)
            for k in range(KT if split else 0):
                await_next(act, "normed")
                for a, b, gain, shift in segments:
                    if shift is not None:
                        ins = act.activation(hT[:, k, a:b], hT[:, k, a:b], ACT.Identity, bias=shift(k))
                if segments[0][3] is not None:
                    link(act, ins)
                act.activation(a_hi[:, k, n0:n1], hT[:, k, n0:n1], ACT.Copy).then_inc(sem("h_rounded"), 1)

        def dve_norm(dve, n0, n1, segments, split=True):
            def rest(k):
                await_next(dve, "h_rounded")
                dve.tensor_tensor(h_lo[:, k, n0:n1], hT[:, k, n0:n1], a_hi[:, k, n0:n1].bitcast(F32),
                                  ALU.subtract).then_inc(sem("h_split"), 1)

            await_next(dve, "inverse_rms")
            for k in range(KT):
                for a, b, gain, shift in segments:
                    ins = dve.scalar_tensor_tensor(hT[:, k, a:b], xT[:, k, a:b], gain(k), mixT[:, 0, a:b],
                                                   ALU.mult, ALU.mult)
                if split:
                    ins.then_inc(sem("normed"), 1)
                    if k >= 2:
                        rest(k - 2)
            if split:
                rest(KT - 2)
                rest(KT - 1)

        def act_split_mix(act, kts, n):
            for k in range(kts):
                act.activation(a_hi[:, k, 0:n], mixT[:, k, 0:n], ACT.Copy).then_inc(sem("mix_rounded"), 1)

        def dve_split_mix(dve, kts, n):
            for k in range(kts):
                await_next(dve, "mix_rounded")
                dve.tensor_tensor(mix_lo[:, k, 0:n], mixT[:, k, 0:n], a_hi[:, k, 0:n].bitcast(F32),
                                  ALU.subtract).then_inc(sem("mix_split"), 1)

        THREE = ((0, 0), (0, 1), (1, 0))

        def hid(f, part, of=None):
            at = f * 2 * T + part * T
            return (Zr if of is None else of)[:, at:at + T]

        def pe_ffn(pe, run, off=0, first=False):
            for f in range(FT):
                w = piece_slot(pe, )
                if f >= 2:
                    pe.wait_ge(sem("hidden_full"), run * FT + f - 1)
                for half in range(2):
                    for k in range(KT):
                        if first and f == 0 and half == 0:
                            await_next(pe, "h_split")
                        for i, (wp, ap) in enumerate(THREE):
                            last = k == KT - 1 and i == 2
                            mm(pe, bank[2 * (f % 2) + half][:, 0:T],
                               w[wp][:, k * 256 + half * P:k * 256 + (half + 1) * P],
                               h(ap, k, off, off + T), start=k == 0 and i == 0, stop=last,
                               last_of="up" if last and half else None)
                stream["release"] = True
            for q in range(2 * FT):
                half, f = divmod(q, FT)
                if q % 4 == 0:
                    w = piece_slot(pe, )
                if half == 0:
                    pe.wait_ge(sem("hidden"), run * FT + f + 1)
                for d in range(4):
                    if f == 0 and half == 1:
                        pe.wait_ge(sem("down_added"), run * 8 + d + 1)
                    for i, (wp, ap) in enumerate(THREE):
                        last = f == FT - 1 and i == 2
                        mm(pe, bank[4 + d][:, 0:T], w[wp][:, (q % 4) * 512 + d * P:(q % 4) * 512 + (d + 1) * P],
                           hid(f, ap), start=f == 0 and i == 0, stop=last, last_of="down" if last else None)
                if q % 4 == 3:
                    stream["release"] = True

        def act_ffn(act, run):
            for f in range(FT + 1):
                if f < FT:
                    split_ahead(act, "act")
                    act.wait_ge(sem("up"), run * FT + f + 1)
                    if f >= 2:
                        act.wait_ge(sem("hidden_full"), run * FT + f - 1)
                    act.activation(mixT[:, f % 2, 0:T], bank[2 * (f % 2)][:, 0:T], ACT.Silu)\
                       .then_inc(sem("silu"), 1)
                if f >= 1:
                    act.wait_ge(sem("hidden_full"), run * FT + f)
                    act.activation(hid(f - 1, 0), hid(f - 1, 1, Z), ACT.Copy).then_inc(sem("hidden_rounded"), 1)
            for j in range(FT // 2):
                split_ahead(act, "act")

        def dve_ffn(dve, run, off, gains):
            for f in range(FT + 1):
                if f < FT:
                    split_ahead(dve, "dve")
                    dve.wait_ge(sem("silu"), run * FT + f + 1)
                    dve.tensor_tensor(hid(f, 1, Z), mixT[:, f % 2, 0:T], bank[2 * (f % 2) + 1][:, 0:T], ALU.mult)\
                       .then_inc(sem("hidden_full"), 1)
                if f >= 1:
                    dve.wait_ge(sem("hidden_rounded"), run * FT + f)
                    dve.tensor_tensor(hid(f - 1, 1), hid(f - 1, 1, Z), hid(f - 1, 0).bitcast(F32), ALU.subtract)\
                       .then_inc(sem("hidden"), 1)
            for j in range(FT // 2):
                split_ahead(dve, "dve")
                if j not in (FT // 4, FT // 2 - 1):
                    continue
                half = int(j > FT // 4)
                for q in range(4 * half, 4 * half + 4):
                    dve.wait_ge(sem("down"), run * 8 + q + 1)
                    ps, x = bank[4 + q % 4][:, 0:T], xT[:, q, off:off + T]
                    dve.scalar_tensor_tensor(x, ps, gains(q), x, ALU.mult, ALU.add).then_inc(sem("down_added"), 1)

        BUF, TURN, MIX = 4, 2, 3
        S = [hT[:, i, 0:512] for i in range(BUF)]
        PT = [hT[:, BUF + i, 0:512] for i in range(2)]

        def pe_attention(pe, units):
            n = len(units)
            s_rd, p_rdy, pt_cp, o_cp = (base(pe, x) for x in ("scores_read", "probs", "probs_turned", "heads_out"))
            for i in range(n + MIX):
                if i < n:
                    u = units[i]
                    if i >= 2:
                        pe.wait_ge(sem("scores_read"), s_rd + i - 1)
                    for j, (l, r, m) in enumerate(u["scores"]):
                        last = j == len(u["scores"]) - 1
                        mm(pe, bank[(6 if u["apart"] else 0) + i % 2][:, 0:m], l, r, start=j == 0, stop=last,
                           last_of="scores" if last and not u["apart"] else None)
                    if u["apart"]:
                        l, r = u["apart"]
                        mm(pe, bank[i % 2][:, 0:u["nk"]], l, r, start=True, stop=True, last_of="scores")
                if 0 <= i - TURN < n:
                    u, j = units[i - TURN], i - TURN
                    pe.wait_ge(sem("probs"), p_rdy + j + 1)
                    if j >= 2:
                        pe.wait_ge(sem("probs_turned"), pt_cp + j - 1)
                    for b in range(u["nk"] // P):
                        ins = pe.transpose(bank[2 + j % 2][:, b * P:(b + 1) * P],
                                           S[j % BUF][:, b * P:(b + 1) * P], const("ident"))
                    ins.then_inc(sem("turned"), 1)
                if i >= MIX:
                    u, j = units[i - MIX], i - MIX
                    pe.wait_ge(sem("probs_turned"), pt_cp + j + 1)
                    if j >= 2:
                        pe.wait_ge(sem("heads_out"), o_cp + j - 1)
                    lo, hi = u["rows"]
                    for b, vt in enumerate(u["v"]):
                        last = b == len(u["v"]) - 1
                        mm(pe, bank[4 + j % 2][lo:hi, 0:P], vt, PT[j % 2][:, b * P:(b + 1) * P],
                           start=b == 0, stop=last, last_of="mixed" if last else None)
            for x in ("scores_read", "probs", "probs_turned", "heads_out"):
                advance(pe, x, n)

        def act_attention(act, units):
            n = len(units)
            nm, td, mx = (base(act, x) for x in ("neg_max", "turned", "mixed"))
            for i in range(n + MIX):
                if i < n:
                    u = units[i]
                    col = (i % BUF) * 8
                    act.wait_ge(sem("neg_max"), nm + i + 1)
                    if u["apart"]:
                        act.activation(sc[:, col + 3:col + 4], sc[:, col + 1:col + 2], ACT.Exp)
                        act.activation(S[i % BUF][:, 0:u["nk"]], S[i % BUF][:, 0:u["nk"]], ACT.Exp,
                                       bias=sc[:, col + 1:col + 2]).then_inc(sem("exps"), 1)
                    else:
                        if u["sink"] is not None:
                            act.activation(sc[:, col + 3:col + 4], u["sink"], ACT.Exp, bias=sc[:, col + 1:col + 2])
                        act.activation(S[i % BUF][:, 0:u["nk"]], S[i % BUF][:, 0:u["nk"]], ACT.Exp,
                                       bias=sc[:, col + 1:col + 2], accum_out=sc[:, col + 2:col + 3])\
                           .then_inc(sem("exps"), 1)
                if 0 <= i - TURN < n:
                    u, j = units[i - TURN], i - TURN
                    act.wait_ge(sem("turned"), td + j + 1)
                    if j >= 2:
                        act.wait_ge(sem("mixed"), mx + j - 1)
                    act.activation(PT[j % 2][:, 0:u["nk"]], bank[2 + j % 2][:, 0:u["nk"]], ACT.Copy)\
                       .then_inc(sem("probs_turned"), 1)
                if i >= MIX:
                    u, j = units[i - MIX], i - MIX
                    act.wait_ge(sem("mixed"), mx + j + 1)
                    lo, hi = u["rows"]
                    act.activation(u["out"], bank[4 + j % 2][lo:hi, 0:P], ACT.Copy)\
                       .then_inc(sem("heads_out"), 1)
            for x in ("neg_max", "turned", "mixed"):
                advance(act, x, n)

        def dve_attention(dve, units):
            n = len(units)
            so, ex, td = (base(dve, x) for x in ("scores", "exps", "turned"))
            for i in range(n + 1):
                if i < n:
                    u = units[i]
                    col = (i % BUF) * 8
                    dve.wait_ge(sem("scores"), so + i + 1)
                    if i >= BUF:
                        dve.wait_ge(sem("turned"), td + i - BUF + 1)
                    src = bank[6 + i % 2] if u["apart"] else bank[i % 2]
                    ins = dve.tensor_tensor_reduce(S[i % BUF][:, 0:u["nk"]], src[:, 0:u["nk"]], u["mask"], 1.0,
                                                   u["init"], ALU.add, ALU.max, sc[:, col:col + 1])
                    if u["apart"]:
                        link(dve, ins)
                    else:
                        ins.then_inc(sem("scores_read"), 1)
                        await_next(dve, "scores_read")
                    dve.tensor_scalar(sc[:, col + 1:col + 2], sc[:, col:col + 1], -1.0, None, ALU.mult)\
                       .then_inc(sem("neg_max"), 1)
                if i >= 1:
                    u, j = units[i - 1], i - 1
                    col = (j % BUF) * 8
                    den = sc[:, col + 2:col + 3]
                    Sj = S[j % BUF][:, 0:u["nk"]]
                    dve.wait_ge(sem("exps"), ex + j + 1)
                    if u["apart"]:
                        ins = dve.tensor_tensor_reduce(Sj, bank[j % 2][:, 0:u["nk"]], Sj, HD ** -0.5, 0.0, ALU.mult,
                                                       ALU.add, den)
                        ins.then_inc(sem("scores_read"), 1)
                        await_next(dve, "scores_read")
                        link(dve, dve.tensor_scalar(sc[:, col + 4:col + 5], den, -1.0, None, ALU.mult))
                        link(dve, dve.tensor_tensor(den, den, sc[:, col + 4:col + 5], ALU.max))
                        link(dve, dve.tensor_tensor(den, den, sc[:, col + 3:col + 4], ALU.max))
                    elif u["sink"] is not None:
                        link(dve, dve.tensor_tensor(den, den, sc[:, col + 3:col + 4], ALU.add))
                    link(dve, dve.reciprocal(sc[:, col + 5:col + 6], den))
                    dve.tensor_scalar(Sj, Sj, sc[:, col + 5:col + 6], None, ALU.mult).then_inc(sem("probs"), 1)
            for x in ("scores", "exps", "turned"):
                advance(dve, x, n)

        def dve_log_sigmoid_a(dve, z, t):
            link(dve, dve.tensor_scalar(t, z, -1.0, None, ALU.mult))
            dve.tensor_tensor(t, t, z, ALU.min).then_inc(sem("neg_abs"), 1)

        def act_log_sigmoid(act, t):
            await_next(act, "neg_abs")
            link(act, act.activation(t, t, ACT.Exp))
            act.activation(t, t, ACT.Ln, bias=1.0).then_inc(sem("log1p"), 1)

        def dve_log_sigmoid_b(dve, z, t, scale):
            link(dve, dve.tensor_scalar(z, z, 0.0, scale, ALU.min, ALU.mult))
            await_next(dve, "log1p")
            link(dve, dve.scalar_tensor_tensor(z, t, -scale, z, ALU.mult, ALU.add))

        G_X, G_CTX = (0, T), (T, 2 * T)

        def b1_groups(layer):
            n = 2 * T if layer == 0 else T
            zt = lambda i, b=n: Zt[:, i, 0:b]
            g = []
            for j, tiles in enumerate(((0, 1), (2, 3), (4, 5))):
                g += feature_major([zt(i) for i in tiles], 0, n)
            for tiles in ((6, 7), (8, 9)):
                g += feature_major([zt(i) for i in tiles], 0, n, HD ** -0.5)
            g += feature_major([zt(10, 2 * T)], 0, 2 * T)
            g += token_major([tok[:, t * 384:t * 384 + P] for t in range(4)], 0, P, P, "same")
            g += feature_major([zt(11), zt(12)], 0, n, HD ** -0.5)
            g += feature_major([zt(13, 2 * T), zt(14, 2 * T)], 0, 2 * T)
            g += token_major([tok[:, t * 384 + P:(t + 1) * 384] for t in range(4)])
            g += feature_major([zt(15), zt(16)], 0, n)
            g += feature_major([lrT(0), lrT(1)], 0, 2 * T, rows_=16)
            return g

        lr_ones = Zt[0:32, 17:19, :]

        def lrT(d):
            return Zt[0:16, 17 + d, :]

        c_mat = Zr[:, 0:KT * P].rearrange("p (k m) -> p k m", k=KT)
        mod_rows = Z[0:4, KT * P:KT * P + 6 * D]

        def pe_mod(pe, layer):
            await_next(pe, "c_split")
            for p in range(MOD_PIECES + 1):
                if p < MOD_PIECES:
                    w = piece_slot(pe)
                    if p >= 2:
                        pe.wait_ge(sem("mod_rows"), base(pe, "mod_rows") + p - 1)
                    for k in range(KT):
                        for part in range(2):
                            last = k == KT - 1 and part == 1
                            mm(pe, bank[p % 2][:, 0:256], c_mat[:, k, :], w[part][:, k * 256:(k + 1) * 256],
                               start=k == 0 and part == 0, stop=last, last_of="mod_sums" if last else None)
                    stream["release"] = True
                if p >= 1:
                    pe.wait_ge(sem("mod_rows"), base(pe, "mod_rows") + p)
                    for j in (2 * p - 2, 2 * p - 1):
                        last = j == 2 * MOD_PIECES - 1
                        mm(pe, bank[4][:, 2 * j:2 * j + 2], mod_rows[:, j * P:(j + 1) * P],
                           cst[0:4, CONST["pair"][0]:CONST["pair"][1]], start=True, stop=True,
                           last_of="modulation" if last else None)
            advance(pe, "mod_rows", MOD_PIECES)
            phase_end(pe)

        def act_mod(act, layer):
            if layer == 0:
                act.wait_ge(sem("vectors_in"), 16 * N_LOADS)
                link(act, act.activation(v("c"), v("c"), ACT.Silu))
            await_next(act, "c_cleared")
            c = v("c").rearrange("p (k s) -> p k s", s=2)
            act.activation(c_mat[:, :, 0:2], c, ACT.Copy).then_inc(sem("c_rounded"), 1)
            for p in range(MOD_PIECES):
                split_ahead(act, "act")
                await_next(act, "mod_sums")
                act.activation(mod_rows[:, p * 256:(p + 1) * 256], bank[p % 2][0:4, 0:256], ACT.Copy)\
                   .then_inc(sem("mod_rows"), 1)
            phase_end(act)

        def dve_mod(dve, layer):
            dve.memset(lr_ones, 1.0)
            if layer == 0:
                dve.wait_ge(sem("vectors_in"), 16 * N_LOADS)
                link(dve, dve.tensor_copy(lvl_mask[:, :, :].rearrange("p l n -> p (l n)"), Z[:, 0:2 * LEVELS * P]))
            dve.memset(c_mat.bitcast(F32), 0.0).then_inc(sem("c_cleared"), 1)
            await_next(dve, "c_rounded")
            dve.tensor_tensor(c_mat[:, :, 2:4], v("c").rearrange("p (k s) -> p k s", s=2),
                              c_mat[:, :, 0:2].bitcast(F32), ALU.subtract).then_inc(sem("c_split"), 1)
            for p in range(MOD_PIECES):
                split_ahead(dve, "dve")
            await_next(dve, "modulation")
            link(dve, dve.tensor_tensor(modT[:, :, :], bank[4][:, 0:96].rearrange("p (j s) -> p j s", s=2),
                                        v("b_mod", layer).unsqueeze(2).to_broadcast([P, 48, 2]), ALU.add))
            for i, name in ((0, "norm1"), (1, "norm2")):
                lo = 8 + 24 * i
                dve.scalar_tensor_tensor(a1[:, i, :, :], modT[:, lo:lo + 8, :], 1.0,
                                         v(name, layer).unsqueeze(2).to_broadcast([P, KT, 2]),
                                         ALU.add, ALU.mult)
            phase_end(dve)

        def b1_segments(which, n):
            segs = [(s * T, (s + 1) * T,
                     (lambda k, s=s: a1[:, which, k, s:s + 1]),
                     (lambda k, s=s: modT[:, 24 * which + k, s:s + 1])) for s in range(n // T)]
            return segs

        U = Zt[:, 19:22, :].rearrange("p a b -> p (a b)")[:, 0:2 * 2 * 258].rearrange("p (c s n) -> p c s n", c=2, s=2)

        def pe_rope(pe, layer):
            for j in range(5):
                if j >= 4:
                    await_next(pe, "rotated_read")
                mm(pe, bank[j % 4][:, 0:T], const("rot"), Zt[:, 6 + j, 0:T], start=True, stop=True,
                   last_of="rotated")
            advance(pe, "rotated_read", 4)
            phase_end(pe)

        def act_rope(act, layer):
            phase_end(act)

        def dve_rope_conv(dve, layer):
            for j in range(5):
                await_next(dve, "rotated")
                z, t = Zt[:, 6 + j, 0:T], hT[:, j, 0:T]
                dve.tensor_tensor(t, bank[j % 4][:, 0:T], const("sin"), ALU.mult).then_inc(sem("rotated_read"), 1)
                link(dve, dve.tensor_tensor(z, z, const("cos"), ALU.mult))
                await_next(dve, "rotated_read")
                dve.tensor_tensor(z, z, t, ALU.add)
            ns = 2 if layer == 0 else 1
            link(dve, dve.memset(U[:, :, :, :], 0.0))
            for c in range(2):
                seg = lambda i: Zt[:, i + c, 0:ns * T].rearrange("p (s n) -> p s n", s=ns)
                w = lambda j: v("conv_w", layer, 2 * j + c, 2 * j + c + 1)
                y = hT[:, 5 + c, 0:ns * T].rearrange("p (s n) -> p s n", s=ns)
                link(dve, dve.tensor_tensor(U[:, c, 0:ns, 1:T + 1], seg(0), seg(4), ALU.mult))
                link(dve, dve.tensor_scalar(y, U[:, c, 0:ns, 0:T], w(0), None, ALU.mult))
                for j in (1, 2):
                    link(dve, dve.scalar_tensor_tensor(y, U[:, c, 0:ns, j:T + j], w(j), y, ALU.mult, ALU.add))
                link(dve, dve.tensor_tensor(mixT[:, c, 0:ns * T].rearrange("p (s n) -> p s n", s=ns), y, seg(2),
                                            ALU.mult))
            phase_end(dve)

        def b1_units(layer):
            units = []
            for s in range(2 if layer == 0 else 1):
                for h in range(8):
                    g, t = divmod(h, 4)
                    r0 = g * HD
                    for q in range(TT):
                        tq = s * T + q * P
                        keys = (0, 2 * T) if s == 0 else (T, 2 * T)
                        nk = keys[1] - keys[0]
                        if s == 0:
                            mask = const("masks", 0, 512) if q == 1 else const("masks", 384, 896)
                        else:
                            mask = const("masks", 128, 384)
                        units.append(dict(apart=None,
                            scores=[(Zt[r0:r0 + HD, 6 + t, tq:tq + P], Zt[r0:r0 + HD, 10, keys[0]:keys[1]], nk)],
                            nk=nk, mask=mask, init=v("sink", layer, h, h + 1), sink=v("sink", layer, h, h + 1),
                            v=[tok[:, b * 384 + g * HD:b * 384 + (g + 1) * HD] for b in range(keys[0] // P, keys[1] // P)],
                            rows=((h % 2) * HD, (h % 2 + 1) * HD),
                            out=mixT[(h % 2) * HD:(h % 2 + 1) * HD, 2 + h // 2, tq:tq + P]))
            return units

        gB = [hflat[:, d * 1024:(d + 1) * 1024].rearrange("p (c n) -> p c n", c=2) for d in range(2)]
        gG = hflat[:, 2048:4096].rearrange("p (t c) -> p t c", t=4)
        gM = [Z[:, i * 1024:(i + 1) * 1024].rearrange("p (c n) -> p c n", c=2) for i in range(2)]
        gE = [Z[:, (2 + i) * 1024:(3 + i) * 1024].rearrange("p (c n) -> p c n", c=2) for i in range(2)]
        gA = Z[:, 19 * 512 - 1024:19 * 512 + 1024].rearrange("p (t h n) -> p t h n", t=4, h=4)
        gK = Z[:, 4096:4352].rearrange("p (c n) -> p c n", c=2)
        gKt = Z[:, 4352:4608]
        gS = Z[:, 4608:5120].rearrange("p (d c n) -> p d c n", d=2, c=2)
        gX = Z[:, 5120:5376].rearrange("p (c n) -> p c n", c=2)
        gQ = Z[:, 0:2048].rearrange("p (d t c n) -> p d t c n", d=2, t=4, c=2)
        gD = sc[:, 16:32].rearrange("p (d t c) -> p d t c", d=2, t=4)

        GQ, GK = Zt[:, 11:13, :], Zt[:, 13:15, :]
        ORDER = ((2, 3, 0, 1), (3, 2, 1, 0))

        def pe_gla_gates(pe, layer):
            for t in range(4):
                for d in range(2):
                    ps = bank[t][:, d * 256:(d + 1) * 256]
                    mm(pe, ps, lr_ones[0:17, d, t * P:(t + 1) * P], gate_w[:, layer, d, :], start=True, stop=True,
                       last_of="gates" if d == 1 else None)
            await_next(pe, "log_gates")
            for d in range(2):
                for c in range(2):
                    for t in range(4):
                        mm(pe, bank[4 + 2 * d + c][:, t * P:(t + 1) * P], gG[:, t, d * 256 + c * P:d * 256 + (c + 1) * P],
                           const("tri" if d == 0 else "tri_r"), start=True, stop=True,
                           last_of="decays" if t == 3 else None)
            phase_end(pe)

        def act_gla_gates(act, layer):
            act_log_sigmoid(act, Z[:, 0:2048])
            for d in range(2):
                for c in range(2):
                    await_next(act, "decays")
                    link(act, act.activation(gB[d][:, c, :], bank[4 + 2 * d + c][:, :], ACT.Copy))
                    edge = slice(P - 1, 512, P) if d == 0 else slice(0, 512, P)
                    act.activation(gD[:, d, :, c], gB[d][:, c, edge], ACT.Exp)
            phase_end(act)

        def dve_gla_gates(dve, layer):
            for t in range(4):
                await_next(dve, "gates")
                ins = dve.tensor_copy(gG[:, t, :], bank[t][:, :])
            link(dve, ins)
            g = hflat[:, 2048:4096]
            dve_log_sigmoid_a(dve, g, Z[:, 0:2048])
            link(dve, dve.tensor_scalar(g, g, 0.0, 1.0 / 16, ALU.min, ALU.mult))
            await_next(dve, "log1p")
            dve.scalar_tensor_tensor(g, Z[:, 0:2048], -1.0 / 16, g, ALU.mult, ALU.add).then_inc(sem("log_gates"), 1)
            phase_end(dve)

        def gla_level(l, buf, d, n):
            h = 1 << l
            x = buf[:, :, 0:n].rearrange("p c (b u h) -> p c b u h", u=2, h=h)
            return x[:, :, :, 0, :], x[:, :, :, 1, :]

        def gram(t, h):
            return bank[2 * t + h % 2][:, (h // 2) * P:(h // 2 + 1) * P]

        def grams(t):
            return psum[:, 2 * t:2 * t + 2, 0:2 * P].rearrange("p u (v n) -> p u v n", v=2)

        def by_bank(t):
            return gA[:, t].rearrange("p (v u) n -> p u v n", v=2)

        def gla_steps():
            return [(l, d) for l in range(LEVELS) for d in range(2)]

        def pe_gla_levels(pe, layer):
            tiles = range(4 if layer == 0 else 2)
            for t in tiles:
                for h in range(4):
                    r = slice((h % 2) * HD, (h % 2 + 1) * HD)
                    mm(pe, gram(t, h), GK[r, h // 2, t * P:(t + 1) * P],
                       GQ[r, h // 2, t * P:(t + 1) * P], start=True, stop=True,
                       last_of="grams" if h == 3 else None)
            rd = base(pe, "gram_read")
            nt = len(tiles)
            for i, (l, d) in enumerate(gla_steps()):
                await_next(pe, "level")
                for t in tiles:
                    pe.wait_ge(sem("gram_read"), rd + i * nt + t + 1)
                    for h in range(4):
                        r = slice((h % 2) * HD, (h % 2 + 1) * HD)
                        m = gM[i % 2][r, h // 2, t * P:(t + 1) * P]
                        mm(pe, gram(t, h), m, m, start=True, stop=True,
                           last_of="grams" if h == 3 else None)
            advance(pe, "gram_read", nt * (1 + 2 * LEVELS))
            phase_end(pe)

        def act_gla_levels(act, layer):
            n = 2 * T if layer == 0 else T
            for i, (l, d) in enumerate(gla_steps()):
                await_next(act, "level_decay")
                e = gE[i % 2][:, :, 0:n]
                act.activation(e, e, ACT.Exp).then_inc(sem("level_exp"), 1)
            phase_end(act)

        def dve_gla_levels(dve, layer):
            n = 2 * T if layer == 0 else T
            nt = n // P
            steps = gla_steps()

            def decay(i):
                l, d = steps[i]
                h = 1 << l
                lo, hi = gla_level(l, gB[d], d, n)
                e_lo, e_hi = gla_level(l, gE[i % 2], d, n)
                m = (lo[:, :, :, h - 1:h] if d == 0 else hi[:, :, :, 0:1])
                for c in range(2):
                    mb = m[:, c].to_broadcast([P, n // (2 * h), h])
                    a, b = (hi, lo) if d == 0 else (lo, hi)
                    ea, eb = (e_hi, e_lo) if d == 0 else (e_lo, e_hi)
                    dve.tensor_tensor(ea[:, c], a[:, c], mb, ALU.subtract)
                    ins = dve.tensor_tensor(eb[:, c], mb, b[:, c], ALU.subtract)
                ins.then_inc(sem("level_decay"), 1)

            def scaled(i):
                l, d = steps[i]
                q_lo, q_hi = gla_level(l, GQ, d, n)
                k_lo, k_hi = gla_level(l, GK, d, n)
                e_lo, e_hi = gla_level(l, gE[i % 2], d, n)
                m_lo, m_hi = gla_level(l, gM[i % 2], d, n)
                await_next(dve, "level_exp")
                if i >= 2:
                    dve.wait_ge(sem("grams"), gr + nt * i)
                for c in range(2):
                    dve.tensor_tensor(m_lo[:, c], (k_lo if d == 0 else q_lo)[:, c], e_lo[:, c], ALU.mult)
                    ins = dve.tensor_tensor(m_hi[:, c], (q_hi if d == 0 else k_hi)[:, c], e_hi[:, c], ALU.mult)
                ins.then_inc(sem("level"), 1)

            gr = base(dve, "grams")
            own = base(dve, "gram_read")
            decay(0)
            for t in range(nt):
                dve.wait_ge(sem("grams"), gr + t + 1)
                eye = const("ident").unsqueeze(1).to_broadcast([P, 2, P])
                for u in range(2):
                    ins = dve.scalar_tensor_tensor(by_bank(t)[:, u], grams(t)[:, u], 2.0, eye, ALU.mult, ALU.mult)
                ins.then_inc(sem("gram_read"), 1)
            for i, (l, d) in enumerate(steps):
                scaled(i)
                if i + 1 < len(steps):
                    decay(i + 1)
                mask = lvl_mask[:, 2 * l + d, :].unsqueeze(1).unsqueeze(1).to_broadcast([P, 2, 2, P])
                for t in range(nt):
                    dve.wait_ge(sem("grams"), gr + nt * (i + 1) + t + 1)
                    dve.wait_ge(sem("gram_read"), own + nt * i + t + 1)
                    dve.copy_predicated(by_bank(t), mask, grams(t))\
                       .then_inc(sem("gram_read"), 1)
            advance(dve, "grams", nt * (1 + 2 * LEVELS))
            advance(dve, "gram_read", nt * (1 + 2 * LEVELS))
            phase_end(dve)

        def pe_gla_out(pe, layer):
            outs = (0, 1, 2, 3) if layer == 0 else (0, 1)
            await_next(pe, "queries_decayed")
            first = {t: True for t in outs}
            for d in range(2):
                for i, t in enumerate(ORDER[d]):
                    if i > 0 and t in outs:
                        await_next(pe, "state")
                        for c in range(2):
                            mm(pe, bank[t][:, c * P:(c + 1) * P], gS[:, d, c, :], gQ[:, d, t, c, :],
                               start=first[t] and c == 0, stop=False, skip_group_check=True,
                               last_of="state_used" if c == 1 else None)
                        first[t] = False
                    elif i > 0:
                        await_next(pe, "state")
                        pe.nop().then_inc(sem("state_used"), 1)
                    if i < 3:
                        await_next(pe, "keys_decayed")
                        for c in range(2):
                            ins = pe.transpose(bank[4][:, c * P:(c + 1) * P], gK[:, c, :], const("ident"))
                        ins.then_inc(sem("keys_turned"), 1)
                        await_next(pe, "keys_copied")
                        for c in range(2):
                            mm(pe, bank[5][:, c * P:(c + 1) * P], gKt[:, c * P:(c + 1) * P],
                               tok[:, t * 384 + P + c * P:t * 384 + P + (c + 1) * P], start=True, stop=True,
                               last_of="state_step" if c == 1 else None)
            for t in outs:
                for h in range(4):
                    mm(pe, bank[t][(h % 2) * HD:(h % 2 + 1) * HD, (h // 2) * P:(h // 2 + 1) * P],
                       tok[:, t * 384 + P + h * HD:t * 384 + P + (h + 1) * HD], gA[:, t, h, :],
                       start=False, stop=True, skip_group_check=True, last_of="gla_sum" if h == 3 else None)
            phase_end(pe)

        def act_gla_out(act, layer):
            outs = (0, 1, 2, 3) if layer == 0 else (0, 1)
            for d in range(2):
                for t in outs:
                    for c in range(2):
                        ins = act.activation(gQ[:, d, t, c, :], gB[d][:, c, t * P:(t + 1) * P], ACT.Exp)
            ins.then_inc(sem("query_exp"), 1)
            for d in range(2):
                for i, t in enumerate(ORDER[d][:3]):
                    if d or i:
                        await_next(act, "keys_decayed")
                    edge = t * P + (P - 1 if d == 0 else 0)
                    for c in range(2):
                        ins = act.activation(gX[:, c, :], gB[d][:, c, t * P:(t + 1) * P], ACT.Exp, scale=-1.0,
                                             bias=gB[d][:, c, edge:edge + 1])
                    ins.then_inc(sem("key_exp"), 1)
                    await_next(act, "keys_turned")
                    act.activation(gKt, bank[4][:, 0:256], ACT.Copy).then_inc(sem("keys_copied"), 1)
            advance(act, "keys_decayed", 1)
            phase_end(act)

        def dve_gla_out(dve, layer):
            outs = (0, 1, 2, 3) if layer == 0 else (0, 1)
            link(dve, dve.memset(gS[:, :, :, :].rearrange("p d c n -> p (d c n)"), 0.0))
            await_next(dve, "query_exp")
            for d in range(2):
                for t in outs:
                    ins = dve.tensor_tensor(gQ[:, d, t, :, :], gQ[:, d, t, :, :], GQ[:, :, t * P:(t + 1) * P], ALU.mult)
            ins.then_inc(sem("queries_decayed"), 1)
            for d in range(2):
                for i, t in enumerate(ORDER[d][:3]):
                    await_next(dve, "key_exp")
                    dve.tensor_tensor(gK[:, :, :], gX[:, :, :], GK[:, :, t * P:(t + 1) * P], ALU.mult)\
                       .then_inc(sem("keys_decayed"), 1)
                    await_next(dve, "state_step")
                    if i > 0:
                        await_next(dve, "state_used")
                    for c in range(2):
                        for r in range(2):
                            rr = slice(r * HD, (r + 1) * HD)
                            s = gS[rr, d, c, rr]
                            ins = dve.scalar_tensor_tensor(s, s, gD[rr, d, t, c:c + 1],
                                                           bank[5][rr, c * P + r * HD:c * P + (r + 1) * HD],
                                                           ALU.mult, ALU.add)
                    link(dve, ins)
                    dve.nop().then_inc(sem("state"), 1)
                await_next(dve, "state_used")
            phase_end(dve)

        def gla_o(layer):
            n = 2 * T if layer == 0 else T
            return n, Z[:, 0:2 * n].rearrange("p (c n) -> p c n", c=2)

        def pe_gla_norm(pe, layer):
            for c in range(2):
                await_next(pe, "gla_squared")
                n = 2 * T if layer == 0 else T
                mm(pe, bank[4 + c][:, 0:n], const("head_mean"), gSq[:, c, 0:n], start=True, stop=True,
                   last_of="gla_mean_square")
            phase_end(pe)

        gSq = hflat[:, 0:1024].rearrange("p (c n) -> p c n", c=2)
        gR = hflat[:, 1024:2048].rearrange("p (c n) -> p c n", c=2)
        gSi = hflat[:, 2048:3072].rearrange("p (c n) -> p c n", c=2)

        def act_gla_norm(act, layer):
            n, o = gla_o(layer)
            for t in range(n // P):
                link(act, act.activation(o[:, :, t * P:(t + 1) * P],
                                         bank[t][:, 0:256].rearrange("p (c n) -> p c n", c=2), ACT.Copy))
            for c in range(2):
                act.activation(gSq[:, c, 0:n], o[:, c, :], ACT.Square).then_inc(sem("gla_squared"), 1)
            for c in range(2):
                await_next(act, "gla_mean_square")
                link(act, act.activation(gR[:, c, 0:n], bank[4 + c][:, 0:n], ACT.Ln, bias=EPS))
                act.activation(gR[:, c, 0:n], gR[:, c, 0:n], ACT.Exp, scale=-0.5).then_inc(sem("gla_rms"), 1)
            for c in range(2):
                act.activation(gSi[:, c, 0:n], Zt[:, 15 + c, 0:n], ACT.Silu).then_inc(sem("gla_silu"), 1)
            phase_end(act)

        def dve_gla_norm(dve, layer):
            n, o = gla_o(layer)
            for c in range(2):
                await_next(dve, "gla_rms")
                link(dve, dve.scalar_tensor_tensor(gR[:, c, 0:n], gR[:, c, 0:n], v("gla_g", layer), o[:, c, :],
                                                   ALU.mult, ALU.mult))
            for c in range(2):
                await_next(dve, "gla_silu")
                dve.tensor_tensor(mixT[:, 6 + c, 0:n], gR[:, c, 0:n], gSi[:, c, 0:n], ALU.mult)
            phase_end(dve)

        def out_groups(kts, n, gains, per_piece):
            res = []
            for d in range(KT):
                c = d % per_piece
                w_ = per_piece * P
                terms = [((lambda w, _, k=k, c=c: w[:, k * w_ + c * P:k * w_ + (c + 1) * P]),
                          (lambda _, p, k=k: mix(p, k, 0, n))) for k in range(kts)]
                evs = [("resid", xT[:, d, s * T:(s + 1) * T], gains(d, s), s * T, (s + 1) * T) for s in range(n // T)]
                res.append((terms, P, n, evs, "new" if c == 0 else "same"))
            return res

        UP = mixT[:, 0:5, :].rearrange("p a b -> p (a b)")[:, 0:4 * 259].rearrange("p (c n) -> p c n", c=4)
        CP = mixflat[:, 1040:1040 + 2 * 286].rearrange("p (c n) -> p c n", c=2)
        SG = sc[:, 44:76].rearrange("p (t c) -> p t c", t=2)
        FC = sc[:, 76:84].rearrange("p (t c) -> p t c", t=2)
        BH = Z[:, 18 * 512:18 * 512 + 1536].rearrange("p (h n) -> p h n", h=4)

        def mv(t, h):
            return tok[:, t * 768 + h * HD:t * 768 + (h + 1) * HD]

        def fv(t, h):
            return tok[:, t * 768 + 256 + h * HD:t * 768 + 256 + (h + 1) * HD]

        def z2(i):
            return Zt[:, i, 0:T]

        def b2_groups(layer):
            g = feature_major([UP[:, 0, 3:259], UP[:, 1, 3:259]], 0, T)
            g += feature_major([UP[:, 2, 3:259], UP[:, 3, 3:259]], 0, T)
            g += token_major([tok[:, t * 768:t * 768 + 256] for t in range(2)])
            g += feature_major([z2(4), z2(5)], 0, T)
            g += feature_major([z2(6), z2(7)], 0, T)
            g += feature_major([z2(8), z2(9)], 0, T)
            for j in range(2):
                g += feature_major([z2(10 + 2 * j), z2(11 + 2 * j)], 0, T, HD ** -0.5)
            for j in range(2):
                g += feature_major([z2(14 + 2 * j), z2(15 + 2 * j)], 0, T)
            for j in range(2):
                g += token_major([tok[:, t * 768 + 256 + 256 * j:t * 768 + 512 + 256 * j] for t in range(2)])
            g += token_major([SG[:, t, :] for t in range(2)], n=16)
            return g

        def act_b2_conv(act, layer):
            act_log_sigmoid(act, sc[:, 0:24].rearrange("p (t c) -> p t c", t=2))
            for c in range(2):
                act.activation(z2(8 + c), z2(8 + c), ACT.Sigmoid).then_inc(sem("glu"), 1)
            for c in range(4):
                await_next(act, "m_conv")
                act.activation(z2(c), z2(c), ACT.Silu)
            phase_end(act)

        def pe_b2_conv(pe, layer):
            await_next(pe, "log_f")
            mm(pe, bank[0][:, 0:4], const("tri"), SG[:, 0, 4:8], start=True, stop=True, last_of=None)
            mm(pe, bank[1][:, 0:4], const("ones"), SG[:, 0, 4:8], start=True, stop=False, last_of=None)
            mm(pe, bank[1][:, 0:4], const("tri"), SG[:, 1, 4:8], start=False, stop=True, last_of="f_sums")
            phase_end(pe)

        def dve_b2_conv(dve, layer):
            bias = v("gate_b", layer).unsqueeze(1).to_broadcast([P, 2, 16])
            link(dve, dve.tensor_tensor(SG[:, :, :], SG[:, :, :], bias, ALU.add))
            z, t = SG[:, :, 4:16], sc[:, 0:24].rearrange("p (t c) -> p t c", t=2)
            dve_log_sigmoid_a(dve, z, t)
            link(dve, dve.tensor_scalar(z, z, 0.0, None, ALU.min))
            await_next(dve, "log1p")
            dve.tensor_tensor(z, z, t, ALU.subtract).then_inc(sem("log_f"), 1)
            for c in range(2):
                link(dve, dve.memset(CP[:, c, 0:30], 0.0))
                dve.memset(UP[:, 2 * c, 0:3], 0.0)
                link(dve, dve.memset(UP[:, 2 * c + 1, 0:3], 0.0))
            for c in range(4):
                w = lambda j: v("m_conv_w", layer, 4 * j + c, 4 * j + c + 1)
                link(dve, dve.tensor_scalar(z2(c), UP[:, c, 0:T], w(0), v("m_conv_b", layer, c, c + 1),
                                            ALU.mult, ALU.add))
                for j in (1, 2):
                    link(dve, dve.scalar_tensor_tensor(z2(c), UP[:, c, j:j + T], w(j), z2(c), ALU.mult, ALU.add))
                dve.scalar_tensor_tensor(z2(c), UP[:, c, 3:3 + T], w(3), z2(c), ALU.mult, ALU.add)\
                   .then_inc(sem("m_conv"), 1)
            for c in range(2):
                await_next(dve, "glu")
                link(dve, dve.tensor_tensor(CP[:, c, 30:30 + T], z2(6 + c), z2(8 + c), ALU.mult))
            for j in range(31):
                for c in range(2):
                    w = v("c_conv_w", layer, 2 * j + c, 2 * j + c + 1)
                    if j == 0:
                        ins = dve.tensor_scalar(z2(6 + c), CP[:, c, 0:T], w, v("c_conv_b", layer, c, c + 1),
                                                ALU.mult, ALU.add)
                    else:
                        ins = dve.scalar_tensor_tensor(z2(6 + c), CP[:, c, j:j + T], w, z2(6 + c), ALU.mult, ALU.add)
                link(dve, ins)
            await_next(dve, "f_sums")
            dve.tensor_copy(FC[:, 0, :], bank[0][:, 0:4])
            dve.tensor_copy(FC[:, 1, :], bank[1][:, 0:4])
            phase_end(dve)

        def pe_b2_ln(pe, layer):
            for c in range(2):
                mm(pe, bank[0][:, 0:T], const("mean"), z2(6 + c), start=c == 0, stop=c == 1,
                   last_of="ln_mean" if c == 1 else None)
            for c in range(2):
                await_next(pe, "ln_squared")
                mm(pe, bank[1][:, 0:T], const("mean"), z2(8 + c), start=c == 0, stop=c == 1,
                   last_of="ln_var" if c == 1 else None)
            phase_end(pe)

        def act_b2_ln(act, layer):
            for c in range(2):
                await_next(act, "ln_centred")
                act.activation(z2(8 + c), z2(6 + c), ACT.Square).then_inc(sem("ln_squared"), 1)
            await_next(act, "ln_var")
            link(act, act.activation(hT[:, 4, 0:T], bank[1][:, 0:T], ACT.Ln, bias=EPS, scale=4.0))
            act.activation(hT[:, 4, 0:T], hT[:, 4, 0:T], ACT.Exp, scale=-0.5).then_inc(sem("ln_rms"), 1)
            for c in range(2):
                await_next(act, "ln_scaled")
                act.activation(mixT[:, 2 + c, 0:T], z2(6 + c), ACT.Silu, bias=v("ln_b", layer, c, c + 1))
            phase_end(act)

        def dve_b2_ln(dve, layer):
            await_next(dve, "ln_mean")
            for c in range(2):
                dve.scalar_tensor_tensor(z2(6 + c), bank[0][:, 0:T], -4.0, z2(6 + c), ALU.mult, ALU.add)\
                   .then_inc(sem("ln_centred"), 1)
            await_next(dve, "ln_rms")
            for c in range(2):
                dve.scalar_tensor_tensor(z2(6 + c), z2(6 + c), v("ln_w", layer, c, c + 1), hT[:, 4, 0:T],
                                         ALU.mult, ALU.mult).then_inc(sem("ln_scaled"), 1)
            phase_end(dve)

        def dve_decay_columns(dve, f0, i0):
            for j in range(4):
                f = [SG[:, t, f0 + j:f0 + j + 1] for t in range(2)]
                dve.tensor_scalar(BH[:, j, 0:P], const("strict"), f[0], None, ALU.mult)
                both = cst[:, CONST["ones"][0]:CONST["strict"][1]]
                ins = dve.tensor_scalar(BH[:, j, P:384], both, f[1], None, ALU.mult)
                if i0 is not None:
                    link(dve, ins)
                    i = [SG[:, t, i0 + j:i0 + j + 1] for t in range(2)]
                    dve.scalar_tensor_tensor(BH[:, j, 0:P], const("ident"), i[0], BH[:, j, 0:P], ALU.mult, ALU.add)
                    dve.scalar_tensor_tensor(BH[:, j, 256:384], const("ident"), i[1], BH[:, j, 256:384],
                                             ALU.mult, ALU.add)
            phase_end(dve)

        def decay_pairs(j, q):
            if q == 0:
                return [(const("tri"), BH[:, j, 0:P], P)]
            return [(const("tri"), BH[:, j, P:384], 256), (const("ones"), BH[:, j, 0:P], P)]

        def causal(q):
            return const("masks", 512, 640) if q == 0 else const("masks", 384, 640)

        def fox_units(part):
            units = []
            for j in range(4):
                h = 4 * part + j
                r = slice((h % 2) * HD, (h % 2 + 1) * HD)
                for q in range(TT):
                    nk = (q + 1) * P
                    units.append(dict(apart=None,
                        scores=[(Zt[r, 10 + h // 2, q * P:(q + 1) * P], Zt[r, 14 + h // 2, 0:nk], nk)] + decay_pairs(j, q),
                        nk=nk, mask=causal(q), init=3 * NEG, sink=None,
                        v=[fv(t, h) for t in range(q + 1)], rows=(r.start, r.stop),
                        out=mixT[r, 4 + h // 2, q * P:(q + 1) * P]))
            return units

        def mlstm_units():
            units = []
            for h in range(4):
                r = slice((h % 2) * HD, (h % 2 + 1) * HD)
                for q in range(TT):
                    nk = (q + 1) * P
                    units.append(dict(
                        apart=(Zt[r, h // 2, q * P:(q + 1) * P], Zt[r, 2 + h // 2, 0:nk]),
                        scores=decay_pairs(h, q), nk=nk, mask=causal(q), init=FC[:, q, h:h + 1], sink=None,
                        v=[mv(t, h) for t in range(q + 1)], rows=(r.start, r.stop),
                        out=Zt[r, 6 + h // 2, q * P:(q + 1) * P]))
            return units

        def pe_m_norm(pe, layer):
            for c in range(2):
                await_next(pe, "m_squared")
                mm(pe, bank[c][:, 0:T], const("head_mean"), z2(8 + c), start=True, stop=True, last_of="m_mean_square")
            phase_end(pe)

        def act_m_norm(act, layer):
            for c in range(2):
                act.activation(z2(8 + c), z2(6 + c), ACT.Square).then_inc(sem("m_squared"), 1)
                act.activation(z2(4 + c), z2(4 + c), ACT.Sigmoid).then_inc(sem("m_gate"), 1)
            for c in range(2):
                await_next(act, "m_mean_square")
                link(act, act.activation(hT[:, 4 + c, 0:T], bank[c][:, 0:T], ACT.Ln, bias=EPS))
                act.activation(hT[:, 4 + c, 0:T], hT[:, 4 + c, 0:T], ACT.Exp, scale=-0.5).then_inc(sem("m_rms"), 1)
            phase_end(act)

        def dve_m_norm(dve, layer):
            for c in range(2):
                await_next(dve, "m_gate")
                await_next(dve, "m_rms")
                link(dve, dve.scalar_tensor_tensor(z2(6 + c), z2(6 + c), v("m_norm", layer, c, c + 1), hT[:, 4 + c, 0:T],
                                                   ALU.mult, ALU.mult))
                dve.tensor_tensor(mixT[:, c, 0:T], z2(6 + c), z2(4 + c), ALU.mult)
            phase_end(dve)

        def x_groups(layer):
            g = []
            for j in range(2):
                g += feature_major([z2(2 * j), z2(2 * j + 1)], 0, T, float(P) ** -0.5)
            for j in range(2):
                g += feature_major([z2(4 + 2 * j), z2(5 + 2 * j)], T, 2 * T)
            for j in range(2):
                g += token_major([tok[:, t * 768 + 256 * j:t * 768 + 256 * (j + 1)] for t in range(2)], 2)
            return g

        def x_units():
            return [dict(apart=None, scores=[(Zt[:, h, q * P:(q + 1) * P], z2(4 + h), T)], nk=T,
                         mask=const("masks", 128, 384), init=3 * NEG, sink=None,
                         v=[tok[:, t * 768 + h * P:t * 768 + (h + 1) * P] for t in range(2)], rows=(0, P),
                         out=mixT[:, h, q * P:(q + 1) * P]) for h in range(4) for q in range(TT)]

        LG = sc[:, 0:16].rearrange("p (t e) -> p t e", t=2)
        RK = sc[:, 16:32].rearrange("p (t e) -> p t e", t=2)
        EX = sc[:, 32:48].rearrange("p (t e) -> p t e", t=2)
        TOP = sc[:, 48:50].rearrange("p (t e) -> p t e", t=2)
        CMP = mixT[:, 0, 0:128].rearrange("p (t i j) -> p t i j", t=2, i=N_EXP)
        EQ = mixT[:, 1, 0:16].rearrange("p (t e) -> p t e", t=2)
        POS = sc[:, 52:72].rearrange("p (t e) -> p t e", t=2)
        GT = sc[:, 72:92].rearrange("p (t e) -> p t e", t=2)
        h_tok = Z[:, 5632:7680].rearrange("p (t n) -> p t n", t=2)
        y_e = Z[:, 7680:8704]
        silu_b = [Z[:, 8704 + i * 256:8960 + i * 256] for i in range(2)]
        hid_tok = [Z[:, 9216 + i * 256:9472 + i * 256] for i in range(2)]
        place_w = [Z[:, 9728 + i * 256:9984 + i * 256] for i in range(2)]
        select_w = Z[:, 10240:10496].rearrange("p (t n) -> p t n", t=2)
        select = Z[:, 10496:10752].rearrange("p (t n) -> p t n", t=2)
        g_part = [a_hi[:, 4 * i:4 * i + 2, :].rearrange("p a b -> p (a b)") for i in range(2)]

        def hid_e(f, part):
            return Zr[:, (2 * f + part) * P:(2 * f + part + 1) * P]
        def router_groups():
            return token_major([LG[:, t, :] for t in range(2)], n=N_EXP)

        def dve_router(dve):
            for t in range(2):
                ins = dve.tensor_tensor(CMP[:, t], LG[:, t].unsqueeze(1).to_broadcast([P, N_EXP, N_EXP]),
                                        LG[:, t].unsqueeze(2).to_broadcast([P, N_EXP, N_EXP]), ALU.is_gt)
            dve.tensor_reduce(TOP[:, :, 0], LG[:, :, :], AX.X, ALU.max)
            link(dve, dve.tensor_copy(EX[:, :, :], LG[:, :, :]))
            link(dve, dve.tensor_reduce(RK[:, :, :], CMP[:, :, :, :], AX.X, ALU.add))
            for j in range(N_EXP - 1):
                m = N_EXP - 1 - j
                link(dve, dve.tensor_tensor(EQ[:, :, 0:m], LG[:, :, j + 1:N_EXP],
                                            LG[:, :, j:j + 1].to_broadcast([P, 2, m]), ALU.is_equal))
                link(dve, dve.tensor_tensor(RK[:, :, j + 1:N_EXP], RK[:, :, j + 1:N_EXP], EQ[:, :, 0:m], ALU.add))
            link(dve, dve.tensor_scalar(RK[:, :, :], RK[:, :, :], 1.5, None, ALU.is_lt))
            dve.tensor_tensor(EX[:, :, :], EX[:, :, :], TOP[:, :, :].to_broadcast([P, 2, N_EXP]), ALU.subtract)\
               .then_inc(sem("logits_below_max"), 1)
            dve.drain().then_inc(sem("choices"), 1)
            await_next(dve, "logits_exp")
            link(dve, dve.tensor_tensor(EX[:, :, :], EX[:, :, :], RK[:, :, :], ALU.mult))
            link(dve, dve.tensor_reduce(TOP[:, :, 0], EX[:, :, :], AX.X, ALU.add))
            link(dve, dve.reciprocal(TOP[:, :, :], TOP[:, :, :]))
            dve.memset(GT[:, :, :], 0.0)
            link(dve, dve.memset(POS[:, :, :], -1.0))
            dve.memset(y_e, 0.0)
            dve.memset(place_w[1], 0.0)
            dve.tensor_tensor(GT[:, :, 0:N_EXP], EX[:, :, :], TOP[:, :, :].to_broadcast([P, 2, N_EXP]), ALU.mult)
            await_next(dve, "choice_counts")
            for t in range(2):
                ins = dve.tensor_tensor(POS[:, t, 0:N_EXP], RK[:, t, :], bank[t][:, 0:N_EXP], ALU.mult)
            link(dve, ins)
            link(dve, dve.tensor_scalar(POS[:, :, 0:N_EXP], POS[:, :, 0:N_EXP], -1.0, None, ALU.add))
            link(dve, dve.tensor_reduce(TOP[:, 0, :], bank[2][:, 0:N_EXP], AX.X, ALU.max))
            link(dve, dve.tensor_scalar(TOP[:, 0, :], TOP[:, 0, :], P + 0.5, None, ALU.is_gt))
            dve.tensor_copy(overflow[:, :], TOP[:, 0, :])
            for t in range(2):
                for d in range(2):
                    await_next(dve, "h_turned")
                    dve.tensor_copy(h_tok[:, t, d * 512:(d + 1) * 512], bank[4 + 2 * t + d][:, :])
            phase_end(dve)

        def act_router(act):
            await_next(act, "logits_below_max")
            act.activation(EX[:, :, :], EX[:, :, :], ACT.Exp).then_inc(sem("logits_exp"), 1)
            phase_end(act)

        def pe_router(pe):
            for t in range(2):
                for k in range(KT):
                    out = bank[4 + 2 * t + k // 4][:, (k % 4) * P:(k % 4 + 1) * P]
                    for part in range(2):
                        mm(pe, out, h(part, k, t * P, (t + 1) * P).bitcast(F32), const("ident"), start=part == 0,
                           stop=part == 1, last_of="h_turned" if part == 1 and k % 4 == 3 else None)
            await_next(pe, "choices")
            mm(pe, bank[0][:, 0:N_EXP], const("tri"), RK[:, 0, :], start=True, stop=True)
            for b, last in ((1, "tri"), (2, "ones")):
                mm(pe, bank[b][:, 0:N_EXP], const("ones"), RK[:, 0, :], start=True, stop=False)
                mm(pe, bank[b][:, 0:N_EXP], const(last), RK[:, 1, :], start=False, stop=True,
                   last_of="choice_counts" if b == 2 else None)
            phase_end(pe)

        PAIRS = FT // 2

        def pe_scatter(pe, pre, s, i):
            pe.wait_ge(sem(pre + "_y_copied"), s * 2 + 2)
            for b in range(4):
                if b >= 2:
                    pe.wait_ge(sem(pre + "_x_added"), s * 4 + b - 1)
                for c in range(2):
                    d = 2 * b + c
                    mm(pe, bank[6 + b % 2][:, c * T:(c + 1) * T], y_e[:, d * P:(d + 1) * P], place_w[1 - i],
                       start=True, stop=True, last_of=pre + "_scattered" if c == 1 else None)

        def dve_add_scattered(dve, pre, s):
            for b in range(4):
                dve.wait_ge(sem(pre + "_scattered"), s * 4 + b + 1)
                x = xT[:, 2 * b:2 * b + 2, 0:T]
                dve.tensor_tensor(x, x, bank[6 + b % 2].rearrange("p (c n) -> p c n", c=2), ALU.add)\
                   .then_inc(sem(pre + "_x_added"), 1)

        def pe_gather(pe, pre, r):
            pe.wait_ge(sem(pre + "_selected"), r + 1)
            for k in range(KT):
                for t in range(2):
                    mm(pe, bank[6 + k // 4][:, (k % 4) * P:(k % 4 + 1) * P], h_tok[:, t, k * P:(k + 1) * P],
                       select[:, t, :], start=t == 0, stop=t == 1,
                       last_of=pre + "_gathered" if k == KT - 1 and t == 1 else None)
            for t in range(2):
                ins = pe.transpose(bank[3][:, t * P:(t + 1) * P], select_w[:, t, :], const("ident"))
            ins.then_inc(sem(pre + "_gates_turned"), 1)

        def act_gather(act, pre, r, i):
            act.wait_ge(sem(pre + "_gathered"), r + 1)
            act.activation(g_part[0], psum[:, 6:8, :].rearrange("p a b -> p (a b)"), ACT.Copy)\
               .then_inc(sem(pre + "_slots_rounded"), 1)
            act.wait_ge(sem(pre + "_gates_turned"), r + 1)
            act.activation(place_w[i], bank[3][:, 0:T], ACT.Copy).then_inc(sem(pre + "_gates_placed"), 1)

        def dve_select(dve, pre, r, e):
            for t in range(2):
                pos = POS[:, t, e]
                dve.tensor_scalar(select[:, t, :], const("iota"), pos, None, ALU.is_equal)
                ins = dve.tensor_scalar(select_w[:, t, :], const("iota"), pos, GT[:, t, e],
                                        ALU.is_equal, ALU.mult)
            ins.then_inc(sem(pre + "_selected"), 1)

        def dve_gather(dve, pre, r):
            dve.wait_ge(sem(pre + "_slots_rounded"), r + 1)
            dve.tensor_tensor(g_part[1], psum[:, 6:8, :].rearrange("p a b -> p (a b)"), g_part[0].bitcast(F32),
                              ALU.subtract).then_inc(sem(pre + "_slots_split"), 1)

        def pe_expert(pe, pre, r, i, it):
            def turn(j):
                pe.wait_ge(sem(pre + "_full"), r * PAIRS + j + 1)
                if j >= 2:
                    pe.wait_ge(sem(pre + "_hidden"), r * PAIRS + j - 1)
                if j == 1:
                    pe.wait_ge(sem(pre + "_gates_placed"), r + 1)
                for c in range(2):
                    ins = pe.transpose(bank[2 + j % 2][:, c * P:(c + 1) * P], hid_tok[j % 2][:, c * P:(c + 1) * P],
                                       const("ident"))
                ins.then_inc(sem(pre + "_turned"), 1)

            pe.wait_ge(sem(pre + "_slots_split"), r + 1)
            for j in range(PAIRS):
                if j >= 2:
                    pe.wait_ge(sem(pre + "_full"), r * PAIRS + j - 1)
                for c in range(2):
                    w = piece_slot(pe, it=it)
                    for k in range(KT):
                        for m, (wp, ap) in enumerate(THREE):
                            last = k == KT - 1 and m == 2
                            mm(pe, bank[j % 2][:, c * 256:(c + 1) * 256], g_part[ap][:, k * P:(k + 1) * P],
                               w[wp][:, k * 256:(k + 1) * 256], start=k == 0 and m == 0, stop=last,
                               last_of=pre + "_up" if last and c else None)
                    stream["release"] = True
                if j >= 1:
                    turn(j - 1)
                if j == 2:
                    pe_scatter(pe, pre, r, i)
            turn(PAIRS - 1)
            for q in range(2 * FT):
                half, f = divmod(q, FT)
                if q % 4 == 0:
                    w = piece_slot(pe, it=it)
                if half == 0 and f % 2 == 0:
                    pe.wait_ge(sem(pre + "_hidden"), r * PAIRS + f // 2 + 1)
                if f == 0:
                    pe.wait_ge(sem(pre + "_y_copied"), r * 2 + half + 1)
                for m, (wp, ap) in enumerate(THREE):
                    last = f == FT - 1 and m == 2
                    mm(pe, bank[4 + half], hid_e(f, ap), w[wp][:, (q % 4) * 512:(q % 4 + 1) * 512],
                       start=f == 0 and m == 0, stop=last, last_of=pre + "_down" if last else None)
                if q % 4 == 3:
                    stream["release"] = True
                if q == FT + 1:
                    pe.wait_ge(sem(pre + "_x_added"), r * 4 + 4)
                    pe_gather(pe, pre, r + 1)

        def act_expert(act, pre, r, i, it):
            for j in range(PAIRS + 1):
                if j < PAIRS:
                    split_ahead(act, "act", 2, it=it)
                    act.wait_ge(sem(pre + "_up"), r * PAIRS + j + 1)
                    if j >= 2:
                        act.wait_ge(sem(pre + "_full"), r * PAIRS + j - 1)
                    act.activation(silu_b[j % 2].rearrange("p (c n) -> p c n", c=2),
                                   bank[j % 2].rearrange("p (c n) -> p c n", c=2)[:, :, 0:P], ACT.Silu)\
                       .then_inc(sem(pre + "_silu"), 1)
                if j >= 1:
                    act.wait_ge(sem(pre + "_turned"), r * PAIRS + j)
                    out = Zr[:, (j - 1) * 4 * P:j * 4 * P].rearrange("p (c u n) -> p c u n", c=2, u=2)[:, :, 0, :]
                    act.activation(out, bank[2 + (j - 1) % 2][:, 0:T].rearrange("p (c n) -> p c n", c=2), ACT.Copy)\
                       .then_inc(sem(pre + "_rounded"), 1)
            for j in range(PAIRS):
                split_ahead(act, "act", it=it)
                if j == PAIRS // 2 + 1:
                    act.wait_ge(sem(pre + "_down"), r * 2 + 1)
                    act.activation(y_e[:, 0:512], bank[4], ACT.Copy).then_inc(sem(pre + "_y_copied"), 1)
                    act_gather(act, pre, r + 1, 1 - i)
            act.wait_ge(sem(pre + "_down"), r * 2 + 2)
            act.activation(y_e[:, 512:1024], bank[5], ACT.Copy).then_inc(sem(pre + "_y_copied"), 1)

        def dve_expert(dve, pre, r, i, it, following):
            for j in range(PAIRS + 1):
                if j < PAIRS:
                    split_ahead(dve, "dve", 2, it=it)
                    dve.wait_ge(sem(pre + "_silu"), r * PAIRS + j + 1)
                    if j >= 2:
                        dve.wait_ge(sem(pre + "_turned"), r * PAIRS + j - 1)
                    dve.tensor_tensor(hid_tok[j % 2].rearrange("p (c n) -> p c n", c=2),
                                      silu_b[j % 2].rearrange("p (c n) -> p c n", c=2),
                                      bank[j % 2].rearrange("p (c n) -> p c n", c=2)[:, :, P:2 * P], ALU.mult)\
                       .then_inc(sem(pre + "_full"), 1)
                if j >= 1:
                    dve.wait_ge(sem(pre + "_rounded"), r * PAIRS + j)
                    parts = Zr[:, (j - 1) * 4 * P:j * 4 * P].rearrange("p (c u n) -> p c u n", c=2, u=2)
                    dve.tensor_tensor(parts[:, :, 1, :], bank[2 + (j - 1) % 2][:, 0:T].rearrange("p (c n) -> p c n", c=2),
                                      parts[:, :, 0, :].bitcast(F32), ALU.subtract).then_inc(sem(pre + "_hidden"), 1)
                if j == 2:
                    dve_add_scattered(dve, pre, r)
            for j in range(PAIRS):
                split_ahead(dve, "dve", it=it)
                if j == 0:
                    dve_select(dve, pre, r + 1, following)
                if j == PAIRS // 2 + 1:
                    dve_gather(dve, pre, r + 1)

        def pe_experts(pe, pre, first):
            n0 = stream["n"]
            pe_gather(pe, pre, 0)
            release_now(pe)
            with pe.Fori(0, N_EXP // 2, 1) as e:
                for i in range(2):
                    pe_expert(pe, pre, e * 2 + i, i, e + first)
                release_now(pe)
            pe_scatter(pe, pre, N_EXP, 0)
            stream["n"] = n0

        def act_experts(act, pre, first):
            n0 = splits["act"]
            for _ in range(2):
                act.nop().then_inc(sem(pre + "_y_copied"), 1)
            act_gather(act, pre, 0, 0)
            with act.Fori(0, N_EXP // 2, 1) as e:
                for i in range(2):
                    act_expert(act, pre, e * 2 + i, i, e + first)
            splits["act"] = n0

        def dve_experts(dve, pre, first):
            n0 = splits["dve"]
            dve_select(dve, pre, 0, slice(0, 1))
            dve_gather(dve, pre, 0)
            with dve.Fori(0, N_EXP // 2, 1) as e:
                for i in range(2):
                    dve_expert(dve, pre, e * 2 + i, i, e + first, bass.ds(e * 2 + i + 1, 1))
            dve_add_scattered(dve, pre, N_EXP)
            splits["dve"] = n0

        def release_now(pe):
            if stream["release"]:
                pe.drain().then_inc(sem("piece_used"), 1)
                stream["release"] = False

        X_ONLY = T
        b2_seg = lambda name, layer: [(0, T, (lambda k: v(name, layer, k, k + 1)), None)]
        mem_seg = lambda layer: b2_seg("norm_x", layer) + [(T, 2 * T, (lambda k: v("norm_mem", layer, k, k + 1)), None)]
        one = lambda q, s: 1.0

        def gate_gain(which):
            return lambda d, s: modT[:, 16 + 24 * which + d, s:s + 1]

        block = ctx.enter_context(nc.Block())

        @block.sync
        def _(sp):
            for name, dst in (("xT", xT[:, :, 0:T]), ("ctxT", xT[:, :, T:2 * T]), ("vectors", vec[:, :]),
                              ("constants", cst[:, :]), ("level_masks", Z[:, 0:2 * LEVELS * P]),
                              ("gate_w", gate_w[:, :, :, :])):
                sp.dma_start(dst, A[name]).then_inc(sem("vectors_in"), 16)

            def load(n, s):
                src = A["stream"][n] if isinstance(n, int) else A["stream"][bass.ds(n, 1)].rearrange("o p c -> (o p) c")
                sp.dma_start(ring[:, s, :], src).then_inc(sem(f"piece_in_{s}"), 16)

            for s in range(SLOTS):
                load(s, s)
            rounds = n_pieces // SLOTS
            with sp.Fori(1, rounds, 1) as r:
                for s in range(SLOTS):
                    sp.wait_ge(sem("piece_used"), (r - 1) * SLOTS + s + 1)
                    load(r * SLOTS + s, s)
            for s in range(n_pieces % SLOTS):
                sp.wait_ge(sem("piece_used"), (rounds - 1) * SLOTS + s + 1)
                load(rounds * SLOTS + s, s)
            sp.wait_ge(sem("phase_dve"), EXPERT_PHASES)
            with sp.If(sp.value_load(overflow[0:1, 0:1], min_val=0, max_val=1) > 0):
                again = N_EXP * FFN_PIECES
                with sp.Fori(0, again // SLOTS, 1) as r:
                    for s in range(SLOTS):
                        sp.wait_ge(sem("piece_used"), n_pieces + r * SLOTS + s - SLOTS + 1)
                        load(r * SLOTS + (n_pieces + s - again), (n_pieces + s) % SLOTS)
            sp.nop()
            sp.wait_ge(sem("y_ready"), 1)
            sp.dma_start(y_out, hT[:, :, 0:T]).then_inc(sem("y_stored"), 16)
            sp.wait_ge(sem("y_stored"), 16)

        @block.tensor
        def _(pe):
            for layer in range(DEPTH):
                n = 2 * T if layer == 0 else T
                pe_mod(pe, layer)
                pe_norm(pe, 0, 2 * T)
                pe_products(pe, b1_groups(layer), "h_split")
                phase_end(pe)
                pe_rope(pe, layer)
                pe_attention(pe, b1_units(layer))
                phase_end(pe)
                pe_gla_gates(pe, layer)
                pe_gla_levels(pe, layer)
                pe_gla_out(pe, layer)
                pe_gla_norm(pe, layer)
                pe_products(pe, out_groups(KT, n, gate_gain(0), 2), "mix_split", "dve")
                phase_end(pe)
                pe_norm(pe, 0, n)
                pe_ffn(pe, 2 * layer, first=True)
                if layer == 0:
                    pe_ffn(pe, 1, T)
                phase_end(pe)
            pe_norm(pe, 0, T)
            phase_end(pe)
            phase_end(pe)
            for layer in range(DEPTH):
                pe_norm(pe, 0, T)
                pe_products(pe, b2_groups(layer), "h_split")
                phase_end(pe)
                pe_b2_conv(pe, layer)
                pe_b2_ln(pe, layer)
                phase_end(pe)
                pe_attention(pe, mlstm_units())
                phase_end(pe)
                pe_m_norm(pe, layer)
                for part in range(2):
                    phase_end(pe)
                    pe_attention(pe, fox_units(part))
                    phase_end(pe)
                pe_products(pe, out_groups(KT, T, one, 2), "mix_split", "dve")
                phase_end(pe)
                pe_norm(pe, 0, 2 * T)
                pe_products(pe, x_groups(layer), "h_split")
                phase_end(pe)
                pe_attention(pe, x_units())
                phase_end(pe)
                pe_products(pe, out_groups(4, T, one, 4), "mix_split", "dve")
                phase_end(pe)
                pe_norm(pe, 0, T)
                if layer == 0:
                    pe_ffn(pe, 3, first=True)
                    phase_end(pe)
                else:
                    pe_products(pe, router_groups(), "h_split")
                    phase_end(pe)
                    pe_router(pe)
                    pe_experts(pe, "e", 0)
                    phase_end(pe)
                    with pe.If(pe.value_load(overflow[0:1, 0:1], min_val=0, max_val=1) > 0):
                        pe_experts(pe, "o", N_EXP // 2)
                    pe.nop()
                    phase_end(pe)
            pe_norm(pe, 0, T)

        @block.scalar
        def _(act):
            for layer in range(DEPTH):
                n = 2 * T if layer == 0 else T
                act_mod(act, layer)
                act_norm(act, 0, 2 * T, b1_segments(0, 2 * T))
                take_products(act, "act", b1_groups(layer))
                phase_end(act)
                act_rope(act, layer)
                act_attention(act, b1_units(layer))
                phase_end(act)
                act_gla_gates(act, layer)
                act_gla_levels(act, layer)
                act_gla_out(act, layer)
                act_gla_norm(act, layer)
                act_split_mix(act, KT, n)
                take_products(act, "act", out_groups(KT, n, gate_gain(0), 2), "dve")
                phase_end(act)
                act_norm(act, 0, n, b1_segments(1, n))
                act_ffn(act, 2 * layer)
                if layer == 0:
                    act_ffn(act, 1)
                phase_end(act)
            act_norm(act, 0, T, [(0, T, None, None)], split=False)
            phase_end(act)
            phase_end(act)
            for layer in range(DEPTH):
                act_norm(act, 0, T, b2_seg("norm_mix", layer))
                take_products(act, "act", b2_groups(layer))
                phase_end(act)
                act_b2_conv(act, layer)
                act_b2_ln(act, layer)
                phase_end(act)
                act_attention(act, mlstm_units())
                phase_end(act)
                act_m_norm(act, layer)
                for part in range(2):
                    phase_end(act)
                    act_attention(act, fox_units(part))
                    phase_end(act)
                act_split_mix(act, KT, T)
                take_products(act, "act", out_groups(KT, T, one, 2), "dve")
                phase_end(act)
                act_norm(act, 0, 2 * T, mem_seg(layer))
                take_products(act, "act", x_groups(layer))
                phase_end(act)
                act_attention(act, x_units())
                phase_end(act)
                act_split_mix(act, 4, T)
                take_products(act, "act", out_groups(4, T, one, 4), "dve")
                phase_end(act)
                act_norm(act, 0, T, b2_seg("norm_ffn", layer))
                if layer == 0:
                    act_ffn(act, 3)
                    phase_end(act)
                else:
                    take_products(act, "act", router_groups())
                    phase_end(act)
                    act_router(act)
                    act_experts(act, "e", 0)
                    phase_end(act)
                    with act.If(act.value_load(overflow[0:1, 0:1], min_val=0, max_val=1) > 0):
                        act_experts(act, "o", N_EXP // 2)
                    act.nop()
                    phase_end(act)
            act_norm(act, 0, T, [(0, T, None, None)], split=False)

        @block.vector
        def _(dve):
            for layer in range(DEPTH):
                n = 2 * T if layer == 0 else T
                dve_mod(dve, layer)
                dve_norm(dve, 0, 2 * T, b1_segments(0, 2 * T))
                take_products(dve, "dve", b1_groups(layer))
                phase_end(dve)
                dve_rope_conv(dve, layer)
                dve_attention(dve, b1_units(layer))
                phase_end(dve)
                dve_gla_gates(dve, layer)
                dve_gla_levels(dve, layer)
                dve_gla_out(dve, layer)
                dve_gla_norm(dve, layer)
                dve_split_mix(dve, KT, n)
                take_products(dve, "dve", out_groups(KT, n, gate_gain(0), 2), "dve")
                phase_end(dve)
                dve_norm(dve, 0, n, b1_segments(1, n))
                dve_ffn(dve, 2 * layer, 0, lambda q: gate_gain(1)(q, 0))
                if layer == 0:
                    dve_ffn(dve, 1, T, lambda q: gate_gain(1)(q, 1))
                phase_end(dve)
            dve_norm(dve, 0, T, [(0, T, (lambda k: v("final1", 0, k, k + 1)), None)], split=False)
            phase_end(dve)
            dve.wait_ge(sem("mem_in"), 16)
            for k in range(KT):
                dve.tensor_copy(xT[:, k, 0:T], hT[:, k, 0:T])
            phase_end(dve)
            for layer in range(DEPTH):
                dve_norm(dve, 0, T, b2_seg("norm_mix", layer))
                take_products(dve, "dve", b2_groups(layer))
                phase_end(dve)
                dve_b2_conv(dve, layer)
                dve_b2_ln(dve, layer)
                dve_decay_columns(dve, 4, 0)
                dve_attention(dve, mlstm_units())
                phase_end(dve)
                dve_m_norm(dve, layer)
                for part in range(2):
                    dve_decay_columns(dve, 8 + 4 * part, None)
                    dve_attention(dve, fox_units(part))
                    phase_end(dve)
                dve_split_mix(dve, KT, T)
                take_products(dve, "dve", out_groups(KT, T, one, 2), "dve")
                phase_end(dve)
                dve_norm(dve, 0, 2 * T, mem_seg(layer))
                take_products(dve, "dve", x_groups(layer))
                phase_end(dve)
                dve_attention(dve, x_units())
                phase_end(dve)
                dve_split_mix(dve, 4, T)
                take_products(dve, "dve", out_groups(4, T, one, 4), "dve")
                phase_end(dve)
                dve_norm(dve, 0, T, b2_seg("norm_ffn", layer))
                if layer == 0:
                    dve_ffn(dve, 3, 0, lambda q: 1.0)
                    phase_end(dve)
                else:
                    take_products(dve, "dve", router_groups())
                    phase_end(dve)
                    dve_router(dve)
                    dve_experts(dve, "e", 0)
                    phase_end(dve)
                    with dve.If(dve.value_load(overflow[0:1, 0:1], min_val=0, max_val=1) > 0):
                        link(dve, dve.tensor_scalar(POS[:, :, :], POS[:, :, :], -float(P), None, ALU.add))
                        dve.memset(place_w[1], 0.0)
                        dve_experts(dve, "o", N_EXP // 2)
                    dve.nop()
                    phase_end(dve)
            dve_norm(dve, 0, T, [(0, T, (lambda k: v("final2", 0, k, k + 1)), None)], split=False)
            dve.drain().then_inc(sem("y_ready"), 1)

        @block.gpsimd
        def _(pool):
            for other in ("pe", "act", "dve"):
                pool.wait_ge(sem(f"phase_{other}"), B1_PHASES)
            pool.dma_start(xT[:, :, T:2 * T], A["memT"]).then_inc(sem("mem_in"), 16)


N_LOADS = 6
EXPERT_PHASES = 53
B1_PHASES = 20


def constants():
    r = np.arange(P)
    c = {}
    c["ident"] = np.eye(P)
    c["mean"] = np.full((P, P), 1.0 / D)
    c["head_mean"] = (r[:, None] // HD == r[None, :] // HD) / HD
    c["tri"] = r[:, None] <= r[None, :]
    c["tri_r"] = r[:, None] >= r[None, :]
    c["ones"] = np.ones((P, P))
    c["strict"] = r[:, None] > r[None, :]
    c["pair"] = (r[:, None] % 2 == np.arange(2)[None, :]) & (r[:, None] < 4)
    c["iota"] = np.tile(r, (P, 1))
    rot = np.zeros((P, P))
    for m in range(P):
        if m % 32 < 16:
            rot[m + 16, m] = -1.0
        else:
            rot[m - 16, m] = 1.0
    c["rot"] = rot
    zero = np.zeros((P, P))
    after = np.where(r[None, :] >= r[:, None], 0.0, NEG)
    upto = np.where(r[None, :] <= r[:, None], 0.0, NEG)
    c["masks"] = np.concatenate([after, zero, zero, zero, upto, zero, zero], 1)
    inv = np.float32(10000.0) ** (-np.arange(16, dtype=np.float32) / np.float32(16))
    t = np.arange(T)
    pos = np.stack([t // 64, t % 64]).astype(np.float32)
    ch = r % HD
    ang = pos[ch // 32] * inv[ch % 16][:, None]
    c["cos"], c["sin"] = np.cos(ang), np.sin(ang)
    out = np.zeros((P, N_CONST), np.float32)
    for name, (a, b) in CONST.items():
        out[:, a:b] = c[name]
    lv = np.zeros((P, 2 * LEVELS, P), np.float32)
    s, q = r[:, None], r[None, :]
    for l in range(LEVELS):
        same = (s >> (l + 1)) == (q >> (l + 1))
        up_s, up_q = (s >> l) & 1, (q >> l) & 1
        lv[:, 2 * l] = same & (up_s == 0) & (up_q == 1)
        lv[:, 2 * l + 1] = same & (up_s == 1) & (up_q == 0)
    return out, lv.reshape(P, -1)


def by_columns(w, width=256):
    k, n = w.shape
    return w.reshape(k // P, P, n // width, width).transpose(2, 1, 0, 3).reshape(-1, P, PIECE)


def ffn_pieces(gate, up, down):
    g = gate.reshape(KT, P, FT, P).transpose(2, 1, 0, 3)
    u = up.reshape(KT, P, FT, P).transpose(2, 1, 0, 3)
    d = down.reshape(FT, P, 2, 512).transpose(2, 0, 1, 3).reshape(2 * FT // 4, 4, P, 512).transpose(0, 2, 1, 3)
    return [np.concatenate([g, u], 3).reshape(FT, P, PIECE), d.reshape(-1, P, PIECE)]


def columns(x, tile=P):
    x = np.asarray(x)
    return x.reshape(-1, P).T


def rows(x):
    x = np.asarray(x).reshape(1, -1)
    return np.broadcast_to(x, (P, x.shape[1]))


def kernel(**inputs):
    import concourse.bacc as bacc
    from concourse.bass_utils import run_bass_kernel_spmd

    i = {k: np.asarray(a) for k, a in inputs.items()}
    pieces = []
    heads = np.array([64 * h + k for t in range(4) for h in (t, t + 4) for k in range(64)])
    for l in range(DEPTH):
        w = i["w_in"][l]
        none = np.zeros((D, 112), np.float32)
        w = np.concatenate([w[:, 0:768], w[:, 768:1280][:, heads], w[:, 1280:2576], none, w[:, 2576:2592], none], 1)
        pieces += [by_columns(i["w_mod"][l]), by_columns(w), by_columns(i["w_out"][l])]
        for _ in range(2 if l == 0 else 1):
            pieces += ffn_pieces(i["w_up"][l][:, 0:FF], i["w_up"][l][:, FF:2 * FF], i["w_down"][l])
    for l in range(DEPTH):
        w = i["w_in_2"][l]
        w = np.concatenate([w[:, 0:1024], w[:, 1032:3080], w[:, 1024:1032], w[:, 3080:3088],
                            np.zeros((D, 240), np.float32)], 1)
        pieces += [by_columns(w), by_columns(i["w_out_2"][l]), by_columns(i["xattn_w_q_2"][l]),
                   by_columns(i["xattn_w_kv_2"][l]), by_columns(i["xattn_w_o_2"][l], 512)]
        if l == 0:
            pieces += ffn_pieces(i["ffn_w_gate_2"][0], i["ffn_w_up_2"][0], i["ffn_w_down_2"][0])
        else:
            pieces.append(by_columns(np.concatenate([i["router_w_2"][0], np.zeros((D, 248), np.float32)], 1)))
            for e in range(N_EXP):
                pieces += ffn_pieces(i["moe_w_gate_2"][0, e], i["moe_w_up_2"][0, e], i["moe_w_down_2"][0, e])

    pieces.append(ffn_pieces(i["moe_w_gate_2"][0, 0], i["moe_w_up_2"][0, 0], i["moe_w_down_2"][0, 0])[0][0:AHEAD])
    vec = np.zeros((P, N_VEC), np.float32)

    def put(name, layer, cols):
        a, b = VEC[name, layer]
        vec[:, a:b] = cols

    for l in range(DEPTH):
        put("b_mod", l, columns(i["b_mod"][l]))
        put("norm1", l, columns(i["norm1_g"][l]))
        put("norm2", l, columns(i["norm2_g"][l]))
        put("conv_w", l, columns(i["conv_w"][l]))
        put("sink", l, rows(i["attn_sink"][l]))
        put("gla_g", l, columns(np.concatenate([i["gla_norm_g"][l], i["gla_norm_g"][l]])))
        put("norm_mix", l, columns(i["norm_mix_w_2"][l]))
        put("m_conv_w", l, columns(i["mlstm_conv_w_2"][l]))
        put("m_conv_b", l, columns(i["mlstm_conv_b_2"][l]))
        put("gate_b", l, rows(np.concatenate([i["mlstm_b_i_2"][l], i["mlstm_b_f_2"][l], i["fox_b_f_2"][l]])))
        put("m_norm", l, columns(i["mlstm_norm_w_2"][l]))
        put("c_conv_w", l, columns(i["conf_conv_w_2"][l]))
        put("c_conv_b", l, columns(i["conf_conv_b_2"][l]))
        put("ln_w", l, columns(i["conf_ln_w_2"][l]))
        put("ln_b", l, columns(i["conf_ln_b_2"][l]))
        put("norm_x", l, columns(i["norm_xattn_w_2"][l]))
        put("norm_mem", l, columns(i["norm_mem_w_2"][l]))
        put("norm_ffn", l, columns(i["norm_ffn_w_2"][l]))
    put("final1", 0, columns(i["final_norm_g"]))
    put("final2", 0, columns(i["norm_final_w_2"]))
    put("c", 0, np.stack([columns(i["c"][0]), columns(i["c_ctx"])], 2).reshape(P, 16))

    gate_w = np.zeros((17, DEPTH, 2, 256), np.float32)
    gate_w[0:16] = i["gla_gate_w"].transpose(2, 0, 1, 3)
    gate_w[16] = i["gla_gate_b"]
    consts, level_masks = constants()

    def turned(x):
        return np.ascontiguousarray(x.T.reshape(KT, P, T).transpose(1, 0, 2))

    arrays = dict(
        stream=np.concatenate(pieces, 0), xT=turned(i["x"][0]), ctxT=turned(i["ctx"][0]), memT=turned(i["mem_2"][0]),
        vectors=vec, constants=consts, level_masks=level_masks, gate_w=gate_w)
    nc = bacc.Bacc("TRN2", target_bir_lowering=False, num_devices=1)
    A = {}
    for name, a in arrays.items():
        A[name] = nc.dram_tensor(f"in_{name}", a.shape, mybir.dt.from_np(a.dtype), kind="ExternalInput").ap()
    y = nc.dram_tensor("out_y", (P, KT, T), F32, kind="ExternalOutput").ap()
    build(nc, A, y)
    r = run_bass_kernel_spmd(nc, [{f"in_{k}": a for k, a in arrays.items()}], core_ids=[0])
    got = r.results[0]["out_y"]
    return np.ascontiguousarray(got.transpose(1, 0, 2).reshape(D, T).T).reshape(1, T, D)
```

```python
from contextlib import ExitStack

import numpy as np

import concourse.bass as bass
from concourse import mybir

F32 = mybir.dt.float32
F32R = mybir.dt.float32r
U8 = mybir.dt.uint8
ALU = mybir.AluOpType
ACT = mybir.ActivationFunctionType
AX = mybir.AxisListType

P = 128
D = 1024
KT = D // P
T = 256
TT = T // P
EPS = 1e-6
DEPTH = 2
FF = 2816
FT = FF // P
HD = 64
N_EXP = 8
PIECE = 2048
SLOTS = 6
SPLITS = 3
AHEAD = 2
FFN_PIECES = FT + 2 * FT // 4
MOD_PIECES = 6 * D // 256
EARLY = 8
NEG = -1.0e30

B1_COLS = dict(b_mod=48, norm1=8, norm2=8, conv_w=6, sink=8, gla_g=1)
B2_COLS = dict(norm_mix=8, m_conv_w=16, m_conv_b=4, gate_b=16, m_norm=2, c_conv_w=62, c_conv_b=2,
               ln_w=2, ln_b=2, norm_x=8, norm_mem=8, norm_ffn=8)


def vector_columns():
    at, n = {}, 0
    for layer in range(DEPTH):
        for name, width in B1_COLS.items():
            at[name, layer] = (n, n + width)
            n += width
    for layer in range(DEPTH):
        for name, width in B2_COLS.items():
            at[name, layer] = (n, n + width)
            n += width
    for name, width in dict(final1=8, final2=8, c=16).items():
        at[name, 0] = (n, n + width)
        n += width
    return at, n


VEC, N_VEC = vector_columns()

CONST = {}
N_CONST = 0
for _name, _w in (("ident", P), ("mean", P), ("head_mean", P), ("tri", P), ("tri_r", P), ("ones", P),
                  ("strict", P), ("rot", P), ("pair", 2), ("iota", P), ("masks", 7 * P), ("cos", T), ("sin", T)):
    CONST[_name] = (N_CONST, N_CONST + _w)
    N_CONST += _w
LEVELS = 7


def build(nc, A, y_out):
    with ExitStack() as ctx:
        place = {"at": -(-nc.sbuf_base // 32) * 32}

        def sb(name, shape, dt=F32, over=None):
            n = int(np.prod(shape[1:])) * (1 if dt == U8 else 4)
            at = place[over] if over else place["at"]
            if not over:
                place[name] = at
                place["at"] += -(-n // 32) * 32
            return nc.alloc_sbuf_tensor_at(name, shape, dt, offset=at)

        xT = sb("xT", [P, KT, 2 * T])
        hT = sb("hT", [P, KT, 2 * T])
        h_lo = sb("h_lo", [P, KT, 2 * T], F32R, over="hT")
        mixT = sb("mixT", [P, KT, 2 * T])
        mix_lo = sb("mix_lo", [P, KT, 2 * T], F32R, over="mixT")
        a_hi = sb("a_hi", [P, KT, 2 * T], F32R)
        Z = sb("Z", [P, FT * 2 * T])
        Zr = sb("Zr", [P, FT * 2 * T], F32R, over="Z")
        tok = sb("tok", [P, 4 * 384])
        ring = sb("ring", [P, SLOTS, PIECE])
        ring_lo = sb("ring_lo", [P, SLOTS, PIECE], F32R, over="ring")
        ring_hi = sb("ring_hi", [P, SPLITS, PIECE], F32R)
        cst = sb("cst", [P, N_CONST])
        vec = sb("vec", [P, N_VEC])
        lvl_mask = sb("lvl_mask", [P, 2 * LEVELS, P], U8)
        gate_w = sb("gate_w", [17, DEPTH, 2, 256])
        modT = sb("modT", [P, DEPTH, 48, 2])
        a1 = sb("a1", [P, DEPTH, 2, KT, 2])
        c_mat = sb("c_mat", [P, KT, 4], F32R)
        mod_rows = sb("mod_rows", [4, 2, 256])
        sc = sb("sc", [P, 96])
        overflow = sb("overflow", [P, 1], mybir.dt.int32)
        assert place["at"] <= nc.sbuf_usable_end
        psum = ctx.enter_context(nc.psum_tensor("psum", [P, 8, 512], F32))
        bank = [psum[:, i, :] for i in range(8)]
        Zt = Z[:, :].rearrange("p (f n) -> p f n", n=2 * T)
        hflat = hT[:, :, :].rearrange("p a b -> p (a b)")
        mixflat = mixT[:, :, :].rearrange("p a b -> p (a b)")

        def const(name, lo=0, hi=None):
            a, b = CONST[name]
            return cst[:, a + lo:(b if hi is None else a + hi)]

        def v(name, layer=0, lo=0, hi=None):
            a, b = VEC[name, layer]
            return vec[:, a + lo:(b if hi is None else a + hi)]

        sems, seen = {}, {}

        def sem(name):
            if name not in sems:
                sems[name] = ctx.enter_context(nc.semaphore(name))
            return sems[name]

        def await_next(e, name, n=1):
            k = seen[e.engine, name] = seen.get((e.engine, name), 0) + n
            e.wait_ge(sem(name), k)

        def base(e, name):
            return seen.get((e.engine, name), 0)

        def advance(e, name, n):
            seen[e.engine, name] = base(e, name) + n

        def link(e, ins):
            name = f"own_{str(e.engine).split('.')[-1]}"
            ins.then_inc(sem(name), 1)
            await_next(e, name)

        def phase_end(e):
            me = {nc.tensor.engine: "pe", nc.scalar.engine: "act", nc.vector.engine: "dve"}[e.engine]
            e.drain().then_inc(sem(f"phase_{me}"), 1)
            for other in ("pe", "act", "dve"):
                if other != me:
                    await_next(e, f"phase_{other}")

        n_pieces = A["stream"].shape[0]
        stream = {"n": 0, "release": False}
        splits = {}
        LOOP = 2 * FFN_PIECES

        def piece_slot(pe, it=0):
            n = stream["n"]
            stream["n"] += 1
            pe.wait_ge(sem("piece_split"), n + 1 + it * LOOP)
            return ring_hi[:, n % SPLITS, :], ring_lo[:, n % SLOTS, :]

        def split_ahead(e, who, more=1, it=0):
            more += 0 if who in splits else AHEAD
            for n in range(splits.get(who, 0), splits.get(who, 0) + more):
                raw, hi, lo = ring[:, n % SLOTS, :], ring_hi[:, n % SPLITS, :], ring_lo[:, n % SLOTS, :]
                if who == "act":
                    e.wait_ge(sem(f"piece_in_{n % SLOTS}"), 16 * (n // SLOTS + 1) + it * (16 * LOOP // SLOTS))
                    if n >= SPLITS:
                        e.wait_ge(sem("piece_used"), n - SPLITS + 1 + it * LOOP)
                    e.activation(hi, raw, ACT.Copy).then_inc(sem("piece_rounded"), 1)
                else:
                    e.wait_ge(sem("piece_rounded"), n + 1 + it * LOOP)
                    e.tensor_tensor(lo, raw, hi.bitcast(F32), ALU.subtract).then_inc(sem("piece_split"), 1)
            splits[who] = splits.get(who, 0) + more

        def mm(pe, *args, last_of=None, **kw):
            ins = pe.matmul(*args, **kw)
            if last_of:
                ins.then_inc(sem(last_of), 1)
            elif stream["release"]:
                ins.then_inc(sem("piece_used"), 1)
                stream["release"] = False
            return ins

        def whose(g, who):
            if isinstance(who, list):
                return who[g]
            return who or ("act" if g % 2 == 0 else "dve")

        def pe_products(pe, groups, ready, who=None, between=lambda g: None):
            counts = {"act": base(pe, "product_out_act"), "dve": base(pe, "product_out_dve")}
            ends = []
            for g, (terms, rows_, n, _, held) in enumerate(groups):
                if g >= 4:
                    w, k = ends[g - 4]
                    pe.wait_ge(sem(f"product_out_{w}"), k)
                if held == "new":
                    hi, lo = piece_slot(pe)
                for k, (stationary, moving) in enumerate(terms):
                    if g == 0:
                        await_next(pe, ready)
                    for i, (w, a) in enumerate(((hi, 0), (hi, 1), (lo, 0))):
                        last = k == len(terms) - 1 and i == 2
                        mm(pe, bank[g % 4][:, 0:n], stationary(w, a), moving(w, a), start=k == 0 and i == 0, stop=last,
                           last_of=f"product_in_{whose(g, who)}" if last else None)
                if g + 1 == len(groups) or groups[g + 1][4] == "new":
                    stream["release"] = True
                w = whose(g, who)
                counts[w] += 1
                ends.append((w, counts[w]))
                between(g)
            for w, k in counts.items():
                seen[pe.engine, f"product_out_{w}"] = k

        def take_products(e, me, groups, who=None, between=lambda g: None):
            for g, (_, rows_, n, evs, held) in enumerate(groups):
                if held == "new":
                    split_ahead(e, me)
                if whose(g, who) != me:
                    between(g)
                    continue
                await_next(e, f"product_in_{me}")
                for ev in evs:
                    if ev[0] == "copy":
                        _, out, scale, a, b = ev
                        src = bank[g % 4][0:rows_, a:b]
                        if me == "act":
                            ins = e.activation(out, src, ACT.Copy, scale=scale)
                        elif scale == 1.0:
                            ins = e.tensor_copy(out, src)
                        else:
                            ins = e.tensor_scalar(out, src, scale, None, ALU.mult)
                    elif ev[0] == "sigmoid":
                        ins = e.activation(ev[1], bank[g % 4][:, 0:n], ACT.Sigmoid)
                    elif ev[0] == "gated":
                        _, out, gate, count = ev
                        e.wait_ge(sem("product_out_act"), count)
                        ins = e.tensor_tensor(out, bank[g % 4][:, 0:n], gate, ALU.mult)
                    else:
                        _, x, gain, a, b = ev
                        ins = e.scalar_tensor_tensor(x, bank[g % 4][0:rows_, a:b], gain, x, ALU.mult, ALU.add)
                ins.then_inc(sem(f"product_out_{me}"), 1)
                between(g)

        def h(part, k, a, b):
            return (h_lo if part else a_hi)[:, k, a:b]

        def mix(part, k, a, b):
            return (mix_lo if part else a_hi)[:, k, a:b]

        def copy(out, n, scale=1.0):
            return [("copy", out, scale, 0, n)]

        def feature_major(outs, a, b, scale=1.0, rows_=P):
            res = []
            for c, out in enumerate(outs):
                terms = [((lambda w, _, k=k, c=c: w[:, k * 256 + c * P:k * 256 + (c + 1) * P]),
                          (lambda _, p, k=k: h(p, k, a, b))) for k in range(KT)]
                res.append((terms, rows_, b - a, copy(out, b - a, scale), "new" if c == 0 else "same"))
            return res

        def token_major(outs, first=0, lo=0, n=256, held="new"):
            res = []
            for i, out in enumerate(outs):
                t0 = (first + i) * P
                wide = 256 if lo == 0 else n
                terms = [((lambda _, p, k=k, t0=t0: h(p, k, t0, t0 + P)),
                          (lambda w, _, k=k: w[:, k * 256 + lo:k * 256 + lo + wide])) for k in range(KT)]
                res.append((terms, P, wide, copy(out, n), held if i == 0 else "same"))
            return res

        def pe_norm(pe, n0, n1):
            for k in range(KT):
                await_next(pe, "squared")
                mm(pe, bank[0][:, n0:n1], const("mean"), hT[:, k, n0:n1], start=k == 0, stop=k == KT - 1,
                   last_of="mean_square" if k == KT - 1 else None)

        def act_norm(act, n0, n1, segments, split=True):
            for k in range(KT):
                act.activation(hT[:, k, n0:n1], xT[:, k, n0:n1], ACT.Square).then_inc(sem("squared"), 1)
            await_next(act, "mean_square")
            rs = mixT[:, 0, n0:n1]
            link(act, act.activation(rs, bank[0][:, n0:n1], ACT.Ln, bias=EPS))
            act.activation(rs, rs, ACT.Exp, scale=-0.5).then_inc(sem("inverse_rms"), 1)
            for k in range(KT if split else 0):
                await_next(act, "normed")
                for a, b, gain, shift in segments:
                    if shift is not None:
                        ins = act.activation(hT[:, k, a:b], hT[:, k, a:b], ACT.Identity, bias=shift(k))
                if segments[0][3] is not None:
                    link(act, ins)
                act.activation(a_hi[:, k, n0:n1], hT[:, k, n0:n1], ACT.Copy).then_inc(sem("h_rounded"), 1)

        def dve_norm(dve, n0, n1, segments, split=True):
            def rest(k):
                await_next(dve, "h_rounded")
                dve.tensor_tensor(h_lo[:, k, n0:n1], hT[:, k, n0:n1], a_hi[:, k, n0:n1].bitcast(F32),
                                  ALU.subtract).then_inc(sem("h_split"), 1)

            await_next(dve, "inverse_rms")
            for k in range(KT):
                for a, b, gain, shift in segments:
                    ins = dve.scalar_tensor_tensor(hT[:, k, a:b], xT[:, k, a:b], gain(k), mixT[:, 0, a:b],
                                                   ALU.mult, ALU.mult)
                if split:
                    ins.then_inc(sem("normed"), 1)
                    if k >= 2:
                        rest(k - 2)
            if split:
                rest(KT - 2)
                rest(KT - 1)

        def act_split_mix(act, kts, n):
            for k in range(kts):
                act.activation(a_hi[:, k, 0:n], mixT[:, k, 0:n], ACT.Copy).then_inc(sem("mix_rounded"), 1)

        def dve_split_mix(dve, kts, n):
            for k in range(kts):
                await_next(dve, "mix_rounded")
                dve.tensor_tensor(mix_lo[:, k, 0:n], mixT[:, k, 0:n], a_hi[:, k, 0:n].bitcast(F32),
                                  ALU.subtract).then_inc(sem("mix_split"), 1)

        THREE = ((0, 0), (0, 1), (1, 0))

        def hid(f, part, of=None):
            at = f * 2 * T + part * T
            return (Zr if of is None else of)[:, at:at + T]

        def pe_ffn(pe, run, off=0, first=False):
            for f in range(FT):
                w = piece_slot(pe, )
                if f >= 2:
                    pe.wait_ge(sem("hidden_full"), run * FT + f - 1)
                for half in range(2):
                    for k in range(KT):
                        if first and f == 0 and half == 0:
                            await_next(pe, "h_split")
                        for i, (wp, ap) in enumerate(THREE):
                            last = k == KT - 1 and i == 2
                            mm(pe, bank[2 * (f % 2) + half][:, 0:T],
                               w[wp][:, k * 256 + half * P:k * 256 + (half + 1) * P],
                               h(ap, k, off, off + T), start=k == 0 and i == 0, stop=last,
                               last_of="up" if last and half else None)
                stream["release"] = True
            for q in range(2 * FT):
                half, f = divmod(q, FT)
                if q % 4 == 0:
                    w = piece_slot(pe, )
                if half == 0:
                    pe.wait_ge(sem("hidden"), run * FT + f + 1)
                for d in range(4):
                    if f == 0 and half == 1:
                        pe.wait_ge(sem("down_added"), run * 8 + d + 1)
                    for i, (wp, ap) in enumerate(THREE):
                        last = f == FT - 1 and i == 2
                        mm(pe, bank[4 + d][:, 0:T], w[wp][:, (q % 4) * 512 + d * P:(q % 4) * 512 + (d + 1) * P],
                           hid(f, ap), start=f == 0 and i == 0, stop=last, last_of="down" if last else None)
                if q % 4 == 3:
                    stream["release"] = True

        def act_ffn(act, run):
            for f in range(FT + 1):
                if f < FT:
                    split_ahead(act, "act")
                    act.wait_ge(sem("up"), run * FT + f + 1)
                    if f >= 2:
                        act.wait_ge(sem("hidden_full"), run * FT + f - 1)
                    act.activation(mixT[:, f % 2, 0:T], bank[2 * (f % 2)][:, 0:T], ACT.Silu)\
                       .then_inc(sem("silu"), 1)
                if f >= 1:
                    act.wait_ge(sem("hidden_full"), run * FT + f)
                    act.activation(hid(f - 1, 0), hid(f - 1, 1, Z), ACT.Copy).then_inc(sem("hidden_rounded"), 1)
            for j in range(FT // 2):
                split_ahead(act, "act")

        def dve_ffn(dve, run, off, gains):
            for f in range(FT + 1):
                if f < FT:
                    split_ahead(dve, "dve")
                    dve.wait_ge(sem("silu"), run * FT + f + 1)
                    dve.tensor_tensor(hid(f, 1, Z), mixT[:, f % 2, 0:T], bank[2 * (f % 2) + 1][:, 0:T], ALU.mult)\
                       .then_inc(sem("hidden_full"), 1)
                if f >= 1:
                    dve.wait_ge(sem("hidden_rounded"), run * FT + f)
                    dve.tensor_tensor(hid(f - 1, 1), hid(f - 1, 1, Z), hid(f - 1, 0).bitcast(F32), ALU.subtract)\
                       .then_inc(sem("hidden"), 1)
            for j in range(FT // 2):
                split_ahead(dve, "dve")
                if j not in (FT // 4, FT // 2 - 1):
                    continue
                half = int(j > FT // 4)
                for q in range(4 * half, 4 * half + 4):
                    dve.wait_ge(sem("down"), run * 8 + q + 1)
                    ps, x = bank[4 + q % 4][:, 0:T], xT[:, q, off:off + T]
                    dve.scalar_tensor_tensor(x, ps, gains(q), x, ALU.mult, ALU.add).then_inc(sem("down_added"), 1)

        BUF, TURN, MIX = 4, 2, 3
        S = [hT[:, i, 0:512] for i in range(BUF)]
        PT = [hT[:, BUF + i, 0:512] for i in range(2)]

        def pe_attention(pe, units):
            n = len(units)
            s_rd, p_rdy, pt_cp, o_cp = (base(pe, x) for x in ("scores_read", "probs", "probs_turned", "heads_out"))
            for i in range(n + MIX):
                if i < n:
                    u = units[i]
                    if i >= 2:
                        pe.wait_ge(sem("scores_read"), s_rd + i - 1)
                    for j, (l, r, m) in enumerate(u["scores"]):
                        last = j == len(u["scores"]) - 1
                        mm(pe, bank[(6 if u["apart"] else 0) + i % 2][:, 0:m], l, r, start=j == 0, stop=last,
                           last_of="scores" if last and not u["apart"] else None)
                    if u["apart"]:
                        l, r = u["apart"]
                        mm(pe, bank[i % 2][:, 0:u["nk"]], l, r, start=True, stop=True, last_of="scores")
                if 0 <= i - TURN < n:
                    u, j = units[i - TURN], i - TURN
                    pe.wait_ge(sem("probs"), p_rdy + j + 1)
                    if j >= 2:
                        pe.wait_ge(sem("probs_turned"), pt_cp + j - 1)
                    for b in range(u["nk"] // P):
                        ins = pe.transpose(bank[2 + j % 2][:, b * P:(b + 1) * P],
                                           S[j % BUF][:, b * P:(b + 1) * P], const("ident"))
                    ins.then_inc(sem("turned"), 1)
                if i >= MIX:
                    u, j = units[i - MIX], i - MIX
                    pe.wait_ge(sem("probs_turned"), pt_cp + j + 1)
                    if j >= 2:
                        pe.wait_ge(sem("heads_out"), o_cp + j - 1)
                    lo, hi = u["rows"]
                    for b, vt in enumerate(u["v"]):
                        last = b == len(u["v"]) - 1
                        mm(pe, bank[4 + j % 2][lo:hi, 0:P], vt, PT[j % 2][:, b * P:(b + 1) * P],
                           start=b == 0, stop=last, last_of="mixed" if last else None)
            for x in ("scores_read", "probs", "probs_turned", "heads_out"):
                advance(pe, x, n)

        def act_attention(act, units):
            n = len(units)
            nm, td, mx = (base(act, x) for x in ("neg_max", "turned", "mixed"))
            for i in range(n + MIX):
                if i < n:
                    u = units[i]
                    col = (i % BUF) * 8
                    act.wait_ge(sem("neg_max"), nm + i + 1)
                    if u["apart"]:
                        act.activation(sc[:, col + 3:col + 4], sc[:, col + 1:col + 2], ACT.Exp)
                        act.activation(S[i % BUF][:, 0:u["nk"]], S[i % BUF][:, 0:u["nk"]], ACT.Exp,
                                       bias=sc[:, col + 1:col + 2]).then_inc(sem("exps"), 1)
                    else:
                        if u["sink"] is not None:
                            act.activation(sc[:, col + 3:col + 4], u["sink"], ACT.Exp, bias=sc[:, col + 1:col + 2])
                        act.activation(S[i % BUF][:, 0:u["nk"]], S[i % BUF][:, 0:u["nk"]], ACT.Exp,
                                       bias=sc[:, col + 1:col + 2], accum_out=sc[:, col + 2:col + 3])\
                           .then_inc(sem("exps"), 1)
                if 0 <= i - TURN < n:
                    u, j = units[i - TURN], i - TURN
                    act.wait_ge(sem("turned"), td + j + 1)
                    if j >= 2:
                        act.wait_ge(sem("mixed"), mx + j - 1)
                    act.activation(PT[j % 2][:, 0:u["nk"]], bank[2 + j % 2][:, 0:u["nk"]], ACT.Copy)\
                       .then_inc(sem("probs_turned"), 1)
                if i >= MIX:
                    u, j = units[i - MIX], i - MIX
                    act.wait_ge(sem("mixed"), mx + j + 1)
                    lo, hi = u["rows"]
                    act.activation(u["out"], bank[4 + j % 2][lo:hi, 0:P], ACT.Copy)\
                       .then_inc(sem("heads_out"), 1)
            for x in ("neg_max", "turned", "mixed"):
                advance(act, x, n)

        def dve_attention(dve, units):
            n = len(units)
            so, ex, td = (base(dve, x) for x in ("scores", "exps", "turned"))
            for i in range(n + 1):
                if i < n:
                    u = units[i]
                    col = (i % BUF) * 8
                    dve.wait_ge(sem("scores"), so + i + 1)
                    if i >= BUF:
                        dve.wait_ge(sem("turned"), td + i - BUF + 1)
                    src = bank[6 + i % 2] if u["apart"] else bank[i % 2]
                    ins = dve.tensor_tensor_reduce(S[i % BUF][:, 0:u["nk"]], src[:, 0:u["nk"]], u["mask"], 1.0,
                                                   u["init"], ALU.add, ALU.max, sc[:, col:col + 1])
                    if u["apart"]:
                        link(dve, ins)
                    else:
                        ins.then_inc(sem("scores_read"), 1)
                        await_next(dve, "scores_read")
                    dve.tensor_scalar(sc[:, col + 1:col + 2], sc[:, col:col + 1], -1.0, None, ALU.mult)\
                       .then_inc(sem("neg_max"), 1)
                if i >= 1:
                    u, j = units[i - 1], i - 1
                    col = (j % BUF) * 8
                    den = sc[:, col + 2:col + 3]
                    Sj = S[j % BUF][:, 0:u["nk"]]
                    dve.wait_ge(sem("exps"), ex + j + 1)
                    if u["apart"]:
                        ins = dve.tensor_tensor_reduce(Sj, bank[j % 2][:, 0:u["nk"]], Sj, HD ** -0.5, 0.0, ALU.mult,
                                                       ALU.add, den)
                        ins.then_inc(sem("scores_read"), 1)
                        await_next(dve, "scores_read")
                        link(dve, dve.tensor_scalar(sc[:, col + 4:col + 5], den, -1.0, None, ALU.mult))
                        link(dve, dve.tensor_tensor(den, den, sc[:, col + 4:col + 5], ALU.max))
                        link(dve, dve.tensor_tensor(den, den, sc[:, col + 3:col + 4], ALU.max))
                    elif u["sink"] is not None:
                        link(dve, dve.tensor_tensor(den, den, sc[:, col + 3:col + 4], ALU.add))
                    link(dve, dve.reciprocal(sc[:, col + 5:col + 6], den))
                    dve.tensor_scalar(Sj, Sj, sc[:, col + 5:col + 6], None, ALU.mult).then_inc(sem("probs"), 1)
            for x in ("scores", "exps", "turned"):
                advance(dve, x, n)

        def dve_log_sigmoid_a(dve, z, t):
            link(dve, dve.tensor_scalar(t, z, -1.0, None, ALU.mult))
            dve.tensor_tensor(t, t, z, ALU.min).then_inc(sem("neg_abs"), 1)

        def act_log_sigmoid(act, t):
            await_next(act, "neg_abs")
            link(act, act.activation(t, t, ACT.Exp))
            act.activation(t, t, ACT.Ln, bias=1.0).then_inc(sem("log1p"), 1)

        def b1_groups(layer):
            n = 2 * T if layer == 0 else T
            zt = lambda i, b=n: Zt[:, i, 0:b]
            g = []
            for j, tiles in enumerate(((0, 1), (2, 3), (4, 5))):
                g += feature_major([zt(i) for i in tiles], 0, n)
            for tiles in ((6, 7), (8, 9)):
                g += feature_major([zt(i) for i in tiles], 0, n, HD ** -0.5)
            g += feature_major([zt(10, 2 * T)], 0, 2 * T)
            g += token_major([tok[:, t * 384:t * 384 + P] for t in range(4)], 0, P, P, "same")
            g += feature_major([zt(11), zt(12)], 0, n, HD ** -0.5)
            g += feature_major([zt(13, 2 * T), zt(14, 2 * T)], 0, 2 * T)
            g += token_major([tok[:, t * 384 + P:(t + 1) * 384] for t in range(4)])
            g += feature_major([zt(15), zt(16)], 0, n)
            g += feature_major([lrT(0), lrT(1)], 0, 2 * T, rows_=16)
            return g

        lr_ones = Zt[0:32, 17:19, :]

        def lrT(d):
            return Zt[0:16, 17 + d, :]

        class Mod:
            def __init__(self, e, me, first, n):
                self.e, self.me, self.first, self.n, self.k = e, me, first, n, 0

            def step(self):
                k, self.k = self.k, self.k + 1
                if self.me == "pe" and k <= self.n:
                    pe_mod_step(self.e, self.first, self.n, k)
                elif self.me != "pe" and k < self.n:
                    split_ahead(self.e, self.me)
                    if self.me == "act":
                        act_mod_rows(self.e, self.first + k)

            def among(self, groups, steps=1):
                def between(g):
                    if g + 1 == len(groups) or groups[g + 1][4] == "new":
                        for _ in range(steps):
                            self.step()
                return between

            def finish(self):
                while self.k <= self.n:
                    self.step()
                if self.me == "dve":
                    dve_mod_take(self.e, self.first, self.n)

        def pe_mod_step(pe, first, n, k):
            m = first + k
            if k >= 1:
                pe.wait_ge(sem("mod_rows"), m)
                for j in range(2):
                    mm(pe, bank[7][:, 4 * (k - 1) + 2 * j:4 * (k - 1) + 2 * j + 2],
                       mod_rows[:, (m - 1) % 2, j * P:(j + 1) * P],
                       cst[0:4, CONST["pair"][0]:CONST["pair"][1]], start=True, stop=True,
                       last_of="mod_columns" if j == 1 else None)
            if k < n:
                w = piece_slot(pe)
                for kt in range(KT):
                    for part in range(2):
                        last = kt == KT - 1 and part == 1
                        mm(pe, bank[6][0:4, 0:256], c_mat[:, kt, :], w[part][:, kt * 256:(kt + 1) * 256],
                           start=kt == 0 and part == 0, stop=last, last_of="mod_sums" if last else None)
                stream["release"] = True

        def act_mod_rows(act, m):
            act.wait_ge(sem("mod_sums"), m + 1)
            if m >= 2:
                act.wait_ge(sem("mod_columns"), m - 1)
            act.activation(mod_rows[:, m % 2, :], bank[6][0:4, 0:256], ACT.Copy).then_inc(sem("mod_rows"), 1)

        def dve_mod_take(dve, first, n):
            layer, p = divmod(first, MOD_PIECES)
            dve.wait_ge(sem("mod_columns"), first + n)
            link(dve, dve.tensor_tensor(modT[:, layer, 2 * p:2 * (p + n), :],
                                        bank[7][:, 0:4 * n].rearrange("p (j s) -> p j s", s=2),
                                        v("b_mod", layer, 2 * p, 2 * (p + n)).unsqueeze(2).to_broadcast([P, 2 * n, 2]),
                                        ALU.add))
            for i, name in ((0, "norm1"), (1, "norm2")):
                lo = 8 + 24 * i
                if 2 * p <= lo < 2 * (p + n):
                    dve.scalar_tensor_tensor(a1[:, layer, i, :, :], modT[:, layer, lo:lo + 8, :], 1.0,
                                             v(name, layer).unsqueeze(2).to_broadcast([P, KT, 2]),
                                             ALU.add, ALU.mult)

        def pe_mod(pe):
            await_next(pe, "c_split")
            Mod(pe, "pe", 0, EARLY).finish()
            phase_end(pe)

        def act_mod(act):
            act.wait_ge(sem("vectors_in"), 16 * N_LOADS)
            link(act, act.activation(v("c"), v("c"), ACT.Silu))
            c = v("c").rearrange("p (k s) -> p k s", s=2)
            act.activation(c_mat[:, :, 0:2], c, ACT.Copy).then_inc(sem("c_rounded"), 1)
            Mod(act, "act", 0, EARLY).finish()
            phase_end(act)

        def dve_mod(dve):
            dve.wait_ge(sem("vectors_in"), 16 * N_LOADS)
            dve.tensor_copy(lvl_mask[:, :, :].rearrange("p l n -> p (l n)"), Z[:, 0:2 * LEVELS * P])
            await_next(dve, "c_rounded")
            dve.tensor_tensor(c_mat[:, :, 2:4], v("c").rearrange("p (k s) -> p k s", s=2),
                              c_mat[:, :, 0:2].bitcast(F32), ALU.subtract).then_inc(sem("c_split"), 1)
            Mod(dve, "dve", 0, EARLY).finish()
            phase_end(dve)

        def b1_segments(layer, which, n):
            segs = [(s * T, (s + 1) * T,
                     (lambda k, s=s: a1[:, layer, which, k, s:s + 1]),
                     (lambda k, s=s: modT[:, layer, 24 * which + k, s:s + 1])) for s in range(n // T)]
            return segs

        U = Zt[:, 19:22, :].rearrange("p a b -> p (a b)")[:, 0:2 * 2 * 258].rearrange("p (c s n) -> p c s n", c=2, s=2)

        def pe_rope(pe, layer):
            for j in range(5):
                if j >= 4:
                    await_next(pe, "rotated_read")
                mm(pe, bank[j % 4][:, 0:T], const("rot"), Zt[:, 6 + j, 0:T], start=True, stop=True,
                   last_of="rotated")
            advance(pe, "rotated_read", 4)
            phase_end(pe)

        def act_rope(act, layer):
            phase_end(act)

        def dve_rope_conv(dve, layer):
            for j in range(5):
                await_next(dve, "rotated")
                z, t = Zt[:, 6 + j, 0:T], hT[:, j, 0:T]
                dve.tensor_tensor(t, bank[j % 4][:, 0:T], const("sin"), ALU.mult).then_inc(sem("rotated_read"), 1)
                link(dve, dve.tensor_tensor(z, z, const("cos"), ALU.mult))
                await_next(dve, "rotated_read")
                dve.tensor_tensor(z, z, t, ALU.add)
            ns = 2 if layer == 0 else 1
            link(dve, dve.memset(U[:, :, :, :], 0.0))
            for c in range(2):
                seg = lambda i: Zt[:, i + c, 0:ns * T].rearrange("p (s n) -> p s n", s=ns)
                w = lambda j: v("conv_w", layer, 2 * j + c, 2 * j + c + 1)
                y = hT[:, 5 + c, 0:ns * T].rearrange("p (s n) -> p s n", s=ns)
                link(dve, dve.tensor_tensor(U[:, c, 0:ns, 1:T + 1], seg(0), seg(4), ALU.mult))
                link(dve, dve.tensor_scalar(y, U[:, c, 0:ns, 0:T], w(0), None, ALU.mult))
                for j in (1, 2):
                    link(dve, dve.scalar_tensor_tensor(y, U[:, c, 0:ns, j:T + j], w(j), y, ALU.mult, ALU.add))
                link(dve, dve.tensor_tensor(mixT[:, c, 0:ns * T].rearrange("p (s n) -> p s n", s=ns), y, seg(2),
                                            ALU.mult))
            phase_end(dve)

        def b1_units(layer):
            units = []
            for s in range(2 if layer == 0 else 1):
                for h in range(8):
                    g, t = divmod(h, 4)
                    r0 = g * HD
                    for q in range(TT):
                        tq = s * T + q * P
                        keys = (0, 2 * T) if s == 0 else (T, 2 * T)
                        nk = keys[1] - keys[0]
                        if s == 0:
                            mask = const("masks", 0, 512) if q == 1 else const("masks", 384, 896)
                        else:
                            mask = const("masks", 128, 384)
                        units.append(dict(apart=None,
                            scores=[(Zt[r0:r0 + HD, 6 + t, tq:tq + P], Zt[r0:r0 + HD, 10, keys[0]:keys[1]], nk)],
                            nk=nk, mask=mask, init=v("sink", layer, h, h + 1), sink=v("sink", layer, h, h + 1),
                            v=[tok[:, b * 384 + g * HD:b * 384 + (g + 1) * HD] for b in range(keys[0] // P, keys[1] // P)],
                            rows=((h % 2) * HD, (h % 2 + 1) * HD),
                            out=mixT[(h % 2) * HD:(h % 2 + 1) * HD, 2 + h // 2, tq:tq + P]))
            return units

        gB = [hflat[:, d * 1024:(d + 1) * 1024].rearrange("p (c n) -> p c n", c=2) for d in range(2)]
        gG = hflat[:, 2048:4096].rearrange("p (t c) -> p t c", t=4)
        gM = [Z[:, i * 1024:(i + 1) * 1024].rearrange("p (c n) -> p c n", c=2) for i in range(2)]
        gE = [Z[:, (2 + i) * 1024:(3 + i) * 1024].rearrange("p (c n) -> p c n", c=2) for i in range(2)]
        gA = Z[:, 19 * 512 - 1024:19 * 512 + 1024].rearrange("p (t h n) -> p t h n", t=4, h=4)
        gK = Z[:, 4096:4352].rearrange("p (c n) -> p c n", c=2)
        gKt = Z[:, 4352:4608]
        gS = Z[:, 4608:5120].rearrange("p (d c n) -> p d c n", d=2, c=2)
        gX = Z[:, 5120:5376].rearrange("p (c n) -> p c n", c=2)
        gQ = Z[:, 0:2048].rearrange("p (d t c n) -> p d t c n", d=2, t=4, c=2)
        gD = sc[:, 16:32].rearrange("p (d t c) -> p d t c", d=2, t=4)

        GQ, GK = Zt[:, 11:13, :], Zt[:, 13:15, :]
        ORDER = ((2, 3, 0, 1), (3, 2, 1, 0))

        def pe_gla_gates(pe, layer):
            for t in range(4):
                for d in range(2):
                    ps = bank[t][:, d * 256:(d + 1) * 256]
                    mm(pe, ps, lr_ones[0:17, d, t * P:(t + 1) * P], gate_w[:, layer, d, :], start=True, stop=True,
                       last_of="gates" if d == 1 else None)
            for half in range(2):
                await_next(pe, "log_gates")
                for d in range(2):
                    for c in range(2):
                        for t in (2 * half, 2 * half + 1):
                            mm(pe, bank[4 + 2 * d + c][:, t * P:(t + 1) * P],
                               gG[:, t, d * 256 + c * P:d * 256 + (c + 1) * P],
                               const("tri" if d == 0 else "tri_r"), start=True, stop=True,
                               last_of="decays" if t == 3 else None)
            phase_end(pe)

        def act_gla_gates(act, layer):
            for half in range(2):
                act_log_sigmoid(act, Z[:, 1024 * half:1024 * (half + 1)])
            for d in range(2):
                for c in range(2):
                    await_next(act, "decays")
                    link(act, act.activation(gB[d][:, c, :], bank[4 + 2 * d + c][:, :], ACT.Copy))
                    edge = slice(P - 1, 512, P) if d == 0 else slice(0, 512, P)
                    act.activation(gD[:, d, :, c], gB[d][:, c, edge], ACT.Exp)
            phase_end(act)

        def dve_gla_gates(dve, layer):
            halves = [(gG[:, 2 * i:2 * i + 2, :].rearrange("p t c -> p (t c)"), Z[:, 1024 * i:1024 * (i + 1)])
                      for i in range(2)]
            for half, (g, t_abs) in enumerate(halves):
                for t in (2 * half, 2 * half + 1):
                    await_next(dve, "gates")
                    ins = dve.tensor_copy(gG[:, t, :], bank[t][:, :])
                link(dve, ins)
                dve_log_sigmoid_a(dve, g, t_abs)
            for g, t_abs in halves:
                link(dve, dve.tensor_scalar(g, g, 0.0, 1.0 / 16, ALU.min, ALU.mult))
            for g, t_abs in halves:
                await_next(dve, "log1p")
                dve.scalar_tensor_tensor(g, t_abs, -1.0 / 16, g, ALU.mult, ALU.add).then_inc(sem("log_gates"), 1)
            phase_end(dve)

        def gla_level(l, buf, d, n):
            h = 1 << l
            x = buf[:, :, 0:n].rearrange("p c (b u h) -> p c b u h", u=2, h=h)
            return x[:, :, :, 0, :], x[:, :, :, 1, :]

        def gram(t, h):
            return bank[2 * t + h % 2][:, (h // 2) * P:(h // 2 + 1) * P]

        def grams(t):
            return psum[:, 2 * t:2 * t + 2, 0:2 * P].rearrange("p u (v n) -> p u v n", v=2)

        def by_bank(t):
            return gA[:, t].rearrange("p (v u) n -> p u v n", v=2)

        def gla_steps():
            return [(l, d) for l in range(LEVELS) for d in range(2)]

        def pe_gla_levels(pe, layer):
            tiles = range(4 if layer == 0 else 2)
            for t in tiles:
                for h in range(4):
                    r = slice((h % 2) * HD, (h % 2 + 1) * HD)
                    mm(pe, gram(t, h), GK[r, h // 2, t * P:(t + 1) * P],
                       GQ[r, h // 2, t * P:(t + 1) * P], start=True, stop=True,
                       last_of="grams" if h == 3 else None)
            rd = base(pe, "gram_read")
            nt = len(tiles)
            for i, (l, d) in enumerate(gla_steps()):
                await_next(pe, "level")
                for t in tiles:
                    pe.wait_ge(sem("gram_read"), rd + i * nt + t + 1)
                    for h in range(4):
                        r = slice((h % 2) * HD, (h % 2 + 1) * HD)
                        m = gM[i % 2][r, h // 2, t * P:(t + 1) * P]
                        mm(pe, gram(t, h), m, m, start=True, stop=True,
                           last_of="grams" if h == 3 else None)
            advance(pe, "gram_read", nt * (1 + 2 * LEVELS))
            phase_end(pe)

        def act_gla_levels(act, layer):
            n = 2 * T if layer == 0 else T
            for i, (l, d) in enumerate(gla_steps()):
                await_next(act, "level_decay")
                e = gE[i % 2][:, :, 0:n]
                act.activation(e, e, ACT.Exp).then_inc(sem("level_exp"), 1)
            phase_end(act)

        def dve_gla_levels(dve, layer):
            n = 2 * T if layer == 0 else T
            nt = n // P
            steps = gla_steps()

            def decay(i):
                l, d = steps[i]
                h = 1 << l
                lo, hi = gla_level(l, gB[d], d, n)
                e_lo, e_hi = gla_level(l, gE[i % 2], d, n)
                m = (lo[:, :, :, h - 1:h] if d == 0 else hi[:, :, :, 0:1])
                for c in range(2):
                    mb = m[:, c].to_broadcast([P, n // (2 * h), h])
                    a, b = (hi, lo) if d == 0 else (lo, hi)
                    ea, eb = (e_hi, e_lo) if d == 0 else (e_lo, e_hi)
                    dve.tensor_tensor(ea[:, c], a[:, c], mb, ALU.subtract)
                    ins = dve.tensor_tensor(eb[:, c], mb, b[:, c], ALU.subtract)
                ins.then_inc(sem("level_decay"), 1)

            def scaled(i):
                l, d = steps[i]
                q_lo, q_hi = gla_level(l, GQ, d, n)
                k_lo, k_hi = gla_level(l, GK, d, n)
                e_lo, e_hi = gla_level(l, gE[i % 2], d, n)
                m_lo, m_hi = gla_level(l, gM[i % 2], d, n)
                await_next(dve, "level_exp")
                if i >= 2:
                    dve.wait_ge(sem("grams"), gr + nt * i)
                for c in range(2):
                    dve.tensor_tensor(m_lo[:, c], (k_lo if d == 0 else q_lo)[:, c], e_lo[:, c], ALU.mult)
                    ins = dve.tensor_tensor(m_hi[:, c], (q_hi if d == 0 else k_hi)[:, c], e_hi[:, c], ALU.mult)
                ins.then_inc(sem("level"), 1)

            gr = base(dve, "grams")
            own = base(dve, "gram_read")
            decay(0)
            for t in range(nt):
                dve.wait_ge(sem("grams"), gr + t + 1)
                eye = const("ident").unsqueeze(1).to_broadcast([P, 2, P])
                for u in range(2):
                    ins = dve.scalar_tensor_tensor(by_bank(t)[:, u], grams(t)[:, u], 2.0, eye, ALU.mult, ALU.mult)
                ins.then_inc(sem("gram_read"), 1)
            for i, (l, d) in enumerate(steps):
                scaled(i)
                if i + 1 < len(steps):
                    decay(i + 1)
                mask = lvl_mask[:, 2 * l + d, :].unsqueeze(1).unsqueeze(1).to_broadcast([P, 2, 2, P])
                for t in range(nt):
                    dve.wait_ge(sem("grams"), gr + nt * (i + 1) + t + 1)
                    dve.wait_ge(sem("gram_read"), own + nt * i + t + 1)
                    dve.copy_predicated(by_bank(t), mask, grams(t))\
                       .then_inc(sem("gram_read"), 1)
            advance(dve, "grams", nt * (1 + 2 * LEVELS))
            advance(dve, "gram_read", nt * (1 + 2 * LEVELS))
            phase_end(dve)

        def pe_gla_out(pe, layer):
            outs = (0, 1, 2, 3) if layer == 0 else (0, 1)
            await_next(pe, "queries_decayed")
            first = {t: True for t in outs}
            for d in range(2):
                for i, t in enumerate(ORDER[d]):
                    if i > 0 and t in outs:
                        await_next(pe, "state")
                        for c in range(2):
                            mm(pe, bank[t][:, c * P:(c + 1) * P], gS[:, d, c, :], gQ[:, d, t, c, :],
                               start=first[t] and c == 0, stop=False, skip_group_check=True,
                               last_of="state_used" if c == 1 else None)
                        first[t] = False
                    elif i > 0:
                        await_next(pe, "state")
                        pe.nop().then_inc(sem("state_used"), 1)
                    if i < 3:
                        await_next(pe, "keys_decayed")
                        for c in range(2):
                            ins = pe.transpose(bank[4][:, c * P:(c + 1) * P], gK[:, c, :], const("ident"))
                        ins.then_inc(sem("keys_turned"), 1)
                        await_next(pe, "keys_copied")
                        for c in range(2):
                            mm(pe, bank[5][:, c * P:(c + 1) * P], gKt[:, c * P:(c + 1) * P],
                               tok[:, t * 384 + P + c * P:t * 384 + P + (c + 1) * P], start=True, stop=True,
                               last_of="state_step" if c == 1 else None)
            for t in outs:
                for h in range(4):
                    mm(pe, bank[t][(h % 2) * HD:(h % 2 + 1) * HD, (h // 2) * P:(h // 2 + 1) * P],
                       tok[:, t * 384 + P + h * HD:t * 384 + P + (h + 1) * HD], gA[:, t, h, :],
                       start=False, stop=True, skip_group_check=True, last_of="gla_sum" if h == 3 else None)
            phase_end(pe)

        def act_gla_out(act, layer):
            outs = (0, 1, 2, 3) if layer == 0 else (0, 1)
            for d in range(2):
                for t in outs:
                    for c in range(2):
                        ins = act.activation(gQ[:, d, t, c, :], gB[d][:, c, t * P:(t + 1) * P], ACT.Exp)
            ins.then_inc(sem("query_exp"), 1)
            for d in range(2):
                for i, t in enumerate(ORDER[d][:3]):
                    if d or i:
                        await_next(act, "keys_decayed")
                    edge = t * P + (P - 1 if d == 0 else 0)
                    for c in range(2):
                        ins = act.activation(gX[:, c, :], gB[d][:, c, t * P:(t + 1) * P], ACT.Exp, scale=-1.0,
                                             bias=gB[d][:, c, edge:edge + 1])
                    ins.then_inc(sem("key_exp"), 1)
                    await_next(act, "keys_turned")
                    act.activation(gKt, bank[4][:, 0:256], ACT.Copy).then_inc(sem("keys_copied"), 1)
            advance(act, "keys_decayed", 1)
            phase_end(act)

        def dve_gla_out(dve, layer):
            outs = (0, 1, 2, 3) if layer == 0 else (0, 1)
            link(dve, dve.memset(gS[:, :, :, :].rearrange("p d c n -> p (d c n)"), 0.0))
            await_next(dve, "query_exp")
            for d in range(2):
                for t in outs:
                    ins = dve.tensor_tensor(gQ[:, d, t, :, :], gQ[:, d, t, :, :], GQ[:, :, t * P:(t + 1) * P], ALU.mult)
            ins.then_inc(sem("queries_decayed"), 1)
            for d in range(2):
                for i, t in enumerate(ORDER[d][:3]):
                    await_next(dve, "key_exp")
                    dve.tensor_tensor(gK[:, :, :], gX[:, :, :], GK[:, :, t * P:(t + 1) * P], ALU.mult)\
                       .then_inc(sem("keys_decayed"), 1)
                    await_next(dve, "state_step")
                    if i > 0:
                        await_next(dve, "state_used")
                    for c in range(2):
                        for r in range(2):
                            rr = slice(r * HD, (r + 1) * HD)
                            s = gS[rr, d, c, rr]
                            ins = dve.scalar_tensor_tensor(s, s, gD[rr, d, t, c:c + 1],
                                                           bank[5][rr, c * P + r * HD:c * P + (r + 1) * HD],
                                                           ALU.mult, ALU.add)
                    link(dve, ins)
                    dve.nop().then_inc(sem("state"), 1)
                await_next(dve, "state_used")
            phase_end(dve)

        def gla_o(layer):
            n = 2 * T if layer == 0 else T
            return n, Z[:, 0:2 * n].rearrange("p (c n) -> p c n", c=2)

        def pe_gla_norm(pe, layer):
            for c in range(2):
                await_next(pe, "gla_squared")
                n = 2 * T if layer == 0 else T
                mm(pe, bank[4 + c][:, 0:n], const("head_mean"), gSq[:, c, 0:n], start=True, stop=True,
                   last_of="gla_mean_square")
            phase_end(pe)

        gSq = hflat[:, 0:1024].rearrange("p (c n) -> p c n", c=2)
        gR = hflat[:, 1024:2048].rearrange("p (c n) -> p c n", c=2)
        gSi = hflat[:, 2048:3072].rearrange("p (c n) -> p c n", c=2)

        def act_gla_norm(act, layer):
            n, o = gla_o(layer)
            for t in range(n // P):
                link(act, act.activation(o[:, :, t * P:(t + 1) * P],
                                         bank[t][:, 0:256].rearrange("p (c n) -> p c n", c=2), ACT.Copy))
            for c in range(2):
                act.activation(gSq[:, c, 0:n], o[:, c, :], ACT.Square).then_inc(sem("gla_squared"), 1)
            for c in range(2):
                await_next(act, "gla_mean_square")
                link(act, act.activation(gR[:, c, 0:n], bank[4 + c][:, 0:n], ACT.Ln, bias=EPS))
                act.activation(gR[:, c, 0:n], gR[:, c, 0:n], ACT.Exp, scale=-0.5).then_inc(sem("gla_rms"), 1)
            for c in range(2):
                act.activation(gSi[:, c, 0:n], Zt[:, 15 + c, 0:n], ACT.Silu).then_inc(sem("gla_silu"), 1)
            phase_end(act)

        def dve_gla_norm(dve, layer):
            n, o = gla_o(layer)
            for c in range(2):
                await_next(dve, "gla_rms")
                link(dve, dve.scalar_tensor_tensor(gR[:, c, 0:n], gR[:, c, 0:n], v("gla_g", layer), o[:, c, :],
                                                   ALU.mult, ALU.mult))
            for c in range(2):
                await_next(dve, "gla_silu")
                dve.tensor_tensor(mixT[:, 6 + c, 0:n], gR[:, c, 0:n], gSi[:, c, 0:n], ALU.mult)
            phase_end(dve)

        def out_groups(kts, n, gains, per_piece):
            res = []
            for d in range(KT):
                c = d % per_piece
                w_ = per_piece * P
                terms = [((lambda w, _, k=k, c=c: w[:, k * w_ + c * P:k * w_ + (c + 1) * P]),
                          (lambda _, p, k=k: mix(p, k, 0, n))) for k in range(kts)]
                evs = [("resid", xT[:, d, s * T:(s + 1) * T], gains(d, s), s * T, (s + 1) * T) for s in range(n // T)]
                res.append((terms, P, n, evs, "new" if c == 0 else "same"))
            return res

        UP = mixT[:, 0:5, :].rearrange("p a b -> p (a b)")[:, 0:4 * 259].rearrange("p (c n) -> p c n", c=4)
        CP = mixflat[:, 1040:1040 + 2 * 286].rearrange("p (c n) -> p c n", c=2)
        SG = sc[:, 44:76].rearrange("p (t c) -> p t c", t=2)
        FC = sc[:, 76:84].rearrange("p (t c) -> p t c", t=2)
        BH = Z[:, 18 * 512:18 * 512 + 1536].rearrange("p (h n) -> p h n", h=4)
        FOX_B = [BH, Z[:, 0:1536].rearrange("p (h n) -> p h n", h=4)]

        def mv(t, h):
            return tok[:, t * 768 + h * HD:t * 768 + (h + 1) * HD]

        def fv(t, h):
            return tok[:, t * 768 + 256 + h * HD:t * 768 + 256 + (h + 1) * HD]

        def z2(i):
            return Zt[:, i, 0:T]

        def b2_groups(layer):
            g = feature_major([z2(8), z2(9)], 0, T)
            g += feature_major([z2(6), z2(7)], 0, T)
            for c in range(2):
                terms, rows_, n, _, held = g[c]
                g[c] = (terms, rows_, n, [("sigmoid", z2(8 + c))], held)
                terms, rows_, n, _, held = g[2 + c]
                g[2 + c] = (terms, rows_, n, [("gated", CP[:, c, 30:30 + T], z2(8 + c), act_outs[layer] + c + 1)], held)
            g += feature_major([UP[:, 0, 3:259], UP[:, 1, 3:259]], 0, T)
            g += feature_major([UP[:, 2, 3:259], UP[:, 3, 3:259]], 0, T)
            g += token_major([SG[:, t, :] for t in range(2)], n=16)
            g += token_major([tok[:, t * 768:t * 768 + 256] for t in range(2)])
            g += feature_major([z2(4), z2(5)], 0, T)
            for j in range(2):
                g += feature_major([z2(10 + 2 * j), z2(11 + 2 * j)], 0, T, HD ** -0.5)
            for j in range(2):
                g += feature_major([z2(14 + 2 * j), z2(15 + 2 * j)], 0, T)
            for j in range(2):
                g += token_major([tok[:, t * 768 + 256 + 256 * j:t * 768 + 512 + 256 * j] for t in range(2)])
            return g

        B2_WHO = ["act", "act", "dve", "dve"] + 22 * ["act"]
        act_outs = [0, 0]

        def dve_convs(dve, layer):
            spread = len(B2_WHO) - 4

            def step(g):
                if g == 0:
                    for c in range(2):
                        dve.memset(CP[:, c, 0:30], 0.0)
                        dve.memset(UP[:, 2 * c, 0:3], 0.0)
                        ins = dve.memset(UP[:, 2 * c + 1, 0:3], 0.0)
                    link(dve, ins)
                if g == 3:
                    dve.wait_ge(sem("product_out_dve"), base(dve, "product_in_dve"))
                if g < 4:
                    return
                for j in range((g - 4) * 31 // spread, (g - 3) * 31 // spread):
                    for c in range(2):
                        w = v("c_conv_w", layer, 2 * j + c, 2 * j + c + 1)
                        if j == 0:
                            ins = dve.tensor_scalar(z2(6 + c), CP[:, c, 0:T], w, v("c_conv_b", layer, c, c + 1),
                                                    ALU.mult, ALU.add)
                        else:
                            ins = dve.scalar_tensor_tensor(z2(6 + c), CP[:, c, j:j + T], w, z2(6 + c),
                                                           ALU.mult, ALU.add)
                    link(dve, ins)
                if g >= 10:
                    c, j = divmod(g - 10, 4)
                    if j == 0:
                        dve.wait_ge(sem("product_out_act"), act_outs[layer] + 3 + c)
                    w = v("m_conv_w", layer, 4 * j + c, 4 * j + c + 1)
                    if j == 0:
                        ins = dve.tensor_scalar(z2(c), UP[:, c, 0:T], w, v("m_conv_b", layer, c, c + 1),
                                                ALU.mult, ALU.add)
                    else:
                        ins = dve.scalar_tensor_tensor(z2(c), UP[:, c, j:j + T], w, z2(c), ALU.mult, ALU.add)
                    if j == 3:
                        ins.then_inc(sem("m_conv"), 1)
                    else:
                        link(dve, ins)
            return step

        def pe_b2_gates_ln(pe, layer):
            for c in range(2):
                mm(pe, bank[2][:, 0:T], const("mean"), z2(6 + c), start=c == 0, stop=c == 1,
                   last_of="ln_mean" if c == 1 else None)
            await_next(pe, "log_f")
            mm(pe, bank[0][:, 0:4], const("tri"), SG[:, 0, 4:8], start=True, stop=True, last_of=None)
            mm(pe, bank[1][:, 0:4], const("ones"), SG[:, 0, 4:8], start=True, stop=False, last_of=None)
            mm(pe, bank[1][:, 0:4], const("tri"), SG[:, 1, 4:8], start=False, stop=True, last_of="f_sums")
            for c in range(2):
                await_next(pe, "ln_squared")
                mm(pe, bank[3][:, 0:T], const("mean"), z2(8 + c), start=c == 0, stop=c == 1,
                   last_of="ln_var" if c == 1 else None)
            phase_end(pe)

        def act_b2_gates_ln(act, layer):
            act_log_sigmoid(act, sc[:, 0:24].rearrange("p (t c) -> p t c", t=2))
            for c in range(2):
                await_next(act, "ln_centred")
                act.activation(z2(8 + c), z2(6 + c), ACT.Square).then_inc(sem("ln_squared"), 1)
            await_next(act, "ln_var")
            link(act, act.activation(hT[:, 4, 0:T], bank[3][:, 0:T], ACT.Ln, bias=EPS, scale=4.0))
            act.activation(hT[:, 4, 0:T], hT[:, 4, 0:T], ACT.Exp, scale=-0.5).then_inc(sem("ln_rms"), 1)
            for c in range(4):
                await_next(act, "m_conv")
                act.activation(z2(c), z2(c), ACT.Silu)
            for c in range(2):
                await_next(act, "ln_scaled")
                act.activation(mixT[:, 2 + c, 0:T], z2(6 + c), ACT.Silu, bias=v("ln_b", layer, c, c + 1))
            phase_end(act)

        def dve_b2_gates_ln(dve, layer):
            bias = v("gate_b", layer).unsqueeze(1).to_broadcast([P, 2, 16])
            link(dve, dve.tensor_tensor(SG[:, :, :], SG[:, :, :], bias, ALU.add))
            z, t = SG[:, :, 4:16], sc[:, 0:24].rearrange("p (t c) -> p t c", t=2)
            dve_log_sigmoid_a(dve, z, t)
            link(dve, dve.tensor_scalar(z, z, 0.0, None, ALU.min))
            await_next(dve, "ln_mean")
            for c in range(2):
                dve.scalar_tensor_tensor(z2(6 + c), bank[2][:, 0:T], -4.0, z2(6 + c), ALU.mult, ALU.add)\
                   .then_inc(sem("ln_centred"), 1)
            advance(dve, "ln_centred", 1)
            await_next(dve, "log1p")
            dve.tensor_tensor(z, z, t, ALU.subtract).then_inc(sem("log_f"), 1)
            await_next(dve, "log_f")
            dve_decay_columns(dve, BH, 4, 0)
            await_next(dve, "f_sums")
            dve.tensor_copy(FC[:, 0, :], bank[0][:, 0:4])
            dve.tensor_copy(FC[:, 1, :], bank[1][:, 0:4])
            await_next(dve, "ln_centred")
            await_next(dve, "ln_rms")
            for c in range(2):
                dve.scalar_tensor_tensor(z2(6 + c), z2(6 + c), v("ln_w", layer, c, c + 1), hT[:, 4, 0:T],
                                         ALU.mult, ALU.mult).then_inc(sem("ln_scaled"), 1)
            phase_end(dve)

        def dve_decay_columns(dve, B, f0, i0):
            for j in range(4):
                f = [SG[:, t, f0 + j:f0 + j + 1] for t in range(2)]
                dve.tensor_scalar(B[:, j, 0:P], const("strict"), f[0], None, ALU.mult)
                both = cst[:, CONST["ones"][0]:CONST["strict"][1]]
                ins = dve.tensor_scalar(B[:, j, P:384], both, f[1], None, ALU.mult)
                if i0 is not None:
                    link(dve, ins)
                    i = [SG[:, t, i0 + j:i0 + j + 1] for t in range(2)]
                    dve.scalar_tensor_tensor(B[:, j, 0:P], const("ident"), i[0], B[:, j, 0:P], ALU.mult, ALU.add)
                    dve.scalar_tensor_tensor(B[:, j, 256:384], const("ident"), i[1], B[:, j, 256:384],
                                             ALU.mult, ALU.add)

        def decay_pairs(B, j, q):
            if q == 0:
                return [(const("tri"), B[:, j, 0:P], P)]
            return [(const("tri"), B[:, j, P:384], 256), (const("ones"), B[:, j, 0:P], P)]

        def causal(q):
            return const("masks", 512, 640) if q == 0 else const("masks", 384, 640)

        def fox_units():
            units = []
            for h in range(8):
                part, j = divmod(h, 4)
                r = slice((h % 2) * HD, (h % 2 + 1) * HD)
                for q in range(TT):
                    nk = (q + 1) * P
                    units.append(dict(apart=None,
                        scores=[(Zt[r, 10 + h // 2, q * P:(q + 1) * P], Zt[r, 14 + h // 2, 0:nk], nk)]
                               + decay_pairs(FOX_B[part], j, q),
                        nk=nk, mask=causal(q), init=3 * NEG, sink=None,
                        v=[fv(t, h) for t in range(q + 1)], rows=(r.start, r.stop),
                        out=mixT[r, 4 + h // 2, q * P:(q + 1) * P]))
            return units

        def mlstm_units():
            units = []
            for h in range(4):
                r = slice((h % 2) * HD, (h % 2 + 1) * HD)
                for q in range(TT):
                    nk = (q + 1) * P
                    units.append(dict(
                        apart=(Zt[r, h // 2, q * P:(q + 1) * P], Zt[r, 2 + h // 2, 0:nk]),
                        scores=decay_pairs(BH, h, q), nk=nk, mask=causal(q), init=FC[:, q, h:h + 1], sink=None,
                        v=[mv(t, h) for t in range(q + 1)], rows=(r.start, r.stop),
                        out=Zt[r, 6 + h // 2, q * P:(q + 1) * P]))
            return units

        def pe_m_norm(pe, layer):
            for c in range(2):
                await_next(pe, "m_squared")
                mm(pe, bank[c][:, 0:T], const("head_mean"), z2(8 + c), start=True, stop=True, last_of="m_mean_square")
            phase_end(pe)

        def act_m_norm(act, layer):
            for c in range(2):
                act.activation(z2(8 + c), z2(6 + c), ACT.Square).then_inc(sem("m_squared"), 1)
                act.activation(z2(4 + c), z2(4 + c), ACT.Sigmoid).then_inc(sem("m_gate"), 1)
            for c in range(2):
                await_next(act, "m_mean_square")
                link(act, act.activation(hT[:, 4 + c, 0:T], bank[c][:, 0:T], ACT.Ln, bias=EPS))
                act.activation(hT[:, 4 + c, 0:T], hT[:, 4 + c, 0:T], ACT.Exp, scale=-0.5).then_inc(sem("m_rms"), 1)
            phase_end(act)

        def dve_m_norm(dve, layer):
            for part in range(2):
                dve_decay_columns(dve, FOX_B[part], 8 + 4 * part, None)
            for c in range(2):
                await_next(dve, "m_gate")
                await_next(dve, "m_rms")
                link(dve, dve.scalar_tensor_tensor(z2(6 + c), z2(6 + c), v("m_norm", layer, c, c + 1), hT[:, 4 + c, 0:T],
                                                   ALU.mult, ALU.mult))
                dve.tensor_tensor(mixT[:, c, 0:T], z2(6 + c), z2(4 + c), ALU.mult)
            phase_end(dve)

        def x_groups(layer):
            g = []
            for j in range(2):
                g += feature_major([z2(2 * j), z2(2 * j + 1)], 0, T, float(P) ** -0.5)
            for j in range(2):
                g += feature_major([z2(4 + 2 * j), z2(5 + 2 * j)], T, 2 * T)
            for j in range(2):
                g += token_major([tok[:, t * 768 + 256 * j:t * 768 + 256 * (j + 1)] for t in range(2)], 2)
            return g

        def x_units():
            return [dict(apart=None, scores=[(Zt[:, h, q * P:(q + 1) * P], z2(4 + h), T)], nk=T,
                         mask=const("masks", 128, 384), init=3 * NEG, sink=None,
                         v=[tok[:, t * 768 + h * P:t * 768 + (h + 1) * P] for t in range(2)], rows=(0, P),
                         out=mixT[:, h, q * P:(q + 1) * P]) for h in range(4) for q in range(TT)]

        LG = sc[:, 0:16].rearrange("p (t e) -> p t e", t=2)
        RK = sc[:, 16:32].rearrange("p (t e) -> p t e", t=2)
        EX = sc[:, 32:48].rearrange("p (t e) -> p t e", t=2)
        TOP = sc[:, 48:50].rearrange("p (t e) -> p t e", t=2)
        CMP = mixT[:, 0, 0:128].rearrange("p (t i j) -> p t i j", t=2, i=N_EXP)
        EQ = mixT[:, 1, 0:16].rearrange("p (t e) -> p t e", t=2)
        POS = sc[:, 52:72].rearrange("p (t e) -> p t e", t=2)
        GT = sc[:, 72:92].rearrange("p (t e) -> p t e", t=2)
        h_tok = Z[:, 5632:7680].rearrange("p (t n) -> p t n", t=2)
        y_e = Z[:, 7680:8704]
        silu_b = [Z[:, 8704 + i * 256:8960 + i * 256] for i in range(2)]
        hid_tok = [Z[:, 9216 + i * 256:9472 + i * 256] for i in range(2)]
        place_w = [Z[:, 9728 + i * 256:9984 + i * 256] for i in range(2)]
        select_w = Z[:, 10240:10496].rearrange("p (t n) -> p t n", t=2)
        select = Z[:, 10496:10752].rearrange("p (t n) -> p t n", t=2)
        g_part = [a_hi[:, 4 * i:4 * i + 2, :].rearrange("p a b -> p (a b)") for i in range(2)]

        def hid_e(f, part):
            return Zr[:, (2 * f + part) * P:(2 * f + part + 1) * P]
        def router_groups():
            return token_major([LG[:, t, :] for t in range(2)], n=N_EXP)

        def dve_router(dve):
            for t in range(2):
                ins = dve.tensor_tensor(CMP[:, t], LG[:, t].unsqueeze(1).to_broadcast([P, N_EXP, N_EXP]),
                                        LG[:, t].unsqueeze(2).to_broadcast([P, N_EXP, N_EXP]), ALU.is_gt)
            dve.tensor_reduce(TOP[:, :, 0], LG[:, :, :], AX.X, ALU.max)
            link(dve, dve.tensor_copy(EX[:, :, :], LG[:, :, :]))
            link(dve, dve.tensor_reduce(RK[:, :, :], CMP[:, :, :, :], AX.X, ALU.add))
            for j in range(N_EXP - 1):
                m = N_EXP - 1 - j
                link(dve, dve.tensor_tensor(EQ[:, :, 0:m], LG[:, :, j + 1:N_EXP],
                                            LG[:, :, j:j + 1].to_broadcast([P, 2, m]), ALU.is_equal))
                link(dve, dve.tensor_tensor(RK[:, :, j + 1:N_EXP], RK[:, :, j + 1:N_EXP], EQ[:, :, 0:m], ALU.add))
            link(dve, dve.tensor_scalar(RK[:, :, :], RK[:, :, :], 1.5, None, ALU.is_lt))
            dve.tensor_tensor(EX[:, :, :], EX[:, :, :], TOP[:, :, :].to_broadcast([P, 2, N_EXP]), ALU.subtract)\
               .then_inc(sem("logits_below_max"), 1)
            dve.drain().then_inc(sem("choices"), 1)
            await_next(dve, "logits_exp")
            link(dve, dve.tensor_tensor(EX[:, :, :], EX[:, :, :], RK[:, :, :], ALU.mult))
            link(dve, dve.tensor_reduce(TOP[:, :, 0], EX[:, :, :], AX.X, ALU.add))
            link(dve, dve.reciprocal(TOP[:, :, :], TOP[:, :, :]))
            dve.memset(GT[:, :, :], 0.0)
            link(dve, dve.memset(POS[:, :, :], -1.0))
            dve.memset(y_e, 0.0)
            dve.memset(place_w[1], 0.0)
            dve.tensor_tensor(GT[:, :, 0:N_EXP], EX[:, :, :], TOP[:, :, :].to_broadcast([P, 2, N_EXP]), ALU.mult)
            await_next(dve, "choice_counts")
            for t in range(2):
                ins = dve.tensor_tensor(POS[:, t, 0:N_EXP], RK[:, t, :], bank[t][:, 0:N_EXP], ALU.mult)
            link(dve, ins)
            link(dve, dve.tensor_scalar(POS[:, :, 0:N_EXP], POS[:, :, 0:N_EXP], -1.0, None, ALU.add))
            link(dve, dve.tensor_reduce(TOP[:, 0, :], bank[2][:, 0:N_EXP], AX.X, ALU.max))
            link(dve, dve.tensor_scalar(TOP[:, 0, :], TOP[:, 0, :], P + 0.5, None, ALU.is_gt))
            dve.tensor_copy(overflow[:, :], TOP[:, 0, :])
            for t in range(2):
                for d in range(2):
                    await_next(dve, "h_turned")
                    dve.tensor_copy(h_tok[:, t, d * 512:(d + 1) * 512], bank[4 + 2 * t + d][:, :])
            phase_end(dve)

        def act_router(act):
            await_next(act, "logits_below_max")
            act.activation(EX[:, :, :], EX[:, :, :], ACT.Exp).then_inc(sem("logits_exp"), 1)
            phase_end(act)

        def pe_router(pe):
            for t in range(2):
                for k in range(KT):
                    out = bank[4 + 2 * t + k // 4][:, (k % 4) * P:(k % 4 + 1) * P]
                    for part in range(2):
                        mm(pe, out, h(part, k, t * P, (t + 1) * P).bitcast(F32), const("ident"), start=part == 0,
                           stop=part == 1, last_of="h_turned" if part == 1 and k % 4 == 3 else None)
            await_next(pe, "choices")
            mm(pe, bank[0][:, 0:N_EXP], const("tri"), RK[:, 0, :], start=True, stop=True)
            for b, last in ((1, "tri"), (2, "ones")):
                mm(pe, bank[b][:, 0:N_EXP], const("ones"), RK[:, 0, :], start=True, stop=False)
                mm(pe, bank[b][:, 0:N_EXP], const(last), RK[:, 1, :], start=False, stop=True,
                   last_of="choice_counts" if b == 2 else None)
            phase_end(pe)

        PAIRS = FT // 2

        def pe_scatter(pe, pre, s, i):
            pe.wait_ge(sem(pre + "_y_copied"), s * 2 + 2)
            for b in range(4):
                if b >= 2:
                    pe.wait_ge(sem(pre + "_x_added"), s * 4 + b - 1)
                for c in range(2):
                    d = 2 * b + c
                    mm(pe, bank[6 + b % 2][:, c * T:(c + 1) * T], y_e[:, d * P:(d + 1) * P], place_w[1 - i],
                       start=True, stop=True, last_of=pre + "_scattered" if c == 1 else None)

        def dve_add_scattered(dve, pre, s):
            for b in range(4):
                dve.wait_ge(sem(pre + "_scattered"), s * 4 + b + 1)
                x = xT[:, 2 * b:2 * b + 2, 0:T]
                dve.tensor_tensor(x, x, bank[6 + b % 2].rearrange("p (c n) -> p c n", c=2), ALU.add)\
                   .then_inc(sem(pre + "_x_added"), 1)

        def pe_gather(pe, pre, r):
            pe.wait_ge(sem(pre + "_selected"), r + 1)
            for k in range(KT):
                for t in range(2):
                    mm(pe, bank[6 + k // 4][:, (k % 4) * P:(k % 4 + 1) * P], h_tok[:, t, k * P:(k + 1) * P],
                       select[:, t, :], start=t == 0, stop=t == 1,
                       last_of=pre + "_gathered" if k == KT - 1 and t == 1 else None)
            for t in range(2):
                ins = pe.transpose(bank[3][:, t * P:(t + 1) * P], select_w[:, t, :], const("ident"))
            ins.then_inc(sem(pre + "_gates_turned"), 1)

        def act_gather(act, pre, r, i):
            act.wait_ge(sem(pre + "_gathered"), r + 1)
            act.activation(g_part[0], psum[:, 6:8, :].rearrange("p a b -> p (a b)"), ACT.Copy)\
               .then_inc(sem(pre + "_slots_rounded"), 1)
            act.wait_ge(sem(pre + "_gates_turned"), r + 1)
            act.activation(place_w[i], bank[3][:, 0:T], ACT.Copy).then_inc(sem(pre + "_gates_placed"), 1)

        def dve_select(dve, pre, r, e):
            for t in range(2):
                pos = POS[:, t, e]
                dve.tensor_scalar(select[:, t, :], const("iota"), pos, None, ALU.is_equal)
                ins = dve.tensor_scalar(select_w[:, t, :], const("iota"), pos, GT[:, t, e],
                                        ALU.is_equal, ALU.mult)
            ins.then_inc(sem(pre + "_selected"), 1)

        def dve_gather(dve, pre, r):
            dve.wait_ge(sem(pre + "_slots_rounded"), r + 1)
            dve.tensor_tensor(g_part[1], psum[:, 6:8, :].rearrange("p a b -> p (a b)"), g_part[0].bitcast(F32),
                              ALU.subtract).then_inc(sem(pre + "_slots_split"), 1)

        def pe_expert(pe, pre, r, i, it):
            def turn(j):
                pe.wait_ge(sem(pre + "_full"), r * PAIRS + j + 1)
                if j >= 2:
                    pe.wait_ge(sem(pre + "_hidden"), r * PAIRS + j - 1)
                if j == 1:
                    pe.wait_ge(sem(pre + "_gates_placed"), r + 1)
                for c in range(2):
                    ins = pe.transpose(bank[2 + j % 2][:, c * P:(c + 1) * P], hid_tok[j % 2][:, c * P:(c + 1) * P],
                                       const("ident"))
                ins.then_inc(sem(pre + "_turned"), 1)

            pe.wait_ge(sem(pre + "_slots_split"), r + 1)
            for j in range(PAIRS):
                if j >= 2:
                    pe.wait_ge(sem(pre + "_full"), r * PAIRS + j - 1)
                for c in range(2):
                    w = piece_slot(pe, it=it)
                    for k in range(KT):
                        for m, (wp, ap) in enumerate(THREE):
                            last = k == KT - 1 and m == 2
                            mm(pe, bank[j % 2][:, c * 256:(c + 1) * 256], g_part[ap][:, k * P:(k + 1) * P],
                               w[wp][:, k * 256:(k + 1) * 256], start=k == 0 and m == 0, stop=last,
                               last_of=pre + "_up" if last and c else None)
                    stream["release"] = True
                if j >= 1:
                    turn(j - 1)
                if j == 2:
                    pe_scatter(pe, pre, r, i)
            turn(PAIRS - 1)
            for q in range(2 * FT):
                half, f = divmod(q, FT)
                if q % 4 == 0:
                    w = piece_slot(pe, it=it)
                if half == 0 and f % 2 == 0:
                    pe.wait_ge(sem(pre + "_hidden"), r * PAIRS + f // 2 + 1)
                if f == 0:
                    pe.wait_ge(sem(pre + "_y_copied"), r * 2 + half + 1)
                for m, (wp, ap) in enumerate(THREE):
                    last = f == FT - 1 and m == 2
                    mm(pe, bank[4 + half], hid_e(f, ap), w[wp][:, (q % 4) * 512:(q % 4 + 1) * 512],
                       start=f == 0 and m == 0, stop=last, last_of=pre + "_down" if last else None)
                if q % 4 == 3:
                    stream["release"] = True
                if q == FT + 1:
                    pe.wait_ge(sem(pre + "_x_added"), r * 4 + 4)
                    pe_gather(pe, pre, r + 1)

        def act_expert(act, pre, r, i, it):
            for j in range(PAIRS + 1):
                if j < PAIRS:
                    split_ahead(act, "act", 2, it=it)
                    act.wait_ge(sem(pre + "_up"), r * PAIRS + j + 1)
                    if j >= 2:
                        act.wait_ge(sem(pre + "_full"), r * PAIRS + j - 1)
                    act.activation(silu_b[j % 2].rearrange("p (c n) -> p c n", c=2),
                                   bank[j % 2].rearrange("p (c n) -> p c n", c=2)[:, :, 0:P], ACT.Silu)\
                       .then_inc(sem(pre + "_silu"), 1)
                if j >= 1:
                    act.wait_ge(sem(pre + "_turned"), r * PAIRS + j)
                    out = Zr[:, (j - 1) * 4 * P:j * 4 * P].rearrange("p (c u n) -> p c u n", c=2, u=2)[:, :, 0, :]
                    act.activation(out, bank[2 + (j - 1) % 2][:, 0:T].rearrange("p (c n) -> p c n", c=2), ACT.Copy)\
                       .then_inc(sem(pre + "_rounded"), 1)
            for j in range(PAIRS):
                split_ahead(act, "act", it=it)
                if j == PAIRS // 2 + 1:
                    act.wait_ge(sem(pre + "_down"), r * 2 + 1)
                    act.activation(y_e[:, 0:512], bank[4], ACT.Copy).then_inc(sem(pre + "_y_copied"), 1)
                    act_gather(act, pre, r + 1, 1 - i)
            act.wait_ge(sem(pre + "_down"), r * 2 + 2)
            act.activation(y_e[:, 512:1024], bank[5], ACT.Copy).then_inc(sem(pre + "_y_copied"), 1)

        def dve_expert(dve, pre, r, i, it, following):
            for j in range(PAIRS + 1):
                if j < PAIRS:
                    split_ahead(dve, "dve", 2, it=it)
                    dve.wait_ge(sem(pre + "_silu"), r * PAIRS + j + 1)
                    if j >= 2:
                        dve.wait_ge(sem(pre + "_turned"), r * PAIRS + j - 1)
                    dve.tensor_tensor(hid_tok[j % 2].rearrange("p (c n) -> p c n", c=2),
                                      silu_b[j % 2].rearrange("p (c n) -> p c n", c=2),
                                      bank[j % 2].rearrange("p (c n) -> p c n", c=2)[:, :, P:2 * P], ALU.mult)\
                       .then_inc(sem(pre + "_full"), 1)
                if j >= 1:
                    dve.wait_ge(sem(pre + "_rounded"), r * PAIRS + j)
                    parts = Zr[:, (j - 1) * 4 * P:j * 4 * P].rearrange("p (c u n) -> p c u n", c=2, u=2)
                    dve.tensor_tensor(parts[:, :, 1, :], bank[2 + (j - 1) % 2][:, 0:T].rearrange("p (c n) -> p c n", c=2),
                                      parts[:, :, 0, :].bitcast(F32), ALU.subtract).then_inc(sem(pre + "_hidden"), 1)
                if j == 2:
                    dve_add_scattered(dve, pre, r)
            for j in range(PAIRS):
                split_ahead(dve, "dve", it=it)
                if j == 0:
                    dve_select(dve, pre, r + 1, following)
                if j == PAIRS // 2 + 1:
                    dve_gather(dve, pre, r + 1)

        def pe_experts(pe, pre, first):
            n0 = stream["n"]
            pe_gather(pe, pre, 0)
            release_now(pe)
            with pe.Fori(0, N_EXP // 2, 1) as e:
                for i in range(2):
                    pe_expert(pe, pre, e * 2 + i, i, e + first)
                release_now(pe)
            pe_scatter(pe, pre, N_EXP, 0)
            stream["n"] = n0

        def act_experts(act, pre, first):
            n0 = splits["act"]
            for _ in range(2):
                act.nop().then_inc(sem(pre + "_y_copied"), 1)
            act_gather(act, pre, 0, 0)
            with act.Fori(0, N_EXP // 2, 1) as e:
                for i in range(2):
                    act_expert(act, pre, e * 2 + i, i, e + first)
            splits["act"] = n0

        def dve_experts(dve, pre, first):
            n0 = splits["dve"]
            dve_select(dve, pre, 0, slice(0, 1))
            dve_gather(dve, pre, 0)
            with dve.Fori(0, N_EXP // 2, 1) as e:
                for i in range(2):
                    dve_expert(dve, pre, e * 2 + i, i, e + first, bass.ds(e * 2 + i + 1, 1))
            dve_add_scattered(dve, pre, N_EXP)
            splits["dve"] = n0

        def release_now(pe):
            if stream["release"]:
                pe.drain().then_inc(sem("piece_used"), 1)
                stream["release"] = False

        b2_seg = lambda name, layer: [(0, T, (lambda k: v(name, layer, k, k + 1)), None)]
        mem_seg = lambda layer: b2_seg("norm_x", layer) + [(T, 2 * T, (lambda k: v("norm_mem", layer, k, k + 1)), None)]
        one = lambda q, s: 1.0

        def gate_gain(layer, which):
            return lambda d, s: modT[:, layer, 16 + 24 * which + d, s:s + 1]

        block = ctx.enter_context(nc.Block())

        @block.sync
        def _(sp):
            for name, dst in (("xT", xT[:, :, 0:T]), ("ctxT", xT[:, :, T:2 * T]), ("vectors", vec[:, :]),
                              ("constants", cst[:, :]), ("level_masks", Z[:, 0:2 * LEVELS * P]),
                              ("gate_w", gate_w[:, :, :, :])):
                sp.dma_start(dst, A[name]).then_inc(sem("vectors_in"), 16)

            def load(n, s):
                src = A["stream"][n] if isinstance(n, int) else A["stream"][bass.ds(n, 1)].rearrange("o p c -> (o p) c")
                sp.dma_start(ring[:, s, :], src).then_inc(sem(f"piece_in_{s}"), 16)

            for s in range(SLOTS):
                load(s, s)
            rounds = n_pieces // SLOTS
            with sp.Fori(1, rounds, 1) as r:
                for s in range(SLOTS):
                    sp.wait_ge(sem("piece_used"), (r - 1) * SLOTS + s + 1)
                    load(r * SLOTS + s, s)
            for s in range(n_pieces % SLOTS):
                sp.wait_ge(sem("piece_used"), (rounds - 1) * SLOTS + s + 1)
                load(rounds * SLOTS + s, s)
            sp.wait_ge(sem("phase_dve"), EXPERT_PHASES)
            with sp.If(sp.value_load(overflow[0:1, 0:1], min_val=0, max_val=1) > 0):
                again = N_EXP * FFN_PIECES
                with sp.Fori(0, again // SLOTS, 1) as r:
                    for s in range(SLOTS):
                        sp.wait_ge(sem("piece_used"), n_pieces + r * SLOTS + s - SLOTS + 1)
                        load(r * SLOTS + (n_pieces + s - again), (n_pieces + s) % SLOTS)
            sp.nop()
            sp.wait_ge(sem("y_ready"), 1)
            sp.dma_start(y_out, hT[:, :, 0:T]).then_inc(sem("y_stored"), 16)
            sp.wait_ge(sem("y_stored"), 16)

        @block.tensor
        def _(pe):
            for layer in range(DEPTH):
                n = 2 * T if layer == 0 else T
                if layer == 0:
                    pe_mod(pe)
                pe_norm(pe, 0, 2 * T)
                groups, mod = b1_groups(layer), Mod(pe, "pe", layer * MOD_PIECES + EARLY, MOD_PIECES - EARLY)
                pe_products(pe, groups, "h_split", None, mod.among(groups))
                mod.finish()
                phase_end(pe)
                pe_rope(pe, layer)
                pe_attention(pe, b1_units(layer))
                phase_end(pe)
                pe_gla_gates(pe, layer)
                pe_gla_levels(pe, layer)
                pe_gla_out(pe, layer)
                pe_gla_norm(pe, layer)
                groups, mod = out_groups(KT, n, gate_gain(layer, 0), 2), Mod(pe, "pe", MOD_PIECES, EARLY)
                pe_products(pe, groups, "mix_split", "dve", mod.among(groups, 2) if layer == 0 else lambda g: None)
                if layer == 0:
                    mod.finish()
                phase_end(pe)
                pe_norm(pe, 0, n)
                pe_ffn(pe, 2 * layer, first=True)
                if layer == 0:
                    pe_ffn(pe, 1, T)
                phase_end(pe)
            pe_norm(pe, 0, T)
            phase_end(pe)
            phase_end(pe)
            for layer in range(DEPTH):
                pe_norm(pe, 0, T)
                pe_products(pe, b2_groups(layer), "h_split", B2_WHO)
                phase_end(pe)
                pe_b2_gates_ln(pe, layer)
                pe_attention(pe, mlstm_units())
                phase_end(pe)
                pe_m_norm(pe, layer)
                pe_attention(pe, fox_units())
                phase_end(pe)
                pe_products(pe, out_groups(KT, T, one, 2), "mix_split", "dve")
                phase_end(pe)
                pe_norm(pe, 0, 2 * T)
                pe_products(pe, x_groups(layer), "h_split")
                phase_end(pe)
                pe_attention(pe, x_units())
                phase_end(pe)
                pe_products(pe, out_groups(4, T, one, 4), "mix_split", "dve")
                phase_end(pe)
                pe_norm(pe, 0, T)
                if layer == 0:
                    pe_ffn(pe, 3, first=True)
                    phase_end(pe)
                else:
                    pe_products(pe, router_groups(), "h_split")
                    phase_end(pe)
                    pe_router(pe)
                    pe_experts(pe, "e", 0)
                    phase_end(pe)
                    with pe.If(pe.value_load(overflow[0:1, 0:1], min_val=0, max_val=1) > 0):
                        pe_experts(pe, "o", N_EXP // 2)
                    pe.nop()
                    phase_end(pe)
            pe_norm(pe, 0, T)

        @block.scalar
        def _(act):
            for layer in range(DEPTH):
                n = 2 * T if layer == 0 else T
                if layer == 0:
                    act_mod(act)
                act_norm(act, 0, 2 * T, b1_segments(layer, 0, 2 * T))
                groups, mod = b1_groups(layer), Mod(act, "act", layer * MOD_PIECES + EARLY, MOD_PIECES - EARLY)
                take_products(act, "act", groups, None, mod.among(groups))
                mod.finish()
                phase_end(act)
                act_rope(act, layer)
                act_attention(act, b1_units(layer))
                phase_end(act)
                act_gla_gates(act, layer)
                act_gla_levels(act, layer)
                act_gla_out(act, layer)
                act_gla_norm(act, layer)
                act_split_mix(act, KT, n)
                groups, mod = out_groups(KT, n, gate_gain(layer, 0), 2), Mod(act, "act", MOD_PIECES, EARLY)
                take_products(act, "act", groups, "dve", mod.among(groups, 2) if layer == 0 else lambda g: None)
                if layer == 0:
                    mod.finish()
                phase_end(act)
                act_norm(act, 0, n, b1_segments(layer, 1, n))
                act_ffn(act, 2 * layer)
                if layer == 0:
                    act_ffn(act, 1)
                phase_end(act)
            act_norm(act, 0, T, [(0, T, None, None)], split=False)
            phase_end(act)
            phase_end(act)
            for layer in range(DEPTH):
                act_norm(act, 0, T, b2_seg("norm_mix", layer))
                act_outs[layer] = base(act, "product_in_act")
                take_products(act, "act", b2_groups(layer), B2_WHO)
                phase_end(act)
                act_b2_gates_ln(act, layer)
                act_attention(act, mlstm_units())
                phase_end(act)
                act_m_norm(act, layer)
                act_attention(act, fox_units())
                phase_end(act)
                act_split_mix(act, KT, T)
                take_products(act, "act", out_groups(KT, T, one, 2), "dve")
                phase_end(act)
                act_norm(act, 0, 2 * T, mem_seg(layer))
                take_products(act, "act", x_groups(layer))
                phase_end(act)
                act_attention(act, x_units())
                phase_end(act)
                act_split_mix(act, 4, T)
                take_products(act, "act", out_groups(4, T, one, 4), "dve")
                phase_end(act)
                act_norm(act, 0, T, b2_seg("norm_ffn", layer))
                if layer == 0:
                    act_ffn(act, 3)
                    phase_end(act)
                else:
                    take_products(act, "act", router_groups())
                    phase_end(act)
                    act_router(act)
                    act_experts(act, "e", 0)
                    phase_end(act)
                    with act.If(act.value_load(overflow[0:1, 0:1], min_val=0, max_val=1) > 0):
                        act_experts(act, "o", N_EXP // 2)
                    act.nop()
                    phase_end(act)
            act_norm(act, 0, T, [(0, T, None, None)], split=False)

        @block.vector
        def _(dve):
            for layer in range(DEPTH):
                n = 2 * T if layer == 0 else T
                if layer == 0:
                    dve_mod(dve)
                dve_norm(dve, 0, 2 * T, b1_segments(layer, 0, 2 * T))
                dve.memset(lr_ones, 1.0)
                groups, mod = b1_groups(layer), Mod(dve, "dve", layer * MOD_PIECES + EARLY, MOD_PIECES - EARLY)
                take_products(dve, "dve", groups, None, mod.among(groups))
                mod.finish()
                phase_end(dve)
                dve_rope_conv(dve, layer)
                dve_attention(dve, b1_units(layer))
                phase_end(dve)
                dve_gla_gates(dve, layer)
                dve_gla_levels(dve, layer)
                dve_gla_out(dve, layer)
                dve_gla_norm(dve, layer)
                dve_split_mix(dve, KT, n)
                groups, mod = out_groups(KT, n, gate_gain(layer, 0), 2), Mod(dve, "dve", MOD_PIECES, EARLY)
                take_products(dve, "dve", groups, "dve", mod.among(groups, 2) if layer == 0 else lambda g: None)
                if layer == 0:
                    mod.finish()
                phase_end(dve)
                dve_norm(dve, 0, n, b1_segments(layer, 1, n))
                dve_ffn(dve, 2 * layer, 0, lambda q: gate_gain(layer, 1)(q, 0))
                if layer == 0:
                    dve_ffn(dve, 1, T, lambda q: gate_gain(layer, 1)(q, 1))
                phase_end(dve)
            dve_norm(dve, 0, T, [(0, T, (lambda k: v("final1", 0, k, k + 1)), None)], split=False)
            phase_end(dve)
            dve.wait_ge(sem("mem_in"), 16)
            for k in range(KT):
                dve.tensor_copy(xT[:, k, 0:T], hT[:, k, 0:T])
            phase_end(dve)
            for layer in range(DEPTH):
                dve_norm(dve, 0, T, b2_seg("norm_mix", layer))
                take_products(dve, "dve", b2_groups(layer), B2_WHO, dve_convs(dve, layer))
                phase_end(dve)
                dve_b2_gates_ln(dve, layer)
                dve_attention(dve, mlstm_units())
                phase_end(dve)
                dve_m_norm(dve, layer)
                dve_attention(dve, fox_units())
                phase_end(dve)
                dve_split_mix(dve, KT, T)
                take_products(dve, "dve", out_groups(KT, T, one, 2), "dve")
                phase_end(dve)
                dve_norm(dve, 0, 2 * T, mem_seg(layer))
                take_products(dve, "dve", x_groups(layer))
                phase_end(dve)
                dve_attention(dve, x_units())
                phase_end(dve)
                dve_split_mix(dve, 4, T)
                take_products(dve, "dve", out_groups(4, T, one, 4), "dve")
                phase_end(dve)
                dve_norm(dve, 0, T, b2_seg("norm_ffn", layer))
                if layer == 0:
                    dve_ffn(dve, 3, 0, lambda q: 1.0)
                    phase_end(dve)
                else:
                    take_products(dve, "dve", router_groups())
                    phase_end(dve)
                    dve_router(dve)
                    dve_experts(dve, "e", 0)
                    phase_end(dve)
                    with dve.If(dve.value_load(overflow[0:1, 0:1], min_val=0, max_val=1) > 0):
                        link(dve, dve.tensor_scalar(POS[:, :, :], POS[:, :, :], -float(P), None, ALU.add))
                        dve.memset(place_w[1], 0.0)
                        dve_experts(dve, "o", N_EXP // 2)
                    dve.nop()
                    phase_end(dve)
            dve_norm(dve, 0, T, [(0, T, (lambda k: v("final2", 0, k, k + 1)), None)], split=False)
            dve.drain().then_inc(sem("y_ready"), 1)

        @block.gpsimd
        def _(pool):
            for other in ("pe", "act", "dve"):
                pool.wait_ge(sem(f"phase_{other}"), B1_PHASES)
            pool.dma_start(xT[:, :, T:2 * T], A["memT"]).then_inc(sem("mem_in"), 16)


N_LOADS = 6
EXPERT_PHASES = 42
B1_PHASES = 19


def constants():
    r = np.arange(P)
    c = {}
    c["ident"] = np.eye(P)
    c["mean"] = np.full((P, P), 1.0 / D)
    c["head_mean"] = (r[:, None] // HD == r[None, :] // HD) / HD
    c["tri"] = r[:, None] <= r[None, :]
    c["tri_r"] = r[:, None] >= r[None, :]
    c["ones"] = np.ones((P, P))
    c["strict"] = r[:, None] > r[None, :]
    c["pair"] = (r[:, None] % 2 == np.arange(2)[None, :]) & (r[:, None] < 4)
    c["iota"] = np.tile(r, (P, 1))
    rot = np.zeros((P, P))
    for m in range(P):
        if m % 32 < 16:
            rot[m + 16, m] = -1.0
        else:
            rot[m - 16, m] = 1.0
    c["rot"] = rot
    zero = np.zeros((P, P))
    after = np.where(r[None, :] >= r[:, None], 0.0, NEG)
    upto = np.where(r[None, :] <= r[:, None], 0.0, NEG)
    c["masks"] = np.concatenate([after, zero, zero, zero, upto, zero, zero], 1)
    inv = np.float32(10000.0) ** (-np.arange(16, dtype=np.float32) / np.float32(16))
    t = np.arange(T)
    pos = np.stack([t // 64, t % 64]).astype(np.float32)
    ch = r % HD
    ang = pos[ch // 32] * inv[ch % 16][:, None]
    c["cos"], c["sin"] = np.cos(ang), np.sin(ang)
    out = np.zeros((P, N_CONST), np.float32)
    for name, (a, b) in CONST.items():
        out[:, a:b] = c[name]
    lv = np.zeros((P, 2 * LEVELS, P), np.float32)
    s, q = r[:, None], r[None, :]
    for l in range(LEVELS):
        same = (s >> (l + 1)) == (q >> (l + 1))
        up_s, up_q = (s >> l) & 1, (q >> l) & 1
        lv[:, 2 * l] = same & (up_s == 0) & (up_q == 1)
        lv[:, 2 * l + 1] = same & (up_s == 1) & (up_q == 0)
    return out, lv.reshape(P, -1)


def by_columns(w, width=256):
    k, n = w.shape
    return w.reshape(k // P, P, n // width, width).transpose(2, 1, 0, 3).reshape(-1, P, PIECE)


def ffn_pieces(gate, up, down):
    g = gate.reshape(KT, P, FT, P).transpose(2, 1, 0, 3)
    u = up.reshape(KT, P, FT, P).transpose(2, 1, 0, 3)
    d = down.reshape(FT, P, 2, 512).transpose(2, 0, 1, 3).reshape(2 * FT // 4, 4, P, 512).transpose(0, 2, 1, 3)
    return [np.concatenate([g, u], 3).reshape(FT, P, PIECE), d.reshape(-1, P, PIECE)]


def among(main, other, steps):
    res = []
    for k in range(len(main)):
        res += [main[k:k + 1], other[k * steps:(k + 1) * steps]]
    return np.concatenate(res + [other[len(main) * steps:]], 0)


def columns(x, tile=P):
    x = np.asarray(x)
    return x.reshape(-1, P).T


def rows(x):
    x = np.asarray(x).reshape(1, -1)
    return np.broadcast_to(x, (P, x.shape[1]))


def kernel(**inputs):
    import concourse.bacc as bacc
    from concourse.bass_utils import run_bass_kernel_spmd

    i = {k: np.asarray(a) for k, a in inputs.items()}
    pieces = []
    early_mod = [by_columns(i["w_mod"][1])[0:EARLY], np.zeros((0, P, PIECE), np.float32)]
    heads = np.array([64 * h + k for t in range(4) for h in (t, t + 4) for k in range(64)])
    for l in range(DEPTH):
        w = i["w_in"][l]
        none = np.zeros((D, 112), np.float32)
        w = np.concatenate([w[:, 0:768], w[:, 768:1280][:, heads], w[:, 1280:2576], none, w[:, 2576:2592], none], 1)
        mod = by_columns(i["w_mod"][l])
        if l == 0:
            pieces.append(mod[0:EARLY])
        pieces += [among(by_columns(w), mod[EARLY:], 1), among(by_columns(i["w_out"][l]), early_mod[l], 2)]
        for _ in range(2 if l == 0 else 1):
            pieces += ffn_pieces(i["w_up"][l][:, 0:FF], i["w_up"][l][:, FF:2 * FF], i["w_down"][l])
    for l in range(DEPTH):
        w = i["w_in_2"][l]
        w = np.concatenate([w[:, 1288:1544], w[:, 1032:1288], w[:, 0:512], w[:, 1024:1032], w[:, 3080:3088],
                            np.zeros((D, 240), np.float32), w[:, 512:1024], w[:, 1544:3080]], 1)
        pieces += [by_columns(w), by_columns(i["w_out_2"][l]), by_columns(i["xattn_w_q_2"][l]),
                   by_columns(i["xattn_w_kv_2"][l]), by_columns(i["xattn_w_o_2"][l], 512)]
        if l == 0:
            pieces += ffn_pieces(i["ffn_w_gate_2"][0], i["ffn_w_up_2"][0], i["ffn_w_down_2"][0])
        else:
            pieces.append(by_columns(np.concatenate([i["router_w_2"][0], np.zeros((D, 248), np.float32)], 1)))
            for e in range(N_EXP):
                pieces += ffn_pieces(i["moe_w_gate_2"][0, e], i["moe_w_up_2"][0, e], i["moe_w_down_2"][0, e])

    pieces.append(ffn_pieces(i["moe_w_gate_2"][0, 0], i["moe_w_up_2"][0, 0], i["moe_w_down_2"][0, 0])[0][0:AHEAD])
    vec = np.zeros((P, N_VEC), np.float32)

    def put(name, layer, cols):
        a, b = VEC[name, layer]
        vec[:, a:b] = cols

    for l in range(DEPTH):
        put("b_mod", l, columns(i["b_mod"][l]))
        put("norm1", l, columns(i["norm1_g"][l]))
        put("norm2", l, columns(i["norm2_g"][l]))
        put("conv_w", l, columns(i["conv_w"][l]))
        put("sink", l, rows(i["attn_sink"][l]))
        put("gla_g", l, columns(np.concatenate([i["gla_norm_g"][l], i["gla_norm_g"][l]])))
        put("norm_mix", l, columns(i["norm_mix_w_2"][l]))
        put("m_conv_w", l, columns(i["mlstm_conv_w_2"][l]))
        put("m_conv_b", l, columns(i["mlstm_conv_b_2"][l]))
        put("gate_b", l, rows(np.concatenate([i["mlstm_b_i_2"][l], i["mlstm_b_f_2"][l], i["fox_b_f_2"][l]])))
        put("m_norm", l, columns(i["mlstm_norm_w_2"][l]))
        put("c_conv_w", l, columns(i["conf_conv_w_2"][l]))
        put("c_conv_b", l, columns(i["conf_conv_b_2"][l]))
        put("ln_w", l, columns(i["conf_ln_w_2"][l]))
        put("ln_b", l, columns(i["conf_ln_b_2"][l]))
        put("norm_x", l, columns(i["norm_xattn_w_2"][l]))
        put("norm_mem", l, columns(i["norm_mem_w_2"][l]))
        put("norm_ffn", l, columns(i["norm_ffn_w_2"][l]))
    put("final1", 0, columns(i["final_norm_g"]))
    put("final2", 0, columns(i["norm_final_w_2"]))
    put("c", 0, np.stack([columns(i["c"][0]), columns(i["c_ctx"])], 2).reshape(P, 16))

    gate_w = np.zeros((17, DEPTH, 2, 256), np.float32)
    gate_w[0:16] = i["gla_gate_w"].transpose(2, 0, 1, 3)
    gate_w[16] = i["gla_gate_b"]
    consts, level_masks = constants()

    def turned(x):
        return np.ascontiguousarray(x.T.reshape(KT, P, T).transpose(1, 0, 2))

    arrays = dict(
        stream=np.concatenate(pieces, 0), xT=turned(i["x"][0]), ctxT=turned(i["ctx"][0]), memT=turned(i["mem_2"][0]),
        vectors=vec, constants=consts, level_masks=level_masks, gate_w=gate_w)
    nc = bacc.Bacc("TRN2", target_bir_lowering=False, num_devices=1)
    A = {}
    for name, a in arrays.items():
        A[name] = nc.dram_tensor(f"in_{name}", a.shape, mybir.dt.from_np(a.dtype), kind="ExternalInput").ap()
    y = nc.dram_tensor("out_y", (P, KT, T), F32, kind="ExternalOutput").ap()
    build(nc, A, y)
    r = run_bass_kernel_spmd(nc, [{f"in_{k}": a for k, a in arrays.items()}], core_ids=[0])
    got = r.results[0]["out_y"]
    return np.ascontiguousarray(got.transpose(1, 0, 2).reshape(D, T).T).reshape(1, T, D)
```
